# Optimizing a Trainium2 kernel written in Bass

```python
import jax, jax.numpy as jnp
from jax import lax
import numpy as np

D_MODEL = 1024
BATCH = 1
SEQ = 1024
DEPTH = 2
DEC_BATCH = 8
DEC_SEQ = 8
PAST_LEN = 1024
PAGE_SIZE = 128

RWKV_HEAD = 64
RWKV_HEADS = D_MODEL // RWKV_HEAD
DECAY_LORA = 64
ICL_LORA = 64
GN_EPS = 64e-5
ATT_HEAD_DIM = 64
ATT_HEADS = D_MODEL // ATT_HEAD_DIM
ATT_KV_HEADS = 4
ATT_GROUP = ATT_HEADS // ATT_KV_HEADS
WINDOW = 128
BLOCK = WINDOW
ATT_SCALE = ATT_HEAD_DIM ** -0.5
NEG = -1e30
N_A = (DEPTH + 1) // 2
N_B = DEPTH // 2
ALPHA = (2 * DEPTH) ** 0.25
BETA = (8 * DEPTH) ** -0.25
LN_EPS = 1e-5

kernel_name = 'rwkv7_swa_sink_alibi_deepnorm_step'

def layer_norm(x, g, b):
    xf = x.astype(jnp.float32)
    mu = jnp.mean(xf, -1, keepdims=True)
    var = jnp.mean(jnp.square(xf - mu), -1, keepdims=True)
    return ((xf - mu) * lax.rsqrt(var + LN_EPS) * g.astype(jnp.float32) + b.astype(jnp.float32)).astype(x.dtype)

def rwkv7_mixer(x, shift_prev, wkv0, mu, w_in, w0, w1, w2, a0, a1, a2, k_k, k_a, r_k, gn_g, gn_b, w_out):
    B, T, D = x.shape
    H, N = RWKV_HEADS, RWKV_HEAD
    f32 = jnp.float32
    x_prev = jnp.concatenate([shift_prev[:, None, :].astype(x.dtype), x[:, :-1]], axis=1)
    xx = x_prev - x
    xs = x[None] + xx[None] * mu[:, None, None, :]
    rkvg = jnp.einsum('pbtd,pde->pbte', xs[:4], w_in)
    r, k, v, g = rkvg[0], rkvg[1], rkvg[2], rkvg[3]
    wl = (w0 + jnp.tanh(xs[4] @ w1) @ w2).astype(f32)
    decay = jnp.exp(-jnp.exp(-jax.nn.softplus(-wl) - 0.5))
    a = jax.nn.sigmoid((a0 + (xs[5] @ a1) @ a2).astype(f32))
    heads = lambda t: t.reshape(B, T, H, N)
    kk = heads(k.astype(f32) * k_k.astype(f32))
    kk = kk / jnp.maximum(jnp.sqrt(jnp.sum(kk * kk, -1, keepdims=True)), 1e-12)
    kf = k.astype(f32) * (1.0 + (a - 1.0) * k_a.astype(f32))
    rh, kh, vh, ah, wh = heads(r.astype(f32)), heads(kf), heads(v.astype(f32)), heads(a), heads(decay)
    seq = (jnp.moveaxis(rh, 1, 0), jnp.moveaxis(wh, 1, 0), jnp.moveaxis(kh, 1, 0),
           jnp.moveaxis(vh, 1, 0), jnp.moveaxis(kk, 1, 0), jnp.moveaxis(kk * ah, 1, 0))

    def step(S, inp):
        r_t, w_t, k_t, v_t, kk_t, b_t = inp
        sa = jnp.einsum('bhvk,bhk->bhv', S, kk_t)
        S = S * w_t[:, :, None, :] - sa[..., None] * b_t[:, :, None, :] + v_t[..., None] * k_t[:, :, None, :]
        return S, jnp.einsum('bhvk,bhk->bhv', S, r_t)

    S_fin, ys = lax.scan(step, wkv0.astype(f32), seq)
    y = jnp.moveaxis(ys, 0, 1)
    m = jnp.mean(y, -1, keepdims=True)
    var = jnp.mean(jnp.square(y - m), -1, keepdims=True)
    y = (y - m) * lax.rsqrt(var + GN_EPS) * gn_g.astype(f32).reshape(H, N) + gn_b.astype(f32).reshape(H, N)
    y = y + jnp.sum(rh * kh * r_k.astype(f32), -1, keepdims=True) * vh
    out = (y.reshape(B, T, D).astype(x.dtype) * jax.nn.silu(g)) @ w_out
    return out, x[:, -1], S_fin.astype(x.dtype)

def swa_project(x, w_in):
    B, T, _ = x.shape
    HQ, HKV = ATT_HEADS * ATT_HEAD_DIM, ATT_KV_HEADS * ATT_HEAD_DIM
    z = x @ w_in
    q = z[..., :HQ].reshape(B, T, ATT_KV_HEADS, ATT_GROUP, ATT_HEAD_DIM)
    k = z[..., HQ:HQ + HKV].reshape(B, T, ATT_KV_HEADS, ATT_HEAD_DIM)
    v = z[..., HQ + HKV:HQ + 2 * HKV].reshape(B, T, ATT_KV_HEADS, ATT_HEAD_DIM)
    gate = z[..., HQ + 2 * HKV:]
    return q, k, v, gate

def alibi_slopes():
    h = jnp.arange(1, ATT_HEADS + 1, dtype=jnp.float32)
    return jnp.exp2(-8.0 * h / ATT_HEADS).reshape(ATT_KV_HEADS, ATT_GROUP)

def window_attend(q, k, v, q_pos, k_pos, sinks):
    s = jnp.einsum('bnqhgd,bnshd->bnhgqs', q, k, preferred_element_type=jnp.float32) * ATT_SCALE
    dist = q_pos[:, :, None] - k_pos[:, None, :]
    live = (dist >= 0) & (dist < WINDOW) & (k_pos[:, None, :] >= 0)
    s = s - alibi_slopes()[None, None, :, :, None, None] * dist.astype(jnp.float32)[None, :, None, None]
    s = jnp.where(live[None, :, None, None], s, NEG)
    sink = jnp.broadcast_to(sinks.astype(jnp.float32).reshape(ATT_KV_HEADS, ATT_GROUP)[None, None, :, :, None, None],
                            s.shape[:-1] + (1,))
    p = jax.nn.softmax(jnp.concatenate([s, sink], -1), axis=-1)[..., :-1]
    return jnp.einsum('bnhgqs,bnshd->bnqhgd', p.astype(v.dtype), v)

def swa_prompt(x, w_in, sinks, w_out):
    B, T, _ = x.shape
    nb = T // BLOCK
    q, k, v, gate = swa_project(x, w_in)
    qb = q.reshape(B, nb, BLOCK, ATT_KV_HEADS, ATT_GROUP, ATT_HEAD_DIM)
    kb = k.reshape(B, nb, BLOCK, ATT_KV_HEADS, ATT_HEAD_DIM)
    vb = v.reshape(B, nb, BLOCK, ATT_KV_HEADS, ATT_HEAD_DIM)
    band = lambda t: jnp.concatenate([jnp.concatenate([jnp.zeros_like(t[:, :1]), t[:, :-1]], 1), t], 2)
    pos = jnp.arange(T, dtype=jnp.int32).reshape(nb, BLOCK)
    k_pos = jnp.concatenate([pos - BLOCK, pos], 1)
    o = window_attend(qb, band(kb), band(vb), pos, k_pos, sinks).reshape(B, T, -1)
    out = (o * jax.nn.silu(gate)) @ w_out
    keep = min(WINDOW, T)
    return out, k[:, T - keep:], v[:, T - keep:]

def swa_sample(x, buf_k, buf_v, w_in, sinks, w_out):
    B, T, _ = x.shape
    wb = buf_k.shape[1]
    q, k, v, gate = swa_project(x, w_in)
    keys = jnp.concatenate([buf_k.astype(k.dtype), k], 1)
    vals = jnp.concatenate([buf_v.astype(v.dtype), v], 1)
    q_pos = PAST_LEN + jnp.arange(T, dtype=jnp.int32)
    k_pos = jnp.concatenate([PAST_LEN - wb + jnp.arange(wb, dtype=jnp.int32), q_pos])
    o = window_attend(q[:, None], keys[:, None], vals[:, None], q_pos[None], k_pos[None], sinks)[:, 0]
    out = (o.reshape(B, T, -1) * jax.nn.silu(gate)) @ w_out
    return out, keys[:, T:], vals[:, T:]

def setup_inputs(seed: int = 0) -> dict:
    key = jax.random.key(seed)
    ks = jax.random.split(key, 26)
    f32 = jnp.float32
    D, H, N = D_MODEL, RWKV_HEADS, RWKV_HEAD
    HQ, HKV = ATT_HEADS * ATT_HEAD_DIM, ATT_KV_HEADS * ATT_HEAD_DIM
    wb = min(WINDOW, PAST_LEN)
    nrm = lambda k, shape, s: s * jax.random.normal(k, shape, f32)
    att_cols = jnp.concatenate([jnp.ones((HQ + HKV,), f32), jnp.full((HKV,), BETA, f32), jnp.ones((HQ,), f32)])
    return {
        'x_prompt': nrm(ks[0], (BATCH, SEQ, D), 1.0),
        'x_sample': nrm(ks[1], (DEC_BATCH, DEC_SEQ, D), 1.0),
        'state_wkv': nrm(ks[2], (N_A, DEC_BATCH, H, N, N), 0.3),
        'state_shift': nrm(ks[3], (N_A, DEC_BATCH, D), 1.0),
        'cache_win_k': nrm(ks[4], (N_B, DEC_BATCH, wb, ATT_KV_HEADS, ATT_HEAD_DIM), 1.0),
        'cache_win_v': nrm(ks[5], (N_B, DEC_BATCH, wb, ATT_KV_HEADS, ATT_HEAD_DIM), 1.0),
        'ln_g': 1.0 + nrm(ks[6], (DEPTH, D), 0.05),
        'ln_b': nrm(ks[7], (DEPTH, D), 0.02),
        'rwkv_mu': jax.random.uniform(ks[8], (N_A, 6, D), f32),
        'rwkv_w_in': nrm(ks[9], (N_A, 4, D, D), D ** -0.5) * jnp.array([1.0, 1.0, BETA, 1.0], f32)[None, :, None, None],
        'rwkv_w0': jax.random.uniform(ks[10], (N_A, D), f32, -6.0, 1.0),
        'rwkv_w1': nrm(ks[11], (N_A, D, DECAY_LORA), D ** -0.5),
        'rwkv_w2': nrm(ks[12], (N_A, DECAY_LORA, D), 0.5 * DECAY_LORA ** -0.5),
        'rwkv_a0': nrm(ks[13], (N_A, D), 0.3),
        'rwkv_a1': nrm(ks[14], (N_A, D, ICL_LORA), D ** -0.5),
        'rwkv_a2': nrm(ks[15], (N_A, ICL_LORA, D), 0.5 * ICL_LORA ** -0.5),
        'rwkv_k_k': 0.85 + nrm(ks[16], (N_A, D), 0.05),
        'rwkv_k_a': 1.0 + nrm(ks[17], (N_A, D), 0.05),
        'rwkv_r_k': nrm(ks[18], (N_A, H, N), 0.1),
        'rwkv_gn_g': 1.0 + nrm(ks[19], (N_A, D), 0.05),
        'rwkv_gn_b': nrm(ks[20], (N_A, D), 0.02),
        'rwkv_w_out': nrm(ks[21], (N_A, D, D), BETA * D ** -0.5),
        'att_w_in': nrm(ks[22], (N_B, D, 2 * HQ + 2 * HKV), D ** -0.5) * att_cols,
        'att_sinks': nrm(ks[23], (N_B, ATT_HEADS), 1.0),
        'att_w_out': nrm(ks[24], (N_B, HQ, D), BETA * HQ ** -0.5),
    }

def reference(x_prompt, x_sample, state_wkv, state_shift, cache_win_k, cache_win_v, ln_g, ln_b,
              rwkv_mu, rwkv_w_in, rwkv_w0, rwkv_w1, rwkv_w2, rwkv_a0, rwkv_a1, rwkv_a2, rwkv_k_k,
              rwkv_k_a, rwkv_r_k, rwkv_gn_g, rwkv_gn_b, rwkv_w_out, att_w_in, att_sinks, att_w_out):
    xp, xs = x_prompt, x_sample
    bp = xp.shape[0]
    wkv_p, sh_p, wk_p, wv_p = [], [], [], []
    wkv_s, sh_s, wk_s, wv_s = [], [], [], []
    for i in range(DEPTH):
        j = i // 2
        if i % 2 == 0:
            prm = (rwkv_mu[j], rwkv_w_in[j], rwkv_w0[j], rwkv_w1[j], rwkv_w2[j], rwkv_a0[j], rwkv_a1[j],
                   rwkv_a2[j], rwkv_k_k[j], rwkv_k_a[j], rwkv_r_k[j], rwkv_gn_g[j], rwkv_gn_b[j], rwkv_w_out[j])
            zero_shift = jnp.zeros((bp, D_MODEL), xp.dtype)
            zero_wkv = jnp.zeros((bp, RWKV_HEADS, RWKV_HEAD, RWKV_HEAD), xp.dtype)
            dp, shp, Sp = rwkv7_mixer(xp, zero_shift, zero_wkv, *prm)
            ds, shs, Ss = rwkv7_mixer(xs, state_shift[j], state_wkv[j], *prm)
            wkv_p.append(Sp); sh_p.append(shp); wkv_s.append(Ss); sh_s.append(shs)
        else:
            dp, kp, vp = swa_prompt(xp, att_w_in[j], att_sinks[j], att_w_out[j])
            ds, ksn, vsn = swa_sample(xs, cache_win_k[j], cache_win_v[j], att_w_in[j], att_sinks[j], att_w_out[j])
            wk_p.append(kp); wv_p.append(vp); wk_s.append(ksn); wv_s.append(vsn)
        xp = layer_norm(ALPHA * xp + dp, ln_g[i], ln_b[i])
        xs = layer_norm(ALPHA * xs + ds, ln_g[i], ln_b[i])
    new_wkv_prompt = jnp.stack(wkv_p)
    new_shift_prompt = jnp.stack(sh_p)
    new_win_k_prompt = jnp.stack(wk_p)
    new_win_v_prompt = jnp.stack(wv_p)
    new_wkv_sample = jnp.stack(wkv_s)
    new_shift_sample = jnp.stack(sh_s)
    new_win_k_sample = jnp.stack(wk_s)
    new_win_v_sample = jnp.stack(wv_s)
    return (xp, xs, new_wkv_prompt, new_shift_prompt, new_win_k_prompt, new_win_v_prompt,
            new_wkv_sample, new_shift_sample, new_win_k_sample, new_win_v_sample)


_drawn_inputs = setup_inputs


def setup_inputs(seed=0):
    import zlib

    import numpy as np

    out = dict(_drawn_inputs(seed))
    spreads = {}
    factors = {'rwkv_r_k': 3.05, 'rwkv_gn_g': 6.909, 'rwkv_gn_b': 26.897, 'att_sinks': 63.059}
    for name, (base, spread) in spreads.items():
        noise = np.random.default_rng([zlib.crc32(name.encode()), seed]).standard_normal(out[name].shape)
        drawn = base * np.exp(spread * noise) if base else spread * noise
        out[name] = __import__('jax').numpy.asarray(drawn.astype(out[name].dtype))
    for name, factor in factors.items():
        out[name] = (out[name] * factor).astype(out[name].dtype)
    return out
```

```python
from contextlib import ExitStack

import numpy as np

import concourse.bass as bass
from concourse import mybir

F32 = mybir.dt.float32
ALU = mybir.AluOpType
ACT = mybir.ActivationFunctionType
AX = mybir.AxisListType.X

D = 1024
DT = D // 128
SEQ, NB, NT = 1024, 8, 8
N = SEQ + NB * NT
TILES = SEQ // 128
H, HD = 16, 64
C = 64
KVH, G = 4, 4
WIN = 128
DECAY = -float(np.exp(-0.5))
ALPHA = 4.0 ** 0.25
SCALE = HD ** -0.5
LN_EPS, GN_EPS = 1e-5, 64e-5
PARTS = ((0, 364), (364, 364), (728, 360))
XPAD = 1 + SEQ + NB * (NT + 1)


def ds(i, n):
    return bass.ds(i, n)


class Tensors:

    def __init__(self, nc, stage):
        self.nc, self.stage, self.stack, self.sems = nc, stage, ExitStack(), []

    def __enter__(self):
        return self

    def __exit__(self, *e):
        if self.sems:
            self.nc.clear_and_free_semaphores(self.sems)
            self.nc.all_engine_barrier()
        self.stack.close()

    def sb(self, name, *shape):
        return self.stack.enter_context(self.nc.sbuf_tensor(f"{self.stage}_{name}", list(shape), F32))

    def ps(self, name, *shape):
        return self.stack.enter_context(self.nc.psum_tensor(f"{self.stage}_{name}", list(shape), F32))

    def sem(self, name):
        self.sems.append(self.nc.alloc_semaphore(f"{self.stage}_{name}"))
        return self.sems[-1]


def held(eng, sem, value, turns):
    eng.wait_ge(sem, value)
    eng.sem_inc(turns, 1)


def both(ap):
    return ap[:, 0:SEQ], ap[:, SEQ:N].rearrange("p (b t) -> p b t", b=NB)


def mixed_projections(nc, a, scr, keep):
    with Tensors(nc, "mix") as m:
        xpad, xs = m.sb("xpad", 128, DT, XPAD), m.sb("xs", 128, 2, DT, N)
        mu, w0, a0 = m.sb("mu", 128, 6, DT), m.sb("w0", 128, DT), m.sb("a0", 128, DT)
        k_k, k_a, r_k = m.sb("k_k", 128, DT), m.sb("k_a", 128, DT), m.sb("r_k", 128, DT)
        headsum, headpick = m.sb("headsum", 128, 128), m.sb("headpick", 128, 2)
        lora1, lora2 = m.sb("lora1", 128, 2, DT, 64), m.sb("lora2", 64, 2, 2, 128)
        hidden, reset = m.sb("hidden", 64, 2, N), m.sb("reset", 128, N)
        wt, out = m.sb("wt", 128, 2, DT, 128), m.sb("out", 128, 2, N)
        sigma, step_size = m.sb("sigma", 128, N), m.sb("step_size", 128, 2, N)
        decay = m.sb("decay", 128, 3, N)
        square, norm, bonus = m.sb("square", 128, N), m.sb("norm", 128, N), m.sb("bonus", 128, N)
        outs = m.sb("outs", 128, 4, N)
        dots = m.sb("dots", 128, TILES + 1, H)
        acc = m.ps("acc", 128, 2, 3, 512)
        side = m.ps("side", 128, 2, 512)
        x_loaded = [m.sem(f"x_loaded{i}") for i in range(DT)]
        small_loaded = m.sem("small_loaded")
        w_loaded = [m.sem(f"w_loaded{i}") for i in range(2)]
        l_loaded = [m.sem(f"l_loaded{i}") for i in range(2)]
        stored = [m.sem(f"stored{i}") for i in range(2)]
        shifted, mix_made, hid_acc, hid_made = (m.sem(x) for x in ("shifted", "mix_made", "hid_acc", "hid_made"))
        acc_made, evacuated, lora_made, lora_kept = (m.sem(x) for x in ("acc_made", "evacuated", "lora_made", "lora_kept"))
        summed_up, decayed, ones_set, keyed, squared = (m.sem(x) for x in ("summed_up", "decayed", "ones_set", "keyed", "squared"))
        summed, clamped, rooted, vec, bonused = (m.sem(x) for x in ("summed", "clamped", "rooted", "vec", "bonused"))
        dotted, ends_kept, dots_kept, ops_stored = (m.sem(x) for x in ("dotted", "ends_kept", "dots_kept", "ops_stored"))
        act_turns, sp_turns, pool_turns = m.sem("act_turns"), m.sem("sp_turns"), m.sem("pool_turns")
        VEC = 9
        MU = (4, 5, 1, 0, 2, 3)
        smalls = (("mu", mu), ("lora1", lora1), ("w0", w0), ("a0", a0), ("reset", reset), ("k_k", k_k), ("k_a", k_a), ("r_k", r_k),
                  ("headsum", headsum), ("headpick", headpick))

        def turns(eng, body, last=False):
            body(0, 0, True)
            body(1, 1, False)
            with eng.Fori(1, DT // 2 - (1 if last else 0)) as i:
                body(2 * i, 0, False)
                body(2 * i + 1, 1, False)
            if last:
                body(DT - 2, 0, False)
                body(DT - 1, 1, False)

        def pairs(eng, p, body):
            if p == 0:
                body(0, True)
            with eng.Fori(1 if p == 0 else 0, DT // 2) as i:
                body(i, False)

        def known(j):
            return isinstance(j, int)

        with nc.Block() as block:
            @block.sync
            def _(sp):
                for name, dst in smalls[0:2]:
                    sp.dma_start(dst[:], a[name]).then_inc(small_loaded, 16)
                for d in range(DT):
                    sp.dma_start(xpad[:, d, :], a["xpad"][:, d, :]).then_inc(x_loaded[d], 16)
                for name, dst in smalls[2:]:
                    sp.dma_start(dst[:], a[name]).then_inc(small_loaded, 16)

                def store_ops(j):
                    held(sp, vec, VEC * (j + 1), sp_turns)
                    for k, name in enumerate(("kt", "rt", "bh", "kh")):
                        store_tiles(sp, scr[name], j, outs[:, k], ops_stored)

                def body(j, s, first):
                    if not (known(j) and j < 2):
                        held(sp, lora_made, 6 * (j - 1), sp_turns)
                    sp.dma_start(lora2[:, s], a["lora2"][j]).then_inc(l_loaded[s], 16)
                    for k in range(2):
                        if not first:
                            held(sp, acc_made, 3 * (2 * j + k - 1), sp_turns)
                        sp.dma_start(wt[:, k], a["w_in"][k][j]).then_inc(w_loaded[k], 16)
                    if not first:
                        store_ops(j - 1)
                turns(sp, body)
                for p in range(2):
                    def job(i, first, p=p):
                        for s in range(2):
                            sp.wait_ge(acc_made, 3 * (16 + 8 * p + 2 * i + s - 1))
                            sp.dma_start(wt[:, s], a["w_in"][2 + p][2 * i + s]).then_inc(w_loaded[s], 16)
                        if first:
                            store_ops(DT - 1)
                    pairs(sp, p, job)
                sp.wait_ge(ops_stored, 128 * DT)

            @block.gpsimd
            def _(pool):
                def body(j, s, first):
                    held(pool, decayed, 3 * j + 1, pool_turns)
                    prompt, sample = both(decay[:, 1])
                    pool.memset(prompt.rearrange("p (c t) -> p c t", t=C)[:, :, 0:1], 1.0).then_inc(ones_set, 1)
                    pool.memset(sample[:, :, 0:1], 1.0).then_inc(ones_set, 1)
                turns(pool, body)

            @block.tensor
            def _(pe):
                pe.wait_ge(small_loaded, 16 * len(smalls))
                for p in range(2):
                    pe.wait_ge(mix_made, 2 * DT * (p + 1))
                    for k, (n0, n) in enumerate(PARTS):
                        turn = 3 * p + k
                        if turn >= 2:
                            pe.wait_ge(hid_made, turn - 1)
                        for d in range(DT):
                            mm = pe.matmul(side[0:64, turn % 2, 0:n], lora1[:, p, d, :], xs[:, p, d, n0:n0 + n],
                                           start=d == 0, stop=d == DT - 1)
                        mm.then_inc(hid_acc, 1)
                pe.wait_ge(hid_made, 6)

                def part(j_job, s, k, wait):
                    n0, n = PARTS[k]
                    if wait:
                        pe.wait_ge(evacuated, 3 * (j_job - 2) + k + 1)
                    for d in range(DT):
                        mm = pe.matmul(acc[:, s, k, 0:n], wt[:, s, d, :], xs[:, s, d, n0:n0 + n], start=d == 0, stop=d == DT - 1)
                    mm.then_inc(acc_made, 1)

                def dot_products(j):
                    pe.wait_ge(bonused, j + 1)
                    for t in range(TILES + 1):
                        n = min(128, N - 128 * t)
                        mm = pe.matmul(side[0:n, 1, 2 * t:2 * t + 2], bonus[:, 128 * t:128 * t + n], headpick[:], start=True, stop=True)
                    mm.then_inc(dotted, 1)

                def body(j, s, first):
                    pe.wait_ge(l_loaded[s], 8 * (j - s) + 16)
                    if not first:
                        pe.wait_ge(clamped, 3 * j)
                        if not (known(j) and j == 1):
                            pe.wait_ge(dots_kept, j - 1)
                    for l in range(2):
                        for k, (n0, n) in enumerate(PARTS):
                            turn = 3 * l + k
                            if turn >= 2:
                                pe.wait_ge(lora_kept, 6 * j + turn - 1)
                            pe.matmul(side[:, turn % 2, 0:n], lora2[:, s, l, :], hidden[:, l, n0:n0 + n], start=True, stop=True).then_inc(lora_made, 1)
                    if first:
                        pe.wait_ge(mix_made, 2 * DT * 3)
                    pe.wait_ge(w_loaded[0], 16 * (j + 1))
                    part(2 * j, 0, 0, not first)
                    pe.wait_ge(lora_kept, 6 * j + 6)
                    if not first:
                        dot_products(j - 1)
                    part(2 * j, 0, 1, not first)
                    part(2 * j, 0, 2, not first)
                    if first:
                        pe.wait_ge(mix_made, 2 * DT * 4)
                    pe.wait_ge(w_loaded[1], 16 * (j + 1))
                    part(2 * j + 1, 1, 0, not first)
                    pe.wait_ge(squared, j + 1)
                    for k, (n0, n) in enumerate(PARTS):
                        if k == 1 and not first:
                            pe.wait_ge(dots_kept, j)
                        if k == 2:
                            pe.wait_ge(clamped, 3 * j + 1)
                        pe.matmul(side[:, k % 2, 0:n], headsum[:], square[:, n0:n0 + n], start=True, stop=True).then_inc(summed, 1)
                    part(2 * j + 1, 1, 1, not first)
                    part(2 * j + 1, 1, 2, not first)
                turns(pe, body)
                for p in range(2):
                    pe.wait_ge(mix_made, 2 * DT * (5 + p))

                    def job(i, first, p=p):
                        for s in range(2):
                            pe.wait_ge(w_loaded[s], 16 * (DT + 4 * p + i + 1))
                            for k in range(3):
                                part_of(p, i, s, k)
                                if first and s == 0 and k == 1:
                                    pe.wait_ge(clamped, 3 * DT)
                                    dot_products(DT - 1)

                    def part_of(p, i, s, k):
                        n0, n = PARTS[k]
                        pe.wait_ge(evacuated, 3 * (16 + 8 * p + 2 * i + s - 2) + k + 1)
                        for d in range(DT):
                            mm = pe.matmul(acc[:, s, k, 0:n], wt[:, s, d, :], xs[:, p, d, n0:n0 + n], start=d == 0, stop=d == DT - 1)
                        mm.then_inc(acc_made, 1)
                    pairs(pe, p, job)

            @block.scalar
            def _(act):
                act.wait_ge(small_loaded, 16 * len(smalls))
                for p in range(2):
                    for k, (n0, n) in enumerate(PARTS):
                        turn = 3 * p + k
                        act.wait_ge(hid_acc, turn + 1)
                        act.activation(hidden[:, p, n0:n0 + n], side[0:64, turn % 2, 0:n], ACT.Tanh if p == 0 else ACT.Copy).then_inc(hid_made, 1)

                def body(j, s, first):
                    if not first:
                        act.wait_ge(summed_up, j)
                    if not (known(j) and j < 2):
                        act.wait_ge(vec, VEC * (j - 1))
                    for l in range(2):
                        for k, (n0, n) in enumerate(PARTS):
                            held(act, lora_made, 6 * j + 3 * l + k + 1, act_turns)
                            dst = (sigma[:, n0:n0 + n], step_size[:, s, n0:n0 + n])[l]
                            act.activation(dst, side[:, (3 * l + k) % 2, 0:n], ACT.Sigmoid, bias=(w0, a0)[l][:, ds(j, 1)]).then_inc(lora_kept, 1)
                    if not first:
                        act.wait_ge(vec, VEC * j)
                        act.wait_ge(bonused, j)
                        act.wait_ge(ones_set, 2 * j)
                    act.wait_ge(summed_up, j + 1)
                    act.activation(decay[:, 1, 1:N], decay[:, 0, 0:N - 1], ACT.Exp, scale=DECAY).then_inc(decayed, 1)
                    act.activation(decay[:, 2], decay[:, 0], ACT.Exp, scale=-DECAY).then_inc(decayed, 1)
                    act.wait_ge(decayed, 3 * j + 2)
                    act.activation(decay[:, 0], decay[:, 0], ACT.Exp, scale=DECAY).then_inc(decayed, 1)
                    for k, (n0, n) in enumerate(PARTS):
                        act.wait_ge(acc_made, 6 * j + k + 1)
                        act.activation(out[:, 0, n0:n0 + n], acc[:, 0, k, 0:n], ACT.Copy).then_inc(evacuated, 1)
                    if not first:
                        act.wait_ge(ops_stored, 128 * j)
                        act.wait_ge(summed, 3 * j)
                    held(act, evacuated, 6 * j + 3, act_turns)
                    act.activation(square[:], out[:, 0], ACT.Square, scale=k_k[:, ds(j, 1)]).then_inc(squared, 1)
                    act.activation(outs[:, 0], out[:, 0], ACT.Copy, scale=k_k[:, ds(j, 1)]).then_inc(keyed, 1)
                    act.wait_ge(clamped, 3 * j + 3)
                    act.activation(norm[:], norm[:], ACT.Sqrt).then_inc(rooted, 1)
                    for k, (n0, n) in enumerate(PARTS):
                        act.wait_ge(acc_made, 6 * j + 3 + k + 1)
                        act.activation(out[:, 1, n0:n0 + n], acc[:, 1, k, 0:n], ACT.Copy).then_inc(evacuated, 1)
                turns(act, body)
                act.wait_ge(vec, VEC * DT)
                act.wait_ge(bonused, DT)
                act.wait_ge(keyed, DT)
                for p, name in enumerate(("v", "g")):
                    def job(i, first, p=p, name=name):
                        for s in range(2):
                            n = 16 + 8 * p + 2 * i + s
                            if not first:
                                act.wait_ge(stored[s], 32 * (4 * p + i))
                            for k, (n0, width) in enumerate(PARTS):
                                act.wait_ge(acc_made, 3 * n + k + 1)
                                act.activation(out[:, s, n0:n0 + width], acc[:, s, k, 0:width], ACT.Silu if name == "g" else ACT.Copy).then_inc(evacuated, 1)
                            act.wait_ge(evacuated, 3 * n + 3)
                            store_tiles(act, scr[name], 2 * i + s, out[:, s], stored[s])
                    pairs(act, p, job)
                for s in range(2):
                    act.wait_ge(stored[s], 32 * DT)

            @block.vector
            def _(dve):
                dve.wait_ge(small_loaded, 32)

                def mix(p):
                    for d in range(DT):
                        if p == 0:
                            dve.wait_ge(x_loaded[d], 16)
                        pad = xpad[:, d, 1 + SEQ:].rearrange("p (b t) -> p b t", b=NB)
                        o, x = both(xs[:, p % 2, d, :]), (xpad[:, d, 1:1 + SEQ], pad[:, :, 1:1 + NT])
                        scale = mu[:, MU[p], d:d + 1]
                        dve.tensor_tensor(o[0], xpad[:, d, 0:SEQ], x[0], ALU.subtract).then_inc(shifted, 1)
                        dve.tensor_tensor(o[1], pad[:, :, 0:NT], x[1], ALU.subtract).then_inc(shifted, 1)
                        for k in range(2):
                            dve.wait_ge(shifted, 2 * DT * p + 2 * d + k + 1)
                            dve.scalar_tensor_tensor(o[k], o[k], scale, x[k], ALU.mult, ALU.add).then_inc(mix_made, 1)

                mix(0)
                mix(1)
                dve.wait_ge(hid_acc, 3)
                mix(2)
                dve.wait_ge(hid_acc, 6)
                mix(3)
                dve.wait_ge(small_loaded, 16 * len(smalls))

                def keep_dots(j):
                    dve.wait_ge(dotted, j + 1)
                    full = dots[:, 0:TILES, ds(2 * j, 2)]
                    dve.tensor_copy(full, side[:, 1, 0:2 * TILES].rearrange("p (t h) -> p t h", h=2))
                    dve.tensor_copy(dots[0:NB * NT, TILES:TILES + 1, ds(2 * j, 2)],
                                    side[0:NB * NT, 1, 2 * TILES:2 * TILES + 2].rearrange("p (t h) -> p t h", h=2)).then_inc(dots_kept, 1)

                def body(j, s, first):
                    k_in, r_in, a_in = out[:, 0], out[:, 1], step_size[:, s]
                    p_now, p_before, p_inverse = (decay[:, k] for k in range(3))
                    kt, rt, bh, kh = (outs[:, k] for k in range(4))
                    step = VEC * j
                    dve.wait_ge(lora_kept, 6 * j + 3)
                    if not first:
                        dve.wait_ge(vec, step)
                        dve.wait_ge(ends_kept, 2 * j)
                    dve.tensor_tensor_scan(p_now, reset[:], sigma[:], 0.0, ALU.mult, ALU.add).then_inc(summed_up, 1)
                    if not first:
                        keep_dots(j - 1)
                        dve.wait_ge(ops_stored, 128 * j)
                    if known(j) and j == DT - 1:
                        dve.wait_ge(acc_made, 3 * (2 * DT - 1))
                        mix(4)
                    dve.wait_ge(lora_kept, 6 * j + 6)
                    dve.tensor_scalar(kh, a_in, -1.0, k_a[:, ds(j, 1)], ALU.add, ALU.mult).then_inc(vec, 1)
                    dve.wait_ge(evacuated, 6 * j + 3)
                    dve.wait_ge(vec, step + 1)
                    dve.scalar_tensor_tensor(kh, kh, 1.0, k_in, ALU.add, ALU.mult).then_inc(vec, 1)
                    for k, (n0, n) in enumerate(PARTS):
                        dve.wait_ge(summed, 3 * j + k + 1)
                        dve.tensor_scalar(norm[:, n0:n0 + n], side[:, k % 2, 0:n], 1e-24, None, ALU.max).then_inc(clamped, 1)
                    dve.wait_ge(rooted, j + 1)
                    dve.reciprocal(norm[:], norm[:]).then_inc(vec, 1)
                    dve.wait_ge(keyed, j + 1)
                    dve.wait_ge(vec, step + 3)
                    dve.tensor_tensor(kt, kt, norm[:], ALU.mult).then_inc(vec, 1)
                    dve.wait_ge(vec, step + 4)
                    dve.tensor_tensor(bh, kt, a_in, ALU.mult).then_inc(vec, 1)
                    dve.wait_ge(ones_set, 2 * j + 2)
                    dve.wait_ge(vec, step + 5)
                    dve.tensor_tensor(kt, kt, p_before, ALU.mult).then_inc(vec, 1)
                    dve.wait_ge(decayed, 3 * j + 3)
                    dve.tensor_tensor(bh, bh, p_inverse, ALU.mult).then_inc(vec, 1)
                    prompt, sample = both(p_now)
                    dve.tensor_copy(keep["ends"][:, ds(j, 1), :],
                                    prompt.rearrange("p (o c t) -> p o c t", o=1, t=C)[:, :, :, C - 1]).then_inc(ends_kept, 1)
                    dve.tensor_copy(keep["ends_sample"][:, ds(j, 1), :],
                                    sample.rearrange("p (o b) t -> p o b t", o=1)[:, :, :, NT - 1]).then_inc(ends_kept, 1)
                    dve.wait_ge(evacuated, 6 * j + 6)
                    dve.scalar_tensor_tensor(bonus[:], r_in, r_k[:, ds(j, 1)], kh, ALU.mult, ALU.mult).then_inc(bonused, 1)
                    dve.tensor_tensor(rt, r_in, p_now, ALU.mult).then_inc(vec, 1)
                    dve.wait_ge(bonused, j + 1)
                    dve.tensor_tensor(kh, kh, p_inverse, ALU.mult).then_inc(vec, 1)
                turns(dve, body, last=True)
                dve.wait_ge(acc_made, 6 * DT)
                mix(5)
                keep_dots(DT - 1)
                dve.wait_ge(dots_kept, DT)
                chunks = keep["bonus"][:, 0:2 * TILES, :].rearrange("p (t q) j -> p t q j", q=2)
                for q in range(2):
                    for h in range(2):
                        src = dots[64 * q:64 * q + 64, 0:TILES, :].rearrange("p t (j h) -> p t j h", h=2)[:, :, :, h]
                        dve.tensor_copy(chunks[64 * h:64 * h + 64, :, q, :], src).then_inc(dots_kept, 1)
                for h in range(2):
                    src = dots[0:64, TILES:TILES + 1, :].rearrange("p t (j h) -> p t j h", h=2)[:, :, :, h]
                    dve.tensor_copy(keep["bonus"][64 * h:64 * h + 64, 2 * TILES:2 * TILES + 1, :], src).then_inc(dots_kept, 1)


def store_tiles(eng, dram, j, row, stored):
    tiles = dram.shape[2]
    eng.dma_start(dram[0:TILES].rearrange("t p j n -> p t j n")[:, :, j, :],
                  row[:, 0:SEQ].rearrange("p (t n) -> p t n", t=TILES)).then_inc(stored, 16)
    eng.dma_start(dram[TILES, :, j, 0:NB * NT], row[:, SEQ:N]).then_inc(stored, 16)


def delta_rule(nc, a, scr, keep, outp):
    with Tensors(nc, "delta") as m:
        ops, v_in, gate = m.sb("ops", 128, 4, DT, 128), m.sb("v_in", 128, DT, 128), m.sb("gate", 128, DT, 128)
        wide = m.sb("wide", 128, 4, 16, 128)
        grams = m.sb("grams", 128, 16, 4, 128)
        below = m.sb("below", 128, 16, 128)
        inv_t, inv = m.sb("inv_t", 128, 16, 128), m.sb("inv", 128, 16, 128)
        lm = m.sb("lm", 128, 4, 512)
        rows = m.sb("rows", 128, 2, 16, 128)
        v_rows = m.sb("v_rows", 128, 16, 64)
        small, pick = m.sb("small", 128, 16, 64), m.sb("pick", 128, 16, 64)
        coeff, solved, term = m.sb("coeff", 128, 16, 8), m.sb("solved", 128, 16, 8), m.sb("term", 128, 16, 8)
        state = m.sb("state", 128, 2, DT, 64)
        z, u = m.sb("z", 128, 2, 256), m.sb("u", 128, 2, 256)
        y, y2, y3 = m.sb("y", 128, DT, 64), m.sb("y2", 128, DT, 64), m.sb("y3", 128, DT, 64)
        stat = m.sb("stat", 128, 3, DT)
        gated = m.sb("gated", 128, DT, 128)
        gram_mask = m.sb("gram_mask", 128, 2, 4, 128)
        small_mask, block_mask = m.sb("small_mask", 128, 64), m.sb("block_mask", 128, 16)
        row_pick, unit8, level_mask = m.sb("row_pick", 128, 8), m.sb("unit8", 128, 8), m.sb("level_mask", 128, 3, 128)
        block_ones, ident = m.sb("block_ones", 128, 128), m.sb("ident", 128, 128)
        gn_g, gn_b = m.sb("gn_g", 128, DT, 64), m.sb("gn_b", 128, DT, 64)
        ga, gb = m.ps("ga", 128, 512), m.ps("gb", 128, 512)
        wb = m.ps("wb", 128, 2, 512)
        mb = m.ps("mb", 128, 4, 512)
        gbank = (ga, gb)
        consts_loaded = m.sem("consts_loaded")
        ops_loaded, v_loaded, gate_loaded = m.sem("ops_loaded"), m.sem("v_loaded"), m.sem("gate_loaded")
        zeroed, widened = m.sem("zeroed"), m.sem("widened")
        v_turned, v_kept = m.sem("v_turned"), m.sem("v_kept")
        rows_turned, rows_kept = m.sem("rows_turned"), m.sem("rows_kept")
        gram_made, gram_kept, gram_small = m.sem("gram_made"), m.sem("gram_kept"), m.sem("gram_small")
        coeff_made, picked, spread, solving, solved_wide = (m.sem(x) for x in ("coeff_made", "picked", "spread", "solving", "solved_wide"))
        inv_turned, inv_kept = m.sem("inv_turned"), m.sem("inv_kept")
        below_made, lm_made, lm_kept, grown, grown_kept = (m.sem(x) for x in ("below_made", "lm_made", "lm_kept", "grown", "grown_kept"))
        z_made, z_kept, u_made, u_kept, s_made, s_kept = (m.sem(x) for x in ("z_made", "z_kept", "u_made", "u_kept", "s_made", "s_kept"))
        y_made, normed, y_squared, y_rooted, y_turned, y_gated = (m.sem(x) for x in ("y_made", "normed", "y_squared", "y_rooted", "y_turned", "y_gated"))
        y_stored = m.sem("y_stored")
        pe_turns, pool_turns = m.sem("pe_turns"), m.sem("pool_turns")
        NORM = 10

        def passes(eng, body):
            body(0, (0, 1), True)
            with eng.Fori(1, TILES) as t:
                body(t, (0, 1), False)
            body(TILES, (0,), False)

        consts = (("gram_mask", gram_mask), ("small_mask", small_mask), ("block_mask", block_mask), ("row_pick", row_pick),
                  ("unit8", unit8), ("level_mask", level_mask), ("block_ones", block_ones), ("ident", ident),
                  ("gn_g", gn_g), ("gn_b", gn_b))
        sample = lambda qs: len(qs) == 1
        s_sample = m.sb("s_sample", 128, 2, NB, 64)
        spread8, spread_u, spread_v = m.sb("spread8", 128, NB, 64), m.sb("spread_u", 128, NB, 64), m.sb("spread_v", 128, NB, 64)
        seq_mask = m.sb("seq_mask", 128, NB)
        s_next, yr, y_own = m.sb("s_next", 128, NB, 64), m.sb("yr", 128, 64), m.sb("y_own", 128, DT, 64)
        s_loaded, s_stored = [m.sem(f"s_loaded{k}") for k in range(2)], m.sem("s_stored")
        big_made, own_z, own_u, own_u_kept, own_spread, own_y, own_s, own_yr, own_done, chained = (m.sem(x) for x in (
            "big_made", "own_z", "own_u", "own_u_kept", "own_spread", "own_y", "own_s", "own_yr", "own_done", "chained"))

        with nc.Block() as block:
            @block.sync
            def _(sp):
                for name, dst in consts:
                    sp.dma_start(dst[:], a[name]).then_inc(consts_loaded, 16)
                sp.dma_start(seq_mask[:], a["seq_mask"]).then_inc(consts_loaded, 16)

                def body(t, qs, first):
                    n = 64 * len(qs)
                    if not first:
                        sp.wait_ge(gram_made, 8 * t)
                        sp.wait_ge(widened, 8 * t)
                    for k, name in enumerate(("kt", "rt", "bh", "kh")):
                        sp.dma_start(ops[:, k, :, 0:n], scr[name][t, :, :, 0:n]).then_inc(ops_loaded, 16)
                    if not first:
                        sp.wait_ge(v_turned, 4 * t)
                    sp.dma_start(v_in[:, :, 0:n], scr["v"][t, :, :, 0:n]).then_inc(v_loaded, 16)
                    if not first:
                        sp.wait_ge(y_gated, 2 * t)
                        sp.dma_start(scr["y"][t - 1], gated[:]).then_inc(y_stored, 16)
                    sp.dma_start(gate[:, :, 0:n], scr["g"][t, :, :, 0:n]).then_inc(gate_loaded, 16)
                passes(sp, body)
                sp.wait_ge(s_kept, 8 * TILES)
                sp.dma_start(outp["wkv_prompt"], state[:, 0]).then_inc(s_stored, 16)
                for pair in range(DT):
                    if pair >= 2:
                        sp.wait_ge(own_done, pair - 1)
                    sp.dma_start(s_sample[:, pair % 2], a["s_sample"][:, pair]).then_inc(s_loaded[pair % 2], 16)
                    if pair:
                        sp.wait_ge(own_done, pair)
                        sp.dma_start(outp["wkv_sample"][:, pair - 1], s_next[:]).then_inc(s_stored, 16)
                sp.wait_ge(own_done, DT)
                sp.dma_start(outp["wkv_sample"][:, DT - 1], s_next[:]).then_inc(s_stored, 16)
                sp.wait_ge(y_gated, 2 * TILES + 1)
                sp.dma_start(scr["y"][TILES, :, :, 0:64], gated[:, :, 0:64]).then_inc(y_stored, 16)
                sp.wait_ge(y_stored, 16 * (TILES + 1))
                sp.wait_ge(s_stored, 16 * (DT + 1))

            @block.gpsimd
            def _(pool):
                pool.memset(wide[:], 0.0).then_inc(zeroed, 1)
                pool.memset(state[:], 0.0).then_inc(zeroed, 1)
                pool.wait_ge(consts_loaded, 176)
                pool.wait_ge(zeroed, 2)

                def body(t, qs, first):
                    nq = len(qs)
                    pool.wait_ge(ops_loaded, 64 * (t + 1))
                    if not first:
                        pool.wait_ge(below_made, 6 * t)
                    for at, k in enumerate((2, 3, 0, 1)):
                        if not first and k in (2, 3):
                            pool.wait_ge(gram_made, 8 * t)
                            pool.wait_ge(rows_turned, 8 * t)
                        elif not first:
                            pool.wait_ge(y_made, 2 * t)
                        pool.sem_inc(pool_turns, 1)
                        for h in range(2):
                            p = slice(64 * h, 64 * h + 64)
                            dst = wide[p, k].rearrange("p (q j) n -> p q j n", q=2)[:, 0:nq, :, 64 * h:64 * h + 64]
                            src = ops[p, k, :, 0:64 * nq].rearrange("p j (q n) -> p q j n", q=nq)
                            pool.tensor_copy(dst, src).then_inc(widened, 1)
                    for lev in range(3):
                        if lev == 0:
                            pool.wait_ge(widened, 8 * t + 8)
                            pool.wait_ge(gram_kept, 16 * t + 8 * nq)
                        pool.wait_ge(lm_made, 12 * t + 2 * nq * lev)
                        for q in range(nq):
                            pool.tensor_tensor(below[:, 8 * q:8 * q + 8], grams[:, 8 * q:8 * q + 8, 0, :],
                                               level_mask[:, lev:lev + 1, :].broadcast_to([128, 8, 128]), ALU.mult).then_inc(below_made, 1)
                passes(pool, body)

            @block.tensor
            def _(pe):
                pe.wait_ge(consts_loaded, 176)

                def body(t, qs, first):
                    nq, ng = len(qs), 2 * len(qs)
                    pe.wait_ge(v_loaded, 16 * (t + 1))
                    if not first:
                        pe.wait_ge(s_kept, 8 * t)
                    for g in range(ng):
                        if g >= 2:
                            pe.wait_ge(v_kept, 4 * t + g - 1)
                        pe.sem_inc(pe_turns, 1)
                        q, half = g // 2, g % 2
                        for j in range(4):
                            mm = pe.transpose(wb[0:64, g % 2, 128 * j:128 * j + 128],
                                              v_in[:, 4 * half + j, 64 * q:64 * q + 64], ident[:])
                        mm.then_inc(v_turned, 1)
                    pe.wait_ge(widened, 8 * t + 4)
                    for g in range(ng):
                        for k in range(2):
                            turn = 2 * g + k
                            if turn >= 4:
                                pe.wait_ge(rows_kept, 8 * t + turn - 3)
                            elif not first:
                                pe.wait_ge(z_kept, 4 * t)
                                pe.wait_ge(u_kept, 4 * t)
                            for j in range(4):
                                mm = pe.transpose(mb[:, turn % 4, 128 * j:128 * j + 128], wide[:, 2 + k, 4 * g + j, :], ident[:])
                            mm.then_inc(rows_turned, 1)
                    pe.wait_ge(ops_loaded, 64 * (t + 1))
                    for n in range(4 * nq):
                        if n >= 2:
                            pe.wait_ge(gram_kept, 16 * t + 2 * (n - 2) + 2)
                        elif not first:
                            pe.wait_ge(normed, NORM * 2 * t)
                            pe.wait_ge(y_gated, 2 * t)
                        for j in range(2):
                            unit = 2 * n + j
                            q, pair = unit // 8, unit % 8
                            rhs = ops[:, 0:2, pair, 64 * q:64 * q + 64]
                            for k in range(2):
                                mm = pe.matmul(gbank[n % 2][:, 256 * j + 128 * k:256 * j + 128 * k + 128],
                                               wide[:, 2 + k, unit, :], rhs, start=True, stop=True)
                        mm.then_inc(gram_made, 1)
                    for q in range(nq):
                        pe.wait_ge(picked, 2 * t + q + 1)
                        pe.wait_ge(v_kept, 4 * t + ng)
                        pe.matmul(wb[:, q, :], block_ones[:], pick[:, 8 * q:8 * q + 8, :], start=True, stop=True).then_inc(spread, 1)
                    pe.wait_ge(rows_kept, 8 * t + 4 * nq)
                    for g in range(ng):
                        pe.wait_ge(solved_wide, 2 * t + g // 2 + 1)
                        for j in range(4):
                            mm = pe.transpose(mb[:, g, 128 * j:128 * j + 128], inv_t[:, 4 * g + j, :], ident[:])
                        mm.then_inc(inv_turned, 1)
                    for lev in range(3):
                        for g0 in range(0, ng, 2):
                            for g in (g0, g0 + 1):
                                pe.wait_ge(below_made, 6 * t + nq * lev + g // 2 + 1)
                                if lev == 0:
                                    pe.wait_ge(inv_kept, 4 * t + g + 1)
                                else:
                                    pe.wait_ge(grown_kept, 20 * t + 2 * ng * (lev - 1) + 2 * g + 2)
                                if g >= 2:
                                    pe.wait_ge(lm_kept, 12 * t + ng * lev + g - 1)
                                for j in range(4):
                                    mm = pe.matmul(wb[:, g % 2, 128 * j:128 * j + 128], below[:, 4 * g + j, :], inv[:, 4 * g + j, :], start=True, stop=True)
                                mm.then_inc(lm_made, 1)
                            for g in (g0, g0 + 1):
                                pe.wait_ge(lm_kept, 12 * t + ng * lev + g + 1)
                                if lev == 0:
                                    pe.wait_ge(inv_kept, 4 * t + ng)
                                kept = 20 * t + 2 * ng * lev
                                if g >= 2:
                                    pe.wait_ge(grown_kept, kept + (2 if lev < 2 else 1) * (g - 1))
                                elif lev:
                                    pe.wait_ge(grown_kept, kept + 2 * (g - 1))
                                for j in range(4):
                                    mm = pe.matmul(mb[:, 2 * (g % 2), 128 * j:128 * j + 128], lm[:, g, 128 * j:128 * j + 128], inv_t[:, 4 * g + j, :], start=True, stop=True)
                                mm.then_inc(grown, 1)
                                if lev == 2:
                                    continue
                                for j in range(4):
                                    mm = pe.matmul(mb[:, 2 * (g % 2) + 1, 128 * j:128 * j + 128], inv_t[:, 4 * g + j, :], lm[:, g, 128 * j:128 * j + 128], start=True, stop=True)
                                mm.then_inc(grown, 1)
                    pe.wait_ge(grown_kept, 20 * t + 5 * ng)
                    pe.wait_ge(widened, 8 * t + 8)
                    if sample(qs):
                        sample_state()
                        return
                    for q in qs:
                        for half in range(2):
                            at = 4 * t + 2 * q + half
                            if q or not first:
                                pe.wait_ge(s_kept, 2 * (at - 1))
                            else:
                                pe.wait_ge(zeroed, 2)
                            if q:
                                pe.wait_ge(z_kept, at - 1)
                            for j in range(4):
                                unit, pair, o = 8 * q + 4 * half + j, 4 * half + j, mb[:, half, 64 * j:64 * j + 64]
                                pe.matmul(o, wide[:, 0, unit, :], state[:, q, pair, :], start=True, stop=False)
                                mm = pe.matmul(o, grams[:, unit, 2, :], v_rows[:, unit, :], start=False, stop=True)
                            mm.then_inc(z_made, 1)
                        for half in range(2):
                            pe.wait_ge(z_kept, 4 * t + 2 * q + half + 1)
                            if q:
                                pe.wait_ge(u_kept, 4 * t + 2 * q + half - 1)
                            for j in range(4):
                                unit = 8 * q + 4 * half + j
                                mm = pe.matmul(mb[:, 2 + half, 64 * j:64 * j + 64], inv_t[:, unit, :], z[:, half, 64 * j:64 * j + 64], start=True, stop=True)
                            mm.then_inc(u_made, 1)
                        for half in range(2):
                            pe.wait_ge(u_kept, 4 * t + 2 * q + half + 1)
                            for j in range(4):
                                unit, o = 8 * q + 4 * half + j, wb[:, half, 64 * j:64 * j + 64]
                                pe.matmul(o, rows[:, 0, unit, :], u[:, half, 64 * j:64 * j + 64], start=True, stop=False)
                                mm = pe.matmul(o, rows[:, 1, unit, :], v_rows[:, unit, :], start=False, stop=True)
                            mm.then_inc(s_made, 1)
                        if q:
                            pe.wait_ge(normed, NORM * (2 * t + q - 1) + 2)
                        for pair in range(8):
                            unit, half, o = 8 * q + pair, pair // 4, ga[:, 64 * pair:64 * pair + 64]
                            pe.matmul(o, wide[:, 1, unit, :], state[:, q, pair, :], start=True, stop=False)
                            pe.matmul(o, grams[:, unit, 1, :], u[:, half, 64 * (pair % 4):64 * (pair % 4) + 64], start=False, stop=False)
                            mm = pe.matmul(o, grams[:, unit, 3, :], v_rows[:, unit, :], start=False, stop=True)
                        mm.then_inc(y_made, 1)
                    for q in qs:
                        turn_y(2 * t + q)

                def turn_y(chunk):
                    pe.wait_ge(normed, NORM * (chunk + 1))
                    if not (isinstance(chunk, int) and chunk == 0):
                        pe.wait_ge(y_gated, chunk)
                    for j in range(4):
                        mm = pe.transpose(gb[:, 128 * j:128 * j + 128], y3[:, 2 * j:2 * j + 2, :], ident[:])
                    mm.then_inc(y_turned, 1)

                def sample_state():
                    for pair in range(DT):
                        k = pair % 2
                        pe.wait_ge(s_loaded[k], 16 * (pair // 2 + 1))
                        if pair:
                            pe.wait_ge(own_yr, pair)
                        pe.matmul(mb[:, 0, :], wide[:, 0, pair, :], s_sample[:, k], start=True, stop=True)
                        pe.matmul(mb[:, 1, :], wide[:, 1, pair, :], s_sample[:, k], start=True, stop=True)
                        pe.matmul(mb[:, 2, 0:64], grams[:, pair, 2, :], v_rows[:, pair, :], start=True, stop=True).then_inc(big_made, 1)
                        pe.wait_ge(own_z, pair + 1)
                        if pair:
                            pe.wait_ge(own_u_kept, pair)
                        pe.matmul(wb[:, 0, 0:64], inv_t[:, pair, :], z[:, 0, 0:64], start=True, stop=True).then_inc(own_u, 1)
                        pe.wait_ge(own_u_kept, pair + 1)
                        if pair:
                            pe.wait_ge(own_done, pair)
                        pe.matmul(mb[:, 3, 0:64], grams[:, pair, 1, :], u[:, 0, 0:64], start=True, stop=False)
                        pe.matmul(mb[:, 3, 0:64], grams[:, pair, 3, :], v_rows[:, pair, :], start=False, stop=True).then_inc(own_y, 1)
                        pe.wait_ge(own_spread, pair + 1)
                        pe.matmul(wb[:, 1, :], rows[:, 0, pair, :], spread_u[:], start=True, stop=False)
                        pe.matmul(wb[:, 1, :], rows[:, 1, pair, :], spread_v[:], start=False, stop=True).then_inc(own_s, 1)
                    turn_y(2 * TILES)

                passes(pe, body)

            @block.scalar
            def _(act):
                def body(t, qs, first):
                    nq, ng = len(qs), 2 * len(qs)
                    if not first:
                        act.wait_ge(y_made, 2 * t)
                        act.wait_ge(s_made, 4 * t)
                        act.wait_ge(normed, NORM * 2 * t)
                    for g in range(ng):
                        act.wait_ge(v_turned, 4 * t + g + 1)
                        src = wb[0:64, g % 2, :].rearrange("p (j n) -> p j n", j=4)
                        act.activation(v_rows[0:64, 4 * g:4 * g + 4, :], src[:, :, 0:64], ACT.Copy)
                        act.activation(v_rows[64:128, 4 * g:4 * g + 4, :], src[:, :, 64:128], ACT.Copy).then_inc(v_kept, 1)
                    for g in range(ng):
                        for k in range(2):
                            act.wait_ge(rows_turned, 8 * t + 2 * g + k + 1)
                            act.activation(rows[:, k, 4 * g:4 * g + 4, :], mb[:, (2 * g + k) % 4, :].rearrange("p (j n) -> p j n", j=4),
                                           ACT.Copy, scale=-1.0 if k == 0 else 1.0).then_inc(rows_kept, 1)
                    for g in range(ng):
                        act.wait_ge(inv_turned, 4 * t + g + 1)
                        act.activation(inv[:, 4 * g:4 * g + 4, :], mb[:, g, :].rearrange("p (j n) -> p j n", j=4), ACT.Copy).then_inc(inv_kept, 1)
                    for lev in range(3):
                        for g in range(ng):
                            act.wait_ge(lm_made, 12 * t + ng * lev + g + 1)
                            if lev:
                                act.wait_ge(grown, 20 * t + 2 * ng * (lev - 1) + 2 * g + 2)
                            elif not first:
                                act.wait_ge(grown, 20 * t)
                            act.activation(lm[:, g, :], wb[:, g % 2, :], ACT.Copy).then_inc(lm_kept, 1)
                    for pair in range(DT) if sample(qs) else ():
                        act.wait_ge(own_u, pair + 1)
                        if pair:
                            act.wait_ge(own_y, pair)
                            act.wait_ge(own_spread, pair)
                        else:
                            act.wait_ge(s_made, 4 * TILES)
                        act.activation(u[:, 0, 0:64], wb[:, 0, 0:64], ACT.Copy).then_inc(own_u_kept, 1)
                    for q in () if sample(qs) else qs:
                        for half in range(2):
                            n = 4 * t + 2 * q + half
                            act.wait_ge(z_made, n + 1)
                            if q or not first:
                                act.wait_ge(u_made, n - 1)
                            act.activation(z[:, half], mb[:, half, 0:256], ACT.Copy).then_inc(z_kept, 1)
                        for half in range(2):
                            n = 4 * t + 2 * q + half
                            act.wait_ge(u_made, n + 1)
                            if q or not first:
                                act.wait_ge(s_made, n - 1)
                                act.wait_ge(y_made, 2 * t + q)
                            act.activation(u[:, half], mb[:, 2 + half, 0:256], ACT.Copy).then_inc(u_kept, 1)
                    for q in qs:
                        chunk = 2 * t + q
                        act.wait_ge(normed, NORM * chunk + 2)
                        act.activation(y2[:], y[:], ACT.Square).then_inc(y_squared, 1)
                        act.wait_ge(normed, NORM * chunk + 4)
                        act.activation(stat[:, 1], stat[:, 1], ACT.Sqrt).then_inc(y_rooted, 1)
                passes(act, body)

            @block.vector
            def _(dve):
                dve.wait_ge(consts_loaded, 176)

                def norm(t, q, y_in):
                    chunk = 2 * t + q
                    at = NORM * chunk

                    def per(x):
                        return x[:, :].rearrange("p (j o) -> p j o", o=1).broadcast_to([128, DT, 64])

                    dve.wait_ge(normed, at) if not (isinstance(t, int) and chunk == 0) else None
                    dve.tensor_reduce(stat[:, 0], y_in, AX, ALU.add).then_inc(normed, 1)
                    dve.wait_ge(normed, at + 1)
                    if not (isinstance(t, int) and chunk == 0):
                        dve.wait_ge(y_turned, chunk)
                    dve.scalar_tensor_tensor(y[:], per(stat[:, 0]), -1.0 / HD, y_in, ALU.mult, ALU.add).then_inc(normed, 1)
                    dve.wait_ge(y_squared, chunk + 1)
                    dve.tensor_reduce(stat[:, 2], y2[:], AX, ALU.add).then_inc(normed, 1)
                    dve.wait_ge(normed, at + 3)
                    dve.tensor_scalar(stat[:, 1], stat[:, 2], 1.0 / HD, GN_EPS, ALU.mult, ALU.add).then_inc(normed, 1)
                    dve.wait_ge(y_rooted, chunk + 1)
                    dve.reciprocal(stat[:, 2], stat[:, 1]).then_inc(normed, 1)
                    dve.wait_ge(normed, at + 5)
                    dve.tensor_tensor(y[:], y[:], per(stat[:, 2]), ALU.mult).then_inc(normed, 1)
                    bonus = keep["bonus"][:, ds(chunk, 1), :].rearrange("p o (j u) -> p (o j) u", u=1).broadcast_to([128, DT, 64])
                    dve.tensor_tensor(y2[:], v_rows[:, 8 * q:8 * q + 8, :], bonus, ALU.mult).then_inc(normed, 1)
                    dve.wait_ge(normed, at + 6)
                    dve.tensor_tensor(y[:], y[:], gn_g[:], ALU.mult).then_inc(normed, 1)
                    dve.wait_ge(normed, at + 8)
                    dve.tensor_tensor(y[:], y[:], gn_b[:], ALU.add).then_inc(normed, 1)
                    dve.wait_ge(normed, at + 9)
                    dve.tensor_tensor(y3[:], y[:], y2[:], ALU.add).then_inc(normed, 1)
                    dve.wait_ge(y_turned, chunk + 1)
                    dve.wait_ge(gate_loaded, 16 * (t + 1))
                    if q == 0 and not (isinstance(t, int) and t == 0):
                        dve.wait_ge(y_stored, 16 * t)
                    dve.tensor_tensor(gated[:, :, 64 * q:64 * q + 64], gb[:, :].rearrange("p (j n) -> p j n", j=DT),
                                      gate[:, :, 64 * q:64 * q + 64], ALU.mult).then_inc(y_gated, 1)

                def body(t, qs, first):
                    nq, ng = len(qs), 2 * len(qs)
                    kind = 1 if sample(qs) else 0
                    if not first:
                        dve.wait_ge(y_made, 2 * t)
                        dve.wait_ge(below_made, 6 * t)
                    for n in range(4 * nq):
                        dve.wait_ge(gram_made, 8 * t + n + 1)
                        bank = gbank[n % 2]
                        two = bank[:, :].rearrange("p (j k n) -> p j k n", j=2, k=4)
                        dve.tensor_tensor(small[:, 2 * n:2 * n + 2, :], two[:, :, 0, :],
                                          small_mask[:, :].rearrange("p (o n) -> p o n", o=1).broadcast_to([128, 2, 64]), ALU.mult).then_inc(gram_small, 1)
                        for j in range(2):
                            src = two[:, j].rearrange("p k (o n) -> p k o n", o=1).broadcast_to([128, 4, 2, 64])
                            dve.tensor_tensor(grams[:, 2 * n + j].rearrange("p k (h n) -> p k h n", h=2), src,
                                              gram_mask[:, kind].rearrange("p k (h n) -> p k h n", h=2), ALU.mult).then_inc(gram_kept, 1)
                    nu = 8 * nq
                    dve.wait_ge(gram_small, 8 * t + 4 * nq)
                    dve.tensor_reduce(coeff[:, 0:nu, :], small[:, 0:nu, :].rearrange("p u (b n) -> p u n b", b=8), AX, ALU.add).then_inc(coeff_made, 1)
                    dve.wait_ge(coeff_made, t + 1)
                    for q in range(nq):
                        src = coeff[:, 8 * q:8 * q + 8, :].rearrange("p u (o n) -> p u o n", o=1).broadcast_to([128, 8, 8, 8])
                        sel = row_pick[:, :].rearrange("p (u j n) -> p u j n", u=1, n=1).broadcast_to([128, 8, 8, 8])
                        dve.tensor_tensor(pick[:, 8 * q:8 * q + 8, :].rearrange("p u (j n) -> p u j n", j=8), src, sel, ALU.mult).then_inc(picked, 1)
                    at = 15 * t
                    dve.tensor_copy(solved[:, 0:nu, :], unit8[:, :].rearrange("p (o n) -> p o n", o=1).broadcast_to([128, nu, 8])).then_inc(solving, 1)
                    dve.wait_ge(spread, 2 * t + nq)
                    blocks = wb[:, 0:nq, :].rearrange("p q (u j n) -> p (q u) j n", u=8, j=8)
                    for j in range(7):
                        dve.wait_ge(solving, at + 2 * j + 1)
                        left = solved[:, 0:nu, j:j + 1].broadcast_to([128, nu, 7 - j])
                        dve.tensor_tensor(term[:, 0:nu, 0:7 - j], left, blocks[:, :, j, j + 1:8], ALU.mult).then_inc(solving, 1)
                        dve.wait_ge(solving, at + 2 * j + 2)
                        dve.tensor_tensor(solved[:, 0:nu, j + 1:8], solved[:, 0:nu, j + 1:8], term[:, 0:nu, 0:7 - j], ALU.add).then_inc(solving, 1)
                    dve.wait_ge(solving, at + 15)
                    for q in range(nq):
                        src = solved[:, 8 * q:8 * q + 8, :].rearrange("p u (o n) -> p u o n", o=1).broadcast_to([128, 8, 16, 8])
                        sel = block_mask[:, :].rearrange("p (u b n) -> p u b n", u=1, n=1).broadcast_to([128, 8, 16, 8])
                        if not first:
                            dve.wait_ge(u_made, 4 * t)
                        dve.tensor_tensor(inv_t[:, 8 * q:8 * q + 8, :].rearrange("p u (b n) -> p u b n", b=16), src, sel, ALU.mult).then_inc(solved_wide, 1)
                    for lev in range(3):
                        each = 2 if lev < 2 else 1
                        for g in range(ng):
                            for k in range(each):
                                if k == 0:
                                    dve.wait_ge(grown, 20 * t + 2 * ng * lev + each * (g + 1))
                                dst = (inv_t, inv)[k][:, 4 * g:4 * g + 4, :]
                                dve.tensor_tensor(dst, dst, mb[:, 2 * (g % 2) + k, :].rearrange("p (j n) -> p j n", j=4), ALU.add).then_inc(grown_kept, 1)
                    if sample(qs):
                        sample_state()
                        return
                    for q in qs:
                        for half in range(2):
                            n = 4 * t + 2 * q + half
                            dve.wait_ge(s_made, n + 1)
                            new = state[:, 1 - q, 4 * half:4 * half + 4, :]
                            if half == 0 and (q or not first):
                                dve.wait_ge(y_made, 2 * t + q)
                            dve.tensor_tensor(new, state[:, q, 4 * half:4 * half + 4, :],
                                              wb[:, half, 0:256].rearrange("p (j n) -> p j n", j=4), ALU.add).then_inc(s_kept, 1)
                            dve.wait_ge(s_kept, 2 * n + 1)
                            end = keep["ends"][:, 4 * half:4 * half + 4, ds(2 * t + q, 1)].broadcast_to([128, 4, 64])
                            dve.tensor_tensor(new, new, end, ALU.mult).then_inc(s_kept, 1)
                        dve.wait_ge(y_made, 2 * t + q + 1)
                        norm(t, q, ga[:, :].rearrange("p (j n) -> p j n", j=DT))

                def sample_state():
                    own = seq_mask[:, :].rearrange("p (b o) -> p b o", o=1).broadcast_to([128, NB, 64])
                    count = [0]

                    def then(ins):
                        count[0] += 1
                        ins.then_inc(chained, 1)
                        dve.wait_ge(chained, count[0])

                    for pair in range(DT):
                        if not pair:
                            dve.wait_ge(u_made, 4 * TILES)
                        dve.wait_ge(big_made, pair + 1)
                        then(dve.tensor_tensor(spread8[:], mb[:, 0, :].rearrange("p (b n) -> p b n", b=NB), own, ALU.mult))
                        then(dve.tensor_reduce(z[:, 1, 0:64], spread8[:].rearrange("p b n -> p n b"), AX, ALU.add))
                        dve.tensor_tensor(z[:, 0, 0:64], z[:, 1, 0:64], mb[:, 2, 0:64], ALU.add).then_inc(own_z, 1)
                        then(dve.tensor_tensor(spread8[:], mb[:, 1, :].rearrange("p (b n) -> p b n", b=NB), own, ALU.mult))
                        dve.tensor_reduce(yr[:], spread8[:].rearrange("p b n -> p n b"), AX, ALU.add).then_inc(own_yr, 1)
                        dve.wait_ge(own_u_kept, pair + 1)
                        if pair:
                            dve.wait_ge(own_s, pair)
                        for dst, src in ((spread_v, v_rows[:, pair:pair + 1, :]), (spread_u, u[:, 0:1, 0:64])):
                            ins = dve.tensor_tensor(dst[:], src.broadcast_to([128, NB, 64]), own, ALU.mult)
                        ins.then_inc(own_spread, 1)
                        dve.wait_ge(own_y, pair + 1)
                        dve.wait_ge(own_yr, pair + 1)
                        then(dve.tensor_tensor(y_own[:, pair, :], yr[:], mb[:, 3, 0:64], ALU.add))
                        dve.wait_ge(own_s, pair + 1)
                        if pair:
                            dve.wait_ge(s_stored, 16 * (pair + 1))
                        then(dve.tensor_tensor(s_next[:], s_sample[:, pair % 2], wb[:, 1, :].rearrange("p (b n) -> p b n", b=NB), ALU.add))
                        end = keep["ends_sample"][:, pair, :].rearrange("p (b o) -> p b o", o=1).broadcast_to([128, NB, 64])
                        dve.tensor_tensor(s_next[:], s_next[:], end, ALU.mult).then_inc(own_done, 1)
                    dve.wait_ge(chained, count[0])
                    norm(TILES, 0, y_own[:])

                passes(dve, body)


def project_and_norm(nc, a, stage, weights, gain, shift, rhs, load_rhs, residual, load_residual, result, store):
    with Tensors(nc, stage) as m:
        wt = m.sb("wt", 128, 2, DT, 128)
        total, square = m.sb("total", 128, DT, N), m.sb("square", 128, DT, N)
        rstd = m.sb("rstd", 128, N)
        g, b, mean_ones = m.sb("g", 128, DT), m.sb("b", 128, DT), m.sb("mean_ones", 128, 128)
        acc = m.ps("acc", 128, 2, 3, 512)
        small_loaded, rhs_loaded, res_loaded = m.sem("small_loaded"), m.sem("rhs_loaded"), m.sem("res_loaded")
        w_loaded = [m.sem(f"w_loaded{i}") for i in range(2)]
        acc_made, added, mean_made, centred, squared, var_made = (m.sem(x) for x in ("acc_made", "added", "mean_made", "centred", "squared", "var_made"))
        shifted, rooted, inverted, scaled, finished, stored = (m.sem(x) for x in ("shifted", "rooted", "inverted", "scaled", "finished", "stored"))

        def jobs(eng, body):
            body(0, True)
            with eng.Fori(1, DT // 2) as i:
                body(i, False)

        with nc.Block() as block:
            @block.sync
            def _(sp):
                for dst, src in ((g, gain), (b, shift), (mean_ones, a["mean_ones"])):
                    sp.dma_start(dst[:], src).then_inc(small_loaded, 16)
                n_rhs = load_rhs(sp, rhs_loaded)

                def body(i, first):
                    for s in range(2):
                        if not first:
                            sp.wait_ge(acc_made, 3 * (2 * i + s - 1))
                        sp.dma_start(wt[:, s], weights[2 * i + s]).then_inc(w_loaded[s], 16)
                    if first:
                        load_residual(sp, res_loaded)
                jobs(sp, body)
                if store is not None:
                    sp.wait_ge(finished, DT)
                    store(sp, stored)

            @block.tensor
            def _(pe):
                pe.wait_ge(rhs_loaded, rhs_count(load_rhs))

                def body(i, first):
                    for s in range(2):
                        pe.wait_ge(w_loaded[s], 16 * (i + 1))
                        for k, (n0, n) in enumerate(PARTS):
                            if not first:
                                pe.wait_ge(added, 3 * (2 * i + s - 2) + k + 1)
                            for d in range(DT):
                                mm = pe.matmul(acc[:, s, k, 0:n], wt[:, s, d, :], rhs[:, d, n0:n0 + n], start=d == 0, stop=d == DT - 1)
                            mm.then_inc(acc_made, 1)
                jobs(pe, body)
                pe.wait_ge(small_loaded, 48)
                pe.wait_ge(added, 3 * DT)
                for src, s, ready, made in ((total, 0, None, mean_made), (square, 1, squared, var_made)):
                    for k, (n0, n) in enumerate(PARTS):
                        if ready is not None:
                            pe.wait_ge(ready, k + 1)
                        for d in range(DT):
                            mm = pe.matmul(acc[:, s, k, 0:n], mean_ones[:], src[:, d, n0:n0 + n], start=d == 0, stop=d == DT - 1)
                        mm.then_inc(made, 1)

            @block.vector
            def _(dve):
                dve.wait_ge(res_loaded, rhs_count(load_residual))

                def body(i, first):
                    for s in range(2):
                        for k, (n0, n) in enumerate(PARTS):
                            dve.wait_ge(acc_made, 3 * (2 * i + s) + k + 1)
                            row = residual[:, ds(2 * i + s, 1), n0:n0 + n].rearrange("p o n -> p (o n)")
                            out = total[:, ds(2 * i + s, 1), n0:n0 + n].rearrange("p o n -> p (o n)")
                            dve.scalar_tensor_tensor(out, row, ALPHA, acc[:, s, k, 0:n], ALU.mult, ALU.add).then_inc(added, 1)
                jobs(dve, body)
                for k, (n0, n) in enumerate(PARTS):
                    dve.wait_ge(mean_made, k + 1)
                    mean = acc[:, 0, k:k + 1, 0:n].broadcast_to([128, DT, n])
                    dve.tensor_tensor(total[:, :, n0:n0 + n], total[:, :, n0:n0 + n], mean, ALU.subtract).then_inc(centred, 1)
                for k, (n0, n) in enumerate(PARTS):
                    dve.wait_ge(var_made, k + 1)
                    dve.tensor_scalar(rstd[:, n0:n0 + n], acc[:, 1, k, 0:n], LN_EPS, None, ALU.add).then_inc(shifted, 1)
                for k, (n0, n) in enumerate(PARTS):
                    dve.wait_ge(rooted, k + 1)
                    dve.reciprocal(rstd[:, n0:n0 + n], rstd[:, n0:n0 + n]).then_inc(inverted, 1)
                for k, (n0, n) in enumerate(PARTS):
                    dve.wait_ge(inverted, k + 1)
                    inv = rstd[:, n0:n0 + n].rearrange("p (o n) -> p o n", o=1).broadcast_to([128, DT, n])
                    dve.tensor_tensor(total[:, :, n0:n0 + n], total[:, :, n0:n0 + n], inv, ALU.mult).then_inc(scaled, 1)

            @block.scalar
            def _(act):
                act.wait_ge(small_loaded, 48)
                act.wait_ge(acc_made, 3 * DT)
                for k, (n0, n) in enumerate(PARTS):
                    act.wait_ge(centred, k + 1)
                    act.activation(square[:, :, n0:n0 + n], total[:, :, n0:n0 + n], ACT.Square).then_inc(squared, 1)
                for k, (n0, n) in enumerate(PARTS):
                    act.wait_ge(shifted, k + 1)
                    act.activation(rstd[:, n0:n0 + n], rstd[:, n0:n0 + n], ACT.Sqrt).then_inc(rooted, 1)
                act.wait_ge(scaled, 3)
                for d in range(DT):
                    act.activation(result[:, d, :], total[:, d, :], ACT.Identity, scale=g[:, d:d + 1], bias=b[:, d:d + 1]).then_inc(finished, 1)


def rhs_count(load):
    return 16 * load.count


def attention_projections(nc, a, scr, x):
    with Tensors(nc, "qkvg") as m:
        wt, out = m.sb("wt", 128, 2, DT, 128), m.sb("out", 128, 2, N)
        acc = m.ps("acc", 128, 2, 3, 512)
        w_loaded = [m.sem(f"w_loaded{i}") for i in range(2)]
        stored = [m.sem(f"stored{i}") for i in range(2)]
        acc_made, evacuated = m.sem("acc_made"), m.sem("evacuated")
        phases = (("aq", 0, DT), ("ak", DT, 2), ("av", DT + 2, 2), ("ag", DT + 4, DT))

        def pairs(eng, p, body):
            if p == 0:
                body(0, 0, True)
            start = 1 if p == 0 else 0
            with eng.Fori(start, phases[p][2] // 2) as i:
                body(i, phases[p][1] + 2 * i, False)

        with nc.Block() as block:
            @block.sync
            def _(sp):
                for p in range(len(phases)):
                    def body(i, job, first):
                        for s in range(2):
                            if not first:
                                sp.wait_ge(acc_made, 3 * (job + s - 1))
                            sp.dma_start(wt[:, s], a["w_att"][job + s]).then_inc(w_loaded[s], 16)
                    pairs(sp, p, body)

            @block.tensor
            def _(pe):
                for p in range(len(phases)):
                    def body(i, job, first, p=p):
                        for s in range(2):
                            pe.wait_ge(w_loaded[s], 16 * (phases[p][1] // 2 + i + 1))
                            for k, (n0, n) in enumerate(PARTS):
                                if not first:
                                    pe.wait_ge(evacuated, 3 * (job + s - 2) + k + 1)
                                for d in range(DT):
                                    mm = pe.matmul(acc[:, s, k, 0:n], wt[:, s, d, :], x[:, d, n0:n0 + n], start=d == 0, stop=d == DT - 1)
                                mm.then_inc(acc_made, 1)
                    pairs(pe, p, body)

            @block.scalar
            def _(act):
                for p, (name, job0, _) in enumerate(phases):
                    def body(i, job, first, name=name, job0=job0):
                        for s in range(2):
                            if not first:
                                act.wait_ge(stored[s], 32 * (job0 // 2 + i))
                            for k, (n0, n) in enumerate(PARTS):
                                act.wait_ge(acc_made, 3 * (job + s) + k + 1)
                                act.activation(out[:, s, n0:n0 + n], acc[:, s, k, 0:n], ACT.Silu if name == "ag" else ACT.Copy).then_inc(evacuated, 1)
                            act.wait_ge(evacuated, 3 * (job + s) + 3)
                            store_tiles(act, scr[name], 2 * i + s, out[:, s], stored[s])
                    pairs(act, p, body)
                for s in range(2):
                    act.wait_ge(stored[s], 32 * 10)


def attention(nc, a, scr, outp, o):
    with Tensors(nc, "att") as m:
        q_in, k_in = m.sb("q_in", 128, DT, 128), m.sb("k_in", 128, 2, 128)
        v_in, gate = m.sb("v_in", 128, 2, 128), m.sb("gate", 128, DT, 128)
        keys = m.sb("keys", 128, KVH, 2, 2, 128)
        v_rows = m.sb("v_rows", 128, 2, 256)
        bias = m.sb("bias", 128, H, 3, 128)
        score = m.sb("score", 128, H, 256)
        prob_t = m.sb("prob_t", 128, 2, 2, 512)
        sink, ident = m.sb("sink", 128, H), m.sb("ident", 128, 128)
        top, low, sums, extra, recip = (m.sb(x, 128, H) for x in ("top", "low", "sums", "extra", "recip"))
        sc = m.ps("sc", 128, 2, 512)
        turn = m.ps("turn", 128, 4, 512)
        pv = m.ps("pv", 128, 2, 512)
        small_loaded, zeroed, loaded, gate_loaded = (m.sem(x) for x in ("small_loaded", "zeroed", "loaded", "gate_loaded"))
        v_turned, v_kept, widened = m.sem("v_turned"), m.sem("v_kept"), m.sem("widened")
        scored, biased, lowered, raised, divided, normed = (m.sem(x) for x in ("scored", "biased", "lowered", "raised", "divided", "normed"))
        vec, p_turned, p_kept, mixed, gated = (m.sem(x) for x in ("vec", "p_turned", "p_kept", "mixed", "gated"))
        sunk, copied = m.sem("sunk"), m.sem("copied")
        dve_turns, pool_turns = m.sem("dve_turns"), m.sem("pool_turns")

        def blocks(eng, body):
            body(0, 0)
            body(1, 1)
            with eng.Fori(1, TILES // 2) as i:
                body(2 * i, 0)
                body(2 * i + 1, 1)

        def is0(t):
            return isinstance(t, int) and t == 0

        with nc.Block() as block:
            @block.sync
            def _(sp):
                for dst, name in ((bias, "bias"), (sink, "sink"), (ident, "ident")):
                    sp.dma_start(dst[:], a[name]).then_inc(small_loaded, 16)

                def body(t, slot):
                    if not is0(t):
                        sp.wait_ge(scored, 8 * t)
                        sp.wait_ge(widened, 8 * t)
                        sp.wait_ge(v_turned, t)
                    for dst, name in ((q_in, "aq"), (k_in, "ak"), (v_in, "av")):
                        sp.dma_start(dst[:], scr[name][t]).then_inc(loaded, 16)
                    if not is0(t):
                        sp.wait_ge(gated, 8 * t)
                    sp.dma_start(gate[:], scr["ag"][t]).then_inc(gate_loaded, 16)
                blocks(sp, body)
                sp.dma_start(outp["k_prompt"], scr["ak"][TILES - 1]).then_inc(copied, 16)
                sp.dma_start(outp["v_prompt"], scr["av"][TILES - 1]).then_inc(copied, 16)
                sp.wait_ge(copied, 32)

            @block.gpsimd
            def _(pool):
                pool.memset(keys[:], 0.0).then_inc(zeroed, 1)
                pool.wait_ge(zeroed, 1)

                def body(t, slot):
                    pool.wait_ge(loaded, 48 * (t + 1))
                    if not is0(t):
                        pool.wait_ge(scored, 8 * t)
                    pool.sem_inc(pool_turns, 1)
                    for n in range(KVH):
                        for h in range(2):
                            pool.tensor_copy(keys[64 * h:64 * h + 64, n, h, slot, :],
                                             k_in[64 * (n % 2):64 * (n % 2) + 64, n // 2, :]).then_inc(widened, 1)
                blocks(pool, body)

            @block.tensor
            def _(pe):
                pe.wait_ge(small_loaded, 48)

                def body(t, slot):
                    pe.wait_ge(loaded, 48 * (t + 1))
                    if not is0(t):
                        pe.wait_ge(gated, 8 * t)
                        pe.wait_ge(p_kept, 8 * t)
                    for j in range(2):
                        mm = pe.transpose(turn[:, 0, 128 * j:128 * j + 128], v_in[:, j, :], ident[:])
                    mm.then_inc(v_turned, 1)
                    pe.wait_ge(widened, 8 * (t + 1))
                    first = is0(t)
                    for pair in range(8):
                        if pair >= 2:
                            pe.wait_ge(biased, 16 * t + 2 * (pair - 1))
                        rhs = keys[:, pair // 2, :, 0, :] if first else keys[:, pair // 2]
                        n = 256 if first else 512
                        pe.matmul(sc[:, pair % 2, 0:n], q_in[:, pair, :], rhs, start=True, stop=True).then_inc(scored, 1)
                    pe.wait_ge(v_kept, t + 1)
                    for g in range(KVH):
                        pe.wait_ge(normed, 16 * t + 4 * g + 4)
                        for s in (0,) if first else (0, 1):
                            bank = 2 * (g % 2) + s
                            if g >= 2:
                                pe.wait_ge(p_kept, 8 * t + 2 * (g - 1))
                            for h in range(4):
                                mm = pe.transpose(turn[:, bank, 128 * h:128 * h + 128], score[:, 4 * g + h, 128 * s:128 * s + 128], ident[:])
                            mm.then_inc(p_turned, 2 if first else 1)
                        pe.wait_ge(p_kept, 8 * t + 2 * g + 2)
                        if g >= 2:
                            pe.wait_ge(gated, 8 * t + 2 * (g - 1))
                        for s in (0,) if first else (0, 1):
                            mm = pe.matmul(pv[0:64, g % 2, :], v_rows[:, s, 64 * g:64 * g + 64], prob_t[:, g % 2, s, :],
                                           start=s == 0, stop=first or s == 1)
                        mm.then_inc(mixed, 1)
                blocks(pe, body)

            @block.scalar
            def _(act):
                def body(t, slot):
                    first = is0(t)
                    act.wait_ge(v_turned, t + 1)
                    if not first:
                        act.wait_ge(mixed, 4 * t)
                    act.activation(v_rows[:, slot, :], turn[:, 0, 0:256], ACT.Copy).then_inc(v_kept, 1)
                    width = 128 if first else 256
                    for half in range(2):
                        act.wait_ge(lowered, 2 * t + half + 1)
                        for h in range(8 * half, 8 * half + 8):
                            act.activation(score[:, h, 0:width], score[:, h, 0:width], ACT.Exp, bias=low[:, h:h + 1],
                                           accum_out=sums[:, h:h + 1]).then_inc(raised, 1)
                        act.wait_ge(sunk, 2 * t + half + 1)
                        act.activation(extra[:, 8 * half:8 * half + 8], extra[:, 8 * half:8 * half + 8], ACT.Exp).then_inc(raised, 1)
                    for g in range(KVH):
                        for s in (0,) if first else (0, 1):
                            act.wait_ge(p_turned, 8 * t + 2 * g + s + 1)
                            if g >= 2:
                                act.wait_ge(mixed, 4 * t + g - 1)
                            act.activation(prob_t[:, g % 2, s, :], turn[:, 2 * (g % 2) + s, :], ACT.Copy).then_inc(p_kept, 2 if first else 1)
                blocks(act, body)

            @block.vector
            def _(dve):
                dve.wait_ge(small_loaded, 48)

                def body(t, slot):
                    first = is0(t)
                    width = 128 if first else 256
                    if not first:
                        dve.wait_ge(p_turned, 8 * t)
                    for half in range(2):
                        hs = slice(8 * half, 8 * half + 8)
                        for pair in range(4 * half, 4 * half + 4):
                            held(dve, scored, 8 * t + pair + 1, dve_turns)
                            for h in range(2):
                                head = 2 * pair + h
                                table = bias[:, head, 1:2] if first else bias[:, head, 1 - slot:3 - slot]
                                src = sc[:, pair % 2, width * h:width * h + width].rearrange("p (s n) -> p s n", n=128)
                                dve.tensor_tensor_reduce(score[:, head, 0:width].rearrange("p (s n) -> p s n", n=128), src, table,
                                                         SCALE, -1e30, ALU.add, ALU.max, top[:, head:head + 1]).then_inc(biased, 1)
                        at = 8 * t + 4 * half
                        dve.wait_ge(biased, 16 * t + 8 * half + 8)
                        dve.tensor_tensor(low[:, hs], top[:, hs], sink[:, hs], ALU.max).then_inc(vec, 1)
                        dve.wait_ge(vec, at + 1)
                        dve.tensor_scalar(low[:, hs], low[:, hs], -1.0, None, ALU.mult).then_inc(lowered, 1)
                        dve.wait_ge(lowered, 2 * t + half + 1)
                        dve.tensor_tensor(extra[:, hs], low[:, hs], sink[:, hs], ALU.add).then_inc(sunk, 1)
                        dve.wait_ge(raised, 18 * t + 9 * half + 9)
                        dve.tensor_tensor(sums[:, hs], sums[:, hs], extra[:, hs], ALU.add).then_inc(vec, 1)
                        dve.wait_ge(vec, at + 2)
                        dve.reciprocal(recip[:, hs], sums[:, hs]).then_inc(vec, 1)
                        dve.wait_ge(vec, at + 3)
                        for h in range(8 * half, 8 * half + 8):
                            dve.tensor_scalar(score[:, h, 0:width], score[:, h, 0:width], recip[:, h:h + 1], None, ALU.mult).then_inc(normed, 1)
                        dve.wait_ge(normed, 16 * t + 8 * half + 8)
                        dve.tensor_copy(top[:, hs], recip[:, hs]).then_inc(vec, 1)
                    dve.wait_ge(gate_loaded, 16 * (t + 1))
                    for g in range(KVH):
                        dve.wait_ge(mixed, 4 * t + g + 1)
                        for h in range(2):
                            p = slice(64 * h, 64 * h + 64)
                            src = pv[0:64, g % 2, :].rearrange("p (j h n) -> p j h n", j=2, h=2)[:, :, h, :]
                            out = o[p, 2 * g:2 * g + 2, ds(128 * t, 128)]
                            dve.tensor_tensor(out, src, gate[p, 2 * g:2 * g + 2, :], ALU.mult).then_inc(gated, 1)
                blocks(dve, body)


def sample_attention(nc, a, scr, outp, o):
    ROWS, NEW = 128, NB * NT
    with Tensors(nc, "smp") as m:
        q_half = m.sb("q_half", 128, H, NEW)
        wide = m.sb("wide", 128, 2, NB, 128)
        k_all = m.sb("k_all", 128, NB, 2, WIN)
        k_new, v_new = m.sb("k_new", 128, 2, NEW), m.sb("v_new", 128, 2, NEW)
        v_all, v_rows = m.sb("v_all", 128, NB, 256), m.sb("v_rows", NEW, 256)
        gate = m.sb("gate", 128, DT, NEW)
        bias = m.sb("bias", 128, NB, WIN + NEW)
        score = m.sb("score", 128, NB, WIN + NEW)
        prob_t = m.sb("prob_t", 128, 2, 2, 128)
        sink, ident = m.sb("sink", 128, 1), m.sb("ident", 128, 128)
        top, low, sums, extra, recip = (m.sb(x, 128, NB) for x in ("top", "low", "sums", "extra", "recip"))
        sc, turn = m.ps("sc", 128, 2, 512), m.ps("turn", 128, 2, 512)
        pv = m.ps("pv", 128, 4, 512)
        loaded, zeroed, widened, v_turned, v_kept = (m.sem(x) for x in ("loaded", "zeroed", "widened", "v_turned", "v_kept"))
        scored, biased, vec, raised, p_turned, p_kept, mixed, gated = (m.sem(x) for x in (
            "scored", "biased", "vec", "raised", "p_turned", "p_kept", "mixed", "gated"))
        stored = m.sem("stored")

        with nc.Block() as block:
            @block.sync
            def _(sp):
                q = scr["aq"][TILES, :, :, 0:NEW]
                for half in range(2):
                    for h in range(2):
                        dst = q_half[64 * half:64 * half + 64].rearrange("p (j h) n -> p j h n", h=2)[:, :, h, :]
                        sp.dma_start(dst, q[64 * h:64 * h + 64]).then_inc(loaded, 16)
                for dst, src in ((k_new[:], scr["ak"][TILES, :, :, 0:NEW]), (v_new[:], scr["av"][TILES, :, :, 0:NEW]),
                                 (gate[:], scr["ag"][TILES, :, :, 0:NEW]), (k_all[:], a["k_cache"]), (v_all[:], a["v_cache"]),
                                 (bias[:], a["bias_sample"]), (sink[:], a["sink_sample"]), (ident[:], a["ident"])):
                    sp.dma_start(dst, src).then_inc(loaded, 16)
                sp.wait_ge(loaded, 16 * 12)
                for j in range(2):
                    sp.dma_start(outp["k_sample"][:, :, j, 0:WIN - NT], k_all[:, :, j, NT:WIN]).then_inc(stored, 16)
                    sp.dma_start(outp["k_sample"][:, :, j, WIN - NT:WIN], k_new[:, j, :].rearrange("p (b t) -> p b t", b=NB)).then_inc(stored, 16)
                sp.dma_start(outp["v_sample"][0:WIN - NT], v_all[NT:WIN]).then_inc(stored, 16)
                sp.wait_ge(v_kept, 1)
                for b in range(NB):
                    sp.dma_start(outp["v_sample"][WIN - NT:WIN, b, :], v_rows[NT * b:NT * b + NT, :]).then_inc(stored, 16)
                sp.wait_ge(stored, 16 * (5 + NB))

            @block.gpsimd
            def _(pool):
                pool.memset(wide[:], 0.0).then_inc(zeroed, 1)
                pool.wait_ge(zeroed, 1)
                pool.wait_ge(loaded, 16 * 12)
                for n in range(KVH):
                    p = slice(64 * (n % 2), 64 * (n % 2) + 64)
                    for b in range(NB):
                        pool.tensor_copy(wide[p, n // 2, b, 32 * n:32 * n + 32].rearrange("p (g t) -> p g t", g=G),
                                         q_half[p, G * n:G * n + G, NT * b:NT * b + NT]).then_inc(widened, 1)

            @block.tensor
            def _(pe):
                pe.wait_ge(loaded, 16 * 12)
                for j in range(2):
                    mm = pe.transpose(turn[0:NEW, 0, 128 * j:128 * j + 128], v_new[:, j, :], ident[:])
                mm.then_inc(v_turned, 1)
                pe.wait_ge(widened, KVH * NB)
                for b in range(NB):
                    if b >= 2:
                        pe.wait_ge(biased, b - 1)
                    for j in range(2):
                        pe.matmul(sc[:, b % 2, 0:WIN], wide[:, j, b, :], k_all[:, b, j, :], start=j == 0, stop=j == 1)
                    for j in range(2):
                        mm = pe.matmul(sc[:, b % 2, WIN:WIN + NEW], wide[:, j, b, :], k_new[:, j, :], start=j == 0, stop=j == 1)
                    mm.then_inc(scored, 1)
                pe.wait_ge(v_kept, 1)
                pe.wait_ge(vec, 5)
                for b in range(NB):
                    if b >= 2:
                        pe.wait_ge(p_kept, b - 1)
                    pe.transpose(turn[:, b % 2, 0:128], score[:, b, 0:WIN], ident[:])
                    pe.transpose(turn[0:NEW, b % 2, 128:256], score[:, b, WIN:WIN + NEW], ident[:]).then_inc(p_turned, 1)
                    pe.wait_ge(p_kept, b + 1)
                    for j in range(2):
                        out = pv[:, 2 * j + b // 4, 128 * (b % 4):128 * (b % 4) + 128]
                        pe.matmul(out, v_all[:, b, 128 * j:128 * j + 128], prob_t[:, b % 2, 0, :], start=True, stop=False)
                        mm = pe.matmul(out, v_rows[:, 128 * j:128 * j + 128], prob_t[0:NEW, b % 2, 1, :], start=False, stop=True)
                    mm.then_inc(mixed, 1)

            @block.scalar
            def _(act):
                act.wait_ge(v_turned, 1)
                act.activation(v_rows[:], turn[0:NEW, 0, 0:256], ACT.Copy).then_inc(v_kept, 1)
                act.wait_ge(vec, 2)
                for b in range(NB):
                    act.activation(score[:, b, :], score[:, b, :], ACT.Exp, bias=low[:, b:b + 1], accum_out=sums[:, b:b + 1]).then_inc(raised, 1)
                act.activation(extra[:], low[:], ACT.Exp, bias=sink[:]).then_inc(raised, 1)
                for b in range(NB):
                    act.wait_ge(p_turned, b + 1)
                    if b >= 2:
                        act.wait_ge(mixed, b - 1)
                    act.activation(prob_t[:, b % 2, 0, :], turn[:, b % 2, 0:128], ACT.Copy)
                    act.activation(prob_t[0:NEW, b % 2, 1, :], turn[0:NEW, b % 2, 128:256], ACT.Copy).then_inc(p_kept, 1)

            @block.vector
            def _(dve):
                dve.wait_ge(loaded, 16 * 12)
                for b in range(NB):
                    dve.wait_ge(scored, b + 1)
                    dve.tensor_tensor_reduce(score[:, b, :], sc[:, b % 2, 0:WIN + NEW], bias[:, b, :], SCALE, -1e30,
                                             ALU.add, ALU.max, top[:, b:b + 1]).then_inc(biased, 1)
                dve.wait_ge(biased, NB)
                dve.tensor_scalar(low[:], top[:], sink[:], None, ALU.max).then_inc(vec, 1)
                dve.wait_ge(vec, 1)
                dve.tensor_scalar(low[:], low[:], -1.0, None, ALU.mult).then_inc(vec, 1)
                dve.wait_ge(raised, NB + 1)
                dve.tensor_tensor(sums[:], sums[:], extra[:], ALU.add).then_inc(vec, 1)
                dve.wait_ge(vec, 3)
                dve.reciprocal(recip[:], sums[:]).then_inc(vec, 1)
                dve.wait_ge(vec, 4)
                scale = recip[:, :].rearrange("p (b o) -> p b o", o=1).broadcast_to([128, NB, WIN + NEW])
                dve.tensor_tensor(score[:], score[:], scale, ALU.mult).then_inc(vec, 1)
                dve.wait_ge(mixed, NB)
                for n in range(KVH):
                    for h in range(2):
                        src = pv[64 * (n % 2):64 * (n % 2) + 64, 2 * (n // 2):2 * (n // 2) + 2, :]
                        src = src.rearrange("p c (b r) -> p (c b) r", b=4)[:, :, 32 * n:32 * n + 32].rearrange("p b (i h t) -> p i h b t", i=2, h=2)[:, :, h]
                        for i in range(2):
                            p = slice(64 * h, 64 * h + 64)
                            dve.tensor_tensor(o[p, 2 * n + i, SEQ:N].rearrange("p (b t) -> p b t", b=NB), src[:, i],
                                              gate[p, 2 * n + i, :].rearrange("p (b t) -> p b t", b=NB), ALU.mult).then_inc(gated, 1)


_INS = {
    "xpad": (128, DT, XPAD), "mu": (128, 6, DT), "w0": (128, DT), "a0": (128, DT), "lora1": (128, 2, DT, 64),
    "lora2": (DT, 64, 2, 128), "w_in": (4, DT, 128, DT, 128), "k_k": (128, DT), "k_a": (128, DT), "r_k": (128, DT),
    "gn_g": (128, DT, 64), "gn_b": (128, DT, 64), "s_sample": (128, DT, NB, 64), "w_out": (DT, 128, DT, 128),
    "ln_g": (2, 128, DT), "ln_b": (2, 128, DT), "w_att": (20, 128, DT, 128), "w_att_out": (DT, 128, DT, 128),
    "sink": (128, H), "sink_sample": (128, 1), "k_cache": (128, NB, 2, WIN), "v_cache": (128, NB, 256),
}
_OUTS = {
    "y": (128, DT, N), "wkv_prompt": (128, DT, 64), "wkv_sample": (128, DT, NB, 64), "shift": (NB + 1, D),
    "k_prompt": (128, 2, 128), "v_prompt": (128, 2, 128), "k_sample": (128, NB, 2, WIN), "v_sample": (WIN, NB, 256),
}


def constants():
    r = np.arange(128)
    head, tok = r // 64, r % 64
    same = head[:, None] == head[None, :]
    before, upto = tok[:, None] < tok[None, :], tok[:, None] <= tok[None, :]
    seq = tok[:, None] // NT == tok[None, :] // NT
    gram = np.stack([np.stack([-1.0 * (same & before & part), -1.0 * (same & upto & part),
                               1.0 * (same & before & part), 1.0 * (same & upto & part)], 1) for part in (np.ones_like(seq), seq)], 1)
    c = np.arange(64)
    small = -1.0 * ((tok[:, None] // 8 == c // 8) & (tok[:, None] < c))
    levels = np.stack([(r[:, None] // (2 * b) == r // (2 * b)) & (r[:, None] // b % 2 == 0) & (r // b % 2 == 1) for b in (8, 16, 32)], 1)
    slopes = 2.0 ** (-8.0 * np.arange(1, H + 1) / H)
    dead = -1e31
    q, k = r[:, None], r[None, :]
    far, own = q - k + 128, q - k
    tables = [np.where(far < WIN, far, np.nan), np.where(own >= 0, own, np.nan)]
    bias = np.stack([np.stack([np.where(np.isnan(t), dead, -s * np.nan_to_num(t) / SCALE) for t in (tables[0], tables[1], tables[0])], 1)
                     for s in slopes], 1)
    row_t, row_head = r % NT, r // NT
    key = np.arange(WIN)
    cached = row_t[:, None] + WIN - key
    cached = np.where(cached < WIN, cached, np.nan)[:, None, :].repeat(NB, 1)
    c = np.arange(NB * NT)
    new = (row_t[:, None] - c % NT)[:, None, :].repeat(NB, 1).astype(float)
    new = np.where((c // NT == np.arange(NB)[:, None])[None] & (new >= 0), new, np.nan)
    dist = np.concatenate([cached, new], 2)
    bias_s = np.where(np.isnan(dist), dead, -slopes[row_head][:, None, None] * np.nan_to_num(dist) / SCALE)
    reset = np.ones(N)
    reset[0:SEQ:C] = 0
    reset[SEQ::NT] = 0
    return {k: np.ascontiguousarray(v, dtype=np.float32) for k, v in {
        "reset": np.broadcast_to(reset, (128, N)), "headsum": same, "headpick": head[:, None] == np.arange(2),
        "gram_mask": gram, "small_mask": small, "block_mask": r[:, None] // 8 == np.arange(16), "row_pick": r[:, None] % 8 == np.arange(8),
        "unit8": r[:, None] % 8 == np.arange(8), "level_mask": levels, "block_ones": r[:, None] // 8 == r // 8,
        "ident": np.eye(128), "seq_mask": tok[:, None] // NT == np.arange(NB), "mean_ones": np.full((128, 128), 1.0 / D),
        "bias": bias, "bias_sample": bias_s,
    }.items()}


def program(nc, a, outp):
    scr = {}
    for name, tiles in (("v", DT), ("g", DT), ("kt", DT), ("rt", DT), ("bh", DT), ("kh", DT), ("y", DT),
                        ("aq", DT), ("ak", 2), ("av", 2), ("ag", DT)):
        scr[name] = nc.dram_tensor(f"scr_{name}", (TILES + 1, 128, tiles, 128), F32, kind="Internal").ap()

    with Tensors(nc, "shift") as m:
        copied = m.sem("copied")
        with nc.Block() as block:
            @block.sync
            def _(sp):
                sp.dma_start(outp["shift"], a["x_last"]).then_inc(copied, 16)
                sp.wait_ge(copied, 16)

    with Tensors(nc, "rwkv") as m:
        keep = {"bonus": m.sb("bonus", 128, 2 * TILES + 1, DT), "ends": m.sb("ends", 128, DT, SEQ // C),
                "ends_sample": m.sb("ends_sample", 128, DT, NB)}
        mixed_projections(nc, a, scr, keep)
        delta_rule(nc, a, scr, keep, outp)

    with Tensors(nc, "both") as m:
        x = m.sb("x", 128, DT, N)
        with Tensors(nc, "one") as m1:
            rhs, res = m1.sb("rhs", 128, DT, N), m1.sb("res", 128, DT, N)

            def load_y(sp, sem):
                for t in range(TILES + 1):
                    n = min(128, N - 128 * t)
                    sp.dma_start(rhs[:, :, 128 * t:128 * t + n], scr["y"][t, :, :, 0:n]).then_inc(sem, 16)
            load_y.count = TILES + 1

            def load_x(sp, sem):
                sp.dma_start(res[:, :, 0:SEQ], a["xpad"][:, :, 1:1 + SEQ]).then_inc(sem, 16)
                for d in range(DT):
                    pad = a["xpad"][:, d, 1 + SEQ:].rearrange("p (b t) -> p b t", b=NB)
                    sp.dma_start(res[:, d, SEQ:N].rearrange("p (b t) -> p b t", b=NB), pad[:, :, 1:]).then_inc(sem, 16)
            load_x.count = DT + 1
            project_and_norm(nc, a, "out1", a["w_out"], a["ln_g"][0], a["ln_b"][0], rhs, load_y, res, load_x, x, None)
        attention_projections(nc, a, scr, x)
        with Tensors(nc, "two") as m2:
            o = m2.sb("o", 128, DT, N)
            attention(nc, a, scr, outp, o)
            sample_attention(nc, a, scr, outp, o)

            def nothing(sp, sem):
                return None
            nothing.count = 0

            def store_y(sp, sem):
                sp.dma_start(outp["y"], x[:]).then_inc(sem, 16)
                sp.wait_ge(sem, 16)
            project_and_norm(nc, a, "out2", a["w_att_out"], a["ln_g"][1], a["ln_b"][1], o, nothing, x, nothing, x, store_y)


def laid_out(i):
    i = {k: np.asarray(v) for k, v in i.items()}

    def channels(v):
        return np.moveaxis(v.reshape(*v.shape[:-1], DT, 128), -1, 0)

    def weight_tiles(w):
        return w.reshape(DT, 128, -1, 128).transpose(2, 1, 0, 3)

    perm = np.concatenate([np.arange(64) + 64 * (4 * f + 2 * p + h) for f in range(4) for h in range(2) for p in range(2)])
    token_rows = np.concatenate([np.zeros((1, D), np.float32), i["x_prompt"][0]] + [
        r for b in range(NB) for r in (i["state_shift"][0, b][None], i["x_sample"][b])])
    w = i["rwkv_w_in"][0]
    pairs = lambda v: np.repeat(v.reshape(DT, 2, 1, 64).transpose(1, 2, 0, 3), 64, 1).reshape(128, DT, 64)
    arrays = {
        "xpad": channels(token_rows).transpose(0, 2, 1), "mu": channels(i["rwkv_mu"][0]), "w0": channels(i["rwkv_w0"][0]),
        "a0": channels(i["rwkv_a0"][0]),
        "lora1": np.stack([i["rwkv_w1"][0], i["rwkv_a1"][0]]).reshape(2, DT, 128, 64).transpose(2, 0, 1, 3),
        "lora2": np.stack([i["rwkv_w2"][0], i["rwkv_a2"][0]]).reshape(2, 64, DT, 128).transpose(2, 1, 0, 3),
        "w_in": np.stack([weight_tiles(x) for x in (w[1], w[0], w[2], w[3][:, perm])]),
        "k_k": channels(i["rwkv_k_k"][0]), "k_a": channels(i["rwkv_k_a"][0]), "r_k": channels(i["rwkv_r_k"][0].reshape(D)),
        "gn_g": pairs(i["rwkv_gn_g"][0]), "gn_b": pairs(i["rwkv_gn_b"][0]),
        "s_sample": i["state_wkv"][0].reshape(NB, DT, 2, 64, 64).transpose(2, 4, 1, 0, 3).reshape(128, DT, NB, 64),
        "w_out": weight_tiles(i["rwkv_w_out"][0][perm]), "ln_g": np.stack([channels(x) for x in i["ln_g"]]),
        "ln_b": np.stack([channels(x) for x in i["ln_b"]]), "w_att": weight_tiles(i["att_w_in"][0]),
        "w_att_out": weight_tiles(i["att_w_out"][0]), "sink": np.broadcast_to(i["att_sinks"][0], (128, H)),
        "sink_sample": np.repeat(i["att_sinks"][0], NT).reshape(128, 1),
        "k_cache": i["cache_win_k"][0].reshape(NB, WIN, 2, 128).transpose(3, 0, 2, 1),
        "v_cache": i["cache_win_v"][0].reshape(NB, WIN, 256).transpose(1, 0, 2),
    }
    arrays = {k: np.ascontiguousarray(v) for k, v in {**arrays, **constants()}.items()}
    arrays["x_last"] = np.ascontiguousarray(np.concatenate([i["x_prompt"][:, -1], i["x_sample"][:, -1]]))
    return arrays


def kernel(**inputs):
    import concourse.bacc as _bacc
    from concourse.bass_utils import run_bass_kernel_spmd as _run

    arrays = laid_out(inputs)
    nc = _bacc.Bacc("TRN2", target_bir_lowering=False, num_devices=1)
    a = {k: nc.dram_tensor(f"in_{k}", v.shape, F32, kind="ExternalInput").ap() for k, v in arrays.items()}
    outp = {k: nc.dram_tensor(f"out_{k}", shape, F32, kind="ExternalOutput").ap() for k, shape in _OUTS.items()}
    program(nc, a, outp)
    r = _run(nc, [{f"in_{k}": v for k, v in arrays.items()}], core_ids=[0]).results[0]
    got = {k: r[f"out_{k}"] for k in _OUTS}
    y = got["y"].transpose(2, 1, 0).reshape(N, D)
    window = lambda v: v.transpose(2, 1, 0).reshape(1, 1, WIN, KVH, HD)
    return (y[None, :SEQ], y[SEQ:].reshape(NB, NT, D),
            got["wkv_prompt"].reshape(2, 64, DT, 64).transpose(2, 0, 3, 1).reshape(1, 1, H, HD, HD),
            got["shift"][None, :1], window(got["k_prompt"]), window(got["v_prompt"]),
            got["wkv_sample"].reshape(2, 64, DT, NB, 64).transpose(3, 2, 0, 4, 1).reshape(1, NB, H, HD, HD),
            got["shift"][None, 1:],
            got["k_sample"].transpose(1, 3, 2, 0).reshape(1, NB, WIN, KVH, HD),
            got["v_sample"].transpose(1, 0, 2).reshape(1, NB, WIN, KVH, HD))
```

```python
from contextlib import ExitStack

import numpy as np

import concourse.bass as bass
from concourse import mybir

F32 = mybir.dt.float32
F32R = mybir.dt.float32r
ALU = mybir.AluOpType
ACT = mybir.ActivationFunctionType
AX = mybir.AxisListType.X

D = 1024
DT = D // 128
SEQ, NB, NT = 1024, 8, 8
N = SEQ + NB * NT
TILES = SEQ // 128
H, HD = 16, 64
C = 64
KVH, G = 4, 4
WIN = 128
DECAY = -float(np.exp(-0.5))
ALPHA = 4.0 ** 0.25
SCALE = HD ** -0.5
LN_EPS, GN_EPS = 1e-5, 64e-5
PARTS = ((0, 364), (364, 364), (728, 360))
XPAD = 1 + SEQ + NB * (NT + 1)


def ds(i, n):
    return bass.ds(i, n)


class Tensors:

    def __init__(self, nc, stage):
        self.nc, self.stage, self.stack, self.sems = nc, stage, ExitStack(), []

    def __enter__(self):
        return self

    def __exit__(self, *e):
        if self.sems:
            self.nc.clear_and_free_semaphores(self.sems)
            self.nc.all_engine_barrier()
        self.stack.close()

    def sb(self, name, *shape, dtype=F32):
        return self.stack.enter_context(self.nc.sbuf_tensor(f"{self.stage}_{name}", list(shape), dtype))

    def ps(self, name, *shape):
        return self.stack.enter_context(self.nc.psum_tensor(f"{self.stage}_{name}", list(shape), F32))

    def sem(self, name):
        self.sems.append(self.nc.alloc_semaphore(f"{self.stage}_{name}"))
        return self.sems[-1]


def held(eng, sem, value, turns):
    eng.wait_ge(sem, value)
    eng.sem_inc(turns, 1)


def both(ap):
    return ap[:, 0:SEQ], ap[:, SEQ:N].rearrange("p (b t) -> p b t", b=NB)


def mixed_projections(nc, a, scr, keep):
    with Tensors(nc, "mix") as m:
        xpad, xs = m.sb("xpad", 128, DT, XPAD), m.sb("xs", 128, 2, DT, N)
        mu, w0, a0 = m.sb("mu", 128, 6, DT), m.sb("w0", 128, DT), m.sb("a0", 128, DT)
        k_k, k_a, r_k = m.sb("k_k", 128, DT), m.sb("k_a", 128, DT), m.sb("r_k", 128, DT)
        headsum, headpick = m.sb("headsum", 128, 128), m.sb("headpick", 128, 2)
        lora1, lora2 = m.sb("lora1", 128, 2, DT, 64), m.sb("lora2", 64, 2, 2, 128)
        hidden, reset = m.sb("hidden", 64, 2, N), m.sb("reset", 128, N)
        wt, out = m.sb("wt", 128, 2, DT, 128), m.sb("out", 128, 2, N)
        sigma, step_size = m.sb("sigma", 128, N), m.sb("step_size", 128, 2, N)
        decay = m.sb("decay", 128, 3, N)
        square, norm, bonus = m.sb("square", 128, N), m.sb("norm", 128, N), m.sb("bonus", 128, N)
        outs = m.sb("outs", 128, 4, N)
        dots = m.sb("dots", 128, TILES + 1, H)
        acc = m.ps("acc", 128, 2, 3, 512)
        side = m.ps("side", 128, 2, 512)
        x_loaded = [m.sem(f"x_loaded{i}") for i in range(DT)]
        small_loaded = m.sem("small_loaded")
        w_loaded = [m.sem(f"w_loaded{i}") for i in range(2)]
        l_loaded = [m.sem(f"l_loaded{i}") for i in range(2)]
        stored = [m.sem(f"stored{i}") for i in range(2)]
        shifted, mix_made, hid_acc, hid_made = (m.sem(x) for x in ("shifted", "mix_made", "hid_acc", "hid_made"))
        acc_made, evacuated, lora_made, lora_kept = (m.sem(x) for x in ("acc_made", "evacuated", "lora_made", "lora_kept"))
        summed_up, decayed, ones_set, keyed, squared = (m.sem(x) for x in ("summed_up", "decayed", "ones_set", "keyed", "squared"))
        summed, clamped, rooted, vec, bonused = (m.sem(x) for x in ("summed", "clamped", "rooted", "vec", "bonused"))
        dotted, ends_kept, dots_kept, ops_stored = (m.sem(x) for x in ("dotted", "ends_kept", "dots_kept", "ops_stored"))
        act_turns, sp_turns, pool_turns = m.sem("act_turns"), m.sem("sp_turns"), m.sem("pool_turns")
        VEC = 9
        MU = (4, 5, 1, 0, 2, 3)
        smalls = (("mu", mu), ("lora1", lora1), ("w0", w0), ("a0", a0), ("reset", reset), ("k_k", k_k), ("k_a", k_a), ("r_k", r_k),
                  ("headsum", headsum), ("headpick", headpick))

        def turns(eng, body, last=False):
            body(0, 0, True)
            body(1, 1, False)
            with eng.Fori(1, DT // 2 - (1 if last else 0)) as i:
                body(2 * i, 0, False)
                body(2 * i + 1, 1, False)
            if last:
                body(DT - 2, 0, False)
                body(DT - 1, 1, False)

        def pairs(eng, p, body):
            if p == 0:
                body(0, True)
            with eng.Fori(1 if p == 0 else 0, DT // 2) as i:
                body(i, False)

        def known(j):
            return isinstance(j, int)

        with nc.Block() as block:
            @block.sync
            def _(sp):
                for name, dst in smalls[0:2]:
                    sp.dma_start(dst[:], a[name]).then_inc(small_loaded, 16)
                for d in range(DT):
                    sp.dma_start(xpad[:, d, :], a["xpad"][:, d, :]).then_inc(x_loaded[d], 16)
                for name, dst in smalls[2:]:
                    sp.dma_start(dst[:], a[name]).then_inc(small_loaded, 16)

                def store_ops(j):
                    held(sp, vec, VEC * (j + 1), sp_turns)
                    for k, name in enumerate(("kt", "rt", "bh", "kh")):
                        store_tiles(sp, scr[name], j, outs[:, k], ops_stored)

                def body(j, s, first):
                    if not (known(j) and j < 2):
                        held(sp, lora_made, 6 * (j - 1), sp_turns)
                    sp.dma_start(lora2[:, s], a["lora2"][j]).then_inc(l_loaded[s], 16)
                    for k in range(2):
                        if not first:
                            held(sp, acc_made, 3 * (2 * j + k - 1), sp_turns)
                        sp.dma_start(wt[:, k], a["w_in"][k][j]).then_inc(w_loaded[k], 16)
                    if not first:
                        store_ops(j - 1)
                turns(sp, body)
                for p in range(2):
                    def job(i, first, p=p):
                        for s in range(2):
                            sp.wait_ge(acc_made, 3 * (16 + 8 * p + 2 * i + s - 1))
                            sp.dma_start(wt[:, s], a["w_in"][2 + p][2 * i + s]).then_inc(w_loaded[s], 16)
                        if first:
                            store_ops(DT - 1)
                    pairs(sp, p, job)
                sp.wait_ge(ops_stored, 128 * DT)

            @block.gpsimd
            def _(pool):
                def body(j, s, first):
                    held(pool, decayed, 3 * j + 1, pool_turns)
                    prompt, sample = both(decay[:, 1])
                    pool.memset(prompt.rearrange("p (c t) -> p c t", t=C)[:, :, 0:1], 1.0).then_inc(ones_set, 1)
                    pool.memset(sample[:, :, 0:1], 1.0).then_inc(ones_set, 1)
                turns(pool, body)

            @block.tensor
            def _(pe):
                pe.wait_ge(small_loaded, 16 * len(smalls))
                for p in range(2):
                    pe.wait_ge(mix_made, 2 * DT * (p + 1))
                    for k, (n0, n) in enumerate(PARTS):
                        turn = 3 * p + k
                        if turn >= 2:
                            pe.wait_ge(hid_made, turn - 1)
                        for d in range(DT):
                            mm = pe.matmul(side[0:64, turn % 2, 0:n], lora1[:, p, d, :], xs[:, p, d, n0:n0 + n],
                                           start=d == 0, stop=d == DT - 1)
                        mm.then_inc(hid_acc, 1)
                pe.wait_ge(hid_made, 6)

                def part(j_job, s, k, wait):
                    n0, n = PARTS[k]
                    if wait:
                        pe.wait_ge(evacuated, 3 * (j_job - 2) + k + 1)
                    for d in range(DT):
                        mm = pe.matmul(acc[:, s, k, 0:n], wt[:, s, d, :], xs[:, s, d, n0:n0 + n], start=d == 0, stop=d == DT - 1)
                    mm.then_inc(acc_made, 1)

                def dot_products(j):
                    pe.wait_ge(bonused, j + 1)
                    for t in range(TILES + 1):
                        n = min(128, N - 128 * t)
                        mm = pe.matmul(side[0:n, 1, 2 * t:2 * t + 2], bonus[:, 128 * t:128 * t + n], headpick[:], start=True, stop=True)
                    mm.then_inc(dotted, 1)

                def body(j, s, first):
                    pe.wait_ge(l_loaded[s], 8 * (j - s) + 16)
                    if not first:
                        pe.wait_ge(clamped, 3 * j)
                        if not (known(j) and j == 1):
                            pe.wait_ge(dots_kept, j - 1)
                    for l in range(2):
                        for k, (n0, n) in enumerate(PARTS):
                            turn = 3 * l + k
                            if turn >= 2:
                                pe.wait_ge(lora_kept, 6 * j + turn - 1)
                            pe.matmul(side[:, turn % 2, 0:n], lora2[:, s, l, :], hidden[:, l, n0:n0 + n], start=True, stop=True).then_inc(lora_made, 1)
                    if first:
                        pe.wait_ge(mix_made, 2 * DT * 3)
                    pe.wait_ge(w_loaded[0], 16 * (j + 1))
                    part(2 * j, 0, 0, not first)
                    pe.wait_ge(lora_kept, 6 * j + 6)
                    if not first:
                        dot_products(j - 1)
                    part(2 * j, 0, 1, not first)
                    part(2 * j, 0, 2, not first)
                    if first:
                        pe.wait_ge(mix_made, 2 * DT * 4)
                    pe.wait_ge(w_loaded[1], 16 * (j + 1))
                    part(2 * j + 1, 1, 0, not first)
                    pe.wait_ge(squared, j + 1)
                    for k, (n0, n) in enumerate(PARTS):
                        if k == 1 and not first:
                            pe.wait_ge(dots_kept, j)
                        if k == 2:
                            pe.wait_ge(clamped, 3 * j + 1)
                        pe.matmul(side[:, k % 2, 0:n], headsum[:], square[:, n0:n0 + n], start=True, stop=True).then_inc(summed, 1)
                    part(2 * j + 1, 1, 1, not first)
                    part(2 * j + 1, 1, 2, not first)
                turns(pe, body)
                for p in range(2):
                    pe.wait_ge(mix_made, 2 * DT * (5 + p))

                    def job(i, first, p=p):
                        for s in range(2):
                            pe.wait_ge(w_loaded[s], 16 * (DT + 4 * p + i + 1))
                            for k in range(3):
                                part_of(p, i, s, k)
                                if first and s == 0 and k == 1:
                                    pe.wait_ge(clamped, 3 * DT)
                                    dot_products(DT - 1)

                    def part_of(p, i, s, k):
                        n0, n = PARTS[k]
                        pe.wait_ge(evacuated, 3 * (16 + 8 * p + 2 * i + s - 2) + k + 1)
                        for d in range(DT):
                            mm = pe.matmul(acc[:, s, k, 0:n], wt[:, s, d, :], xs[:, p, d, n0:n0 + n], start=d == 0, stop=d == DT - 1)
                        mm.then_inc(acc_made, 1)
                    pairs(pe, p, job)

            @block.scalar
            def _(act):
                act.wait_ge(small_loaded, 16 * len(smalls))
                for p in range(2):
                    for k, (n0, n) in enumerate(PARTS):
                        turn = 3 * p + k
                        act.wait_ge(hid_acc, turn + 1)
                        act.activation(hidden[:, p, n0:n0 + n], side[0:64, turn % 2, 0:n], ACT.Tanh if p == 0 else ACT.Copy).then_inc(hid_made, 1)

                def body(j, s, first):
                    if not first:
                        act.wait_ge(summed_up, j)
                    if not (known(j) and j < 2):
                        act.wait_ge(vec, VEC * (j - 1))
                    for l in range(2):
                        for k, (n0, n) in enumerate(PARTS):
                            held(act, lora_made, 6 * j + 3 * l + k + 1, act_turns)
                            dst = (sigma[:, n0:n0 + n], step_size[:, s, n0:n0 + n])[l]
                            act.activation(dst, side[:, (3 * l + k) % 2, 0:n], ACT.Sigmoid, bias=(w0, a0)[l][:, ds(j, 1)]).then_inc(lora_kept, 1)
                    if not first:
                        act.wait_ge(vec, VEC * j)
                        act.wait_ge(bonused, j)
                        act.wait_ge(ones_set, 2 * j)
                    act.wait_ge(summed_up, j + 1)
                    act.activation(decay[:, 1, 1:N], decay[:, 0, 0:N - 1], ACT.Exp, scale=DECAY).then_inc(decayed, 1)
                    act.activation(decay[:, 2], decay[:, 0], ACT.Exp, scale=-DECAY).then_inc(decayed, 1)
                    act.wait_ge(decayed, 3 * j + 2)
                    act.activation(decay[:, 0], decay[:, 0], ACT.Exp, scale=DECAY).then_inc(decayed, 1)
                    for k, (n0, n) in enumerate(PARTS):
                        act.wait_ge(acc_made, 6 * j + k + 1)
                        act.activation(out[:, 0, n0:n0 + n], acc[:, 0, k, 0:n], ACT.Copy).then_inc(evacuated, 1)
                    if not first:
                        act.wait_ge(ops_stored, 128 * j)
                        act.wait_ge(summed, 3 * j)
                    held(act, evacuated, 6 * j + 3, act_turns)
                    act.activation(square[:], out[:, 0], ACT.Square, scale=k_k[:, ds(j, 1)]).then_inc(squared, 1)
                    act.activation(outs[:, 0], out[:, 0], ACT.Copy, scale=k_k[:, ds(j, 1)]).then_inc(keyed, 1)
                    act.wait_ge(clamped, 3 * j + 3)
                    act.activation(norm[:], norm[:], ACT.Sqrt).then_inc(rooted, 1)
                    for k, (n0, n) in enumerate(PARTS):
                        act.wait_ge(acc_made, 6 * j + 3 + k + 1)
                        act.activation(out[:, 1, n0:n0 + n], acc[:, 1, k, 0:n], ACT.Copy).then_inc(evacuated, 1)
                turns(act, body)
                act.wait_ge(vec, VEC * DT)
                act.wait_ge(bonused, DT)
                act.wait_ge(keyed, DT)
                for p, name in enumerate(("v", "g")):
                    def job(i, first, p=p, name=name):
                        for s in range(2):
                            n = 16 + 8 * p + 2 * i + s
                            if not first:
                                act.wait_ge(stored[s], 32 * (4 * p + i))
                            for k, (n0, width) in enumerate(PARTS):
                                act.wait_ge(acc_made, 3 * n + k + 1)
                                act.activation(out[:, s, n0:n0 + width], acc[:, s, k, 0:width], ACT.Silu if name == "g" else ACT.Copy).then_inc(evacuated, 1)
                            act.wait_ge(evacuated, 3 * n + 3)
                            store_tiles(act, scr[name], 2 * i + s, out[:, s], stored[s])
                    pairs(act, p, job)
                for s in range(2):
                    act.wait_ge(stored[s], 32 * DT)

            @block.vector
            def _(dve):
                dve.wait_ge(small_loaded, 32)

                def mix(p):
                    for d in range(DT):
                        if p == 0:
                            dve.wait_ge(x_loaded[d], 16)
                        pad = xpad[:, d, 1 + SEQ:].rearrange("p (b t) -> p b t", b=NB)
                        o, x = both(xs[:, p % 2, d, :]), (xpad[:, d, 1:1 + SEQ], pad[:, :, 1:1 + NT])
                        scale = mu[:, MU[p], d:d + 1]
                        dve.tensor_tensor(o[0], xpad[:, d, 0:SEQ], x[0], ALU.subtract).then_inc(shifted, 1)
                        dve.tensor_tensor(o[1], pad[:, :, 0:NT], x[1], ALU.subtract).then_inc(shifted, 1)
                        for k in range(2):
                            dve.wait_ge(shifted, 2 * DT * p + 2 * d + k + 1)
                            dve.scalar_tensor_tensor(o[k], o[k], scale, x[k], ALU.mult, ALU.add).then_inc(mix_made, 1)

                mix(0)
                mix(1)
                dve.wait_ge(hid_acc, 3)
                mix(2)
                dve.wait_ge(hid_acc, 6)
                mix(3)
                dve.wait_ge(small_loaded, 16 * len(smalls))

                def keep_dots(j):
                    dve.wait_ge(dotted, j + 1)
                    full = dots[:, 0:TILES, ds(2 * j, 2)]
                    dve.tensor_copy(full, side[:, 1, 0:2 * TILES].rearrange("p (t h) -> p t h", h=2))
                    dve.tensor_copy(dots[0:NB * NT, TILES:TILES + 1, ds(2 * j, 2)],
                                    side[0:NB * NT, 1, 2 * TILES:2 * TILES + 2].rearrange("p (t h) -> p t h", h=2)).then_inc(dots_kept, 1)

                def body(j, s, first):
                    k_in, r_in, a_in = out[:, 0], out[:, 1], step_size[:, s]
                    p_now, p_before, p_inverse = (decay[:, k] for k in range(3))
                    kt, rt, bh, kh = (outs[:, k] for k in range(4))
                    step = VEC * j
                    dve.wait_ge(lora_kept, 6 * j + 3)
                    if not first:
                        dve.wait_ge(vec, step)
                        dve.wait_ge(ends_kept, 2 * j)
                    dve.tensor_tensor_scan(p_now, reset[:], sigma[:], 0.0, ALU.mult, ALU.add).then_inc(summed_up, 1)
                    if not first:
                        keep_dots(j - 1)
                        dve.wait_ge(ops_stored, 128 * j)
                    if known(j) and j == DT - 1:
                        dve.wait_ge(acc_made, 3 * (2 * DT - 1))
                        mix(4)
                    dve.wait_ge(lora_kept, 6 * j + 6)
                    dve.tensor_scalar(kh, a_in, -1.0, k_a[:, ds(j, 1)], ALU.add, ALU.mult).then_inc(vec, 1)
                    dve.wait_ge(evacuated, 6 * j + 3)
                    dve.wait_ge(vec, step + 1)
                    dve.scalar_tensor_tensor(kh, kh, 1.0, k_in, ALU.add, ALU.mult).then_inc(vec, 1)
                    for k, (n0, n) in enumerate(PARTS):
                        dve.wait_ge(summed, 3 * j + k + 1)
                        dve.tensor_scalar(norm[:, n0:n0 + n], side[:, k % 2, 0:n], 1e-24, None, ALU.max).then_inc(clamped, 1)
                    dve.wait_ge(rooted, j + 1)
                    dve.reciprocal(norm[:], norm[:]).then_inc(vec, 1)
                    dve.wait_ge(keyed, j + 1)
                    dve.wait_ge(vec, step + 3)
                    dve.tensor_tensor(kt, kt, norm[:], ALU.mult).then_inc(vec, 1)
                    dve.wait_ge(vec, step + 4)
                    dve.tensor_tensor(bh, kt, a_in, ALU.mult).then_inc(vec, 1)
                    dve.wait_ge(ones_set, 2 * j + 2)
                    dve.wait_ge(vec, step + 5)
                    dve.tensor_tensor(kt, kt, p_before, ALU.mult).then_inc(vec, 1)
                    dve.wait_ge(decayed, 3 * j + 3)
                    dve.tensor_tensor(bh, bh, p_inverse, ALU.mult).then_inc(vec, 1)
                    prompt, sample = both(p_now)
                    dve.tensor_copy(keep["ends"][:, ds(j, 1), :],
                                    prompt.rearrange("p (o c t) -> p o c t", o=1, t=C)[:, :, :, C - 1]).then_inc(ends_kept, 1)
                    dve.tensor_copy(keep["ends_sample"][:, ds(j, 1), :],
                                    sample.rearrange("p (o b) t -> p o b t", o=1)[:, :, :, NT - 1]).then_inc(ends_kept, 1)
                    dve.wait_ge(evacuated, 6 * j + 6)
                    dve.scalar_tensor_tensor(bonus[:], r_in, r_k[:, ds(j, 1)], kh, ALU.mult, ALU.mult).then_inc(bonused, 1)
                    dve.tensor_tensor(rt, r_in, p_now, ALU.mult).then_inc(vec, 1)
                    dve.wait_ge(bonused, j + 1)
                    dve.tensor_tensor(kh, kh, p_inverse, ALU.mult).then_inc(vec, 1)
                turns(dve, body, last=True)
                dve.wait_ge(acc_made, 6 * DT)
                mix(5)
                keep_dots(DT - 1)
                dve.wait_ge(dots_kept, DT)
                chunks = keep["bonus"][:, 0:2 * TILES, :].rearrange("p (t q) j -> p t q j", q=2)
                for q in range(2):
                    for h in range(2):
                        src = dots[64 * q:64 * q + 64, 0:TILES, :].rearrange("p t (j h) -> p t j h", h=2)[:, :, :, h]
                        dve.tensor_copy(chunks[64 * h:64 * h + 64, :, q, :], src).then_inc(dots_kept, 1)
                for h in range(2):
                    src = dots[0:64, TILES:TILES + 1, :].rearrange("p t (j h) -> p t j h", h=2)[:, :, :, h]
                    dve.tensor_copy(keep["bonus"][64 * h:64 * h + 64, 2 * TILES:2 * TILES + 1, :], src).then_inc(dots_kept, 1)


def store_tiles(eng, dram, j, row, stored):
    tiles = dram.shape[2]
    eng.dma_start(dram[0:TILES].rearrange("t p j n -> p t j n")[:, :, j, :],
                  row[:, 0:SEQ].rearrange("p (t n) -> p t n", t=TILES)).then_inc(stored, 16)
    eng.dma_start(dram[TILES, :, j, 0:NB * NT], row[:, SEQ:N]).then_inc(stored, 16)


def delta_rule(nc, a, scr, keep, outp):
    with Tensors(nc, "delta") as m:
        ops, v_in, gate = m.sb("ops", 128, 4, DT, 128), m.sb("v_in", 128, DT, 128), m.sb("gate", 128, DT, 128)
        wide = m.sb("wide", 128, 4, 16, 128)
        grams = m.sb("grams", 128, 16, 4, 128)
        below = m.sb("below", 128, 8, 128)
        inv_t, inv = m.sb("inv_t", 128, 16, 128), m.sb("inv", 128, 8, 128)
        lm = m.sb("lm", 128, 2, 512)
        rows = m.sb("rows", 128, 2, 16, 128)
        v_rows = m.sb("v_rows", 128, 16, 64)
        small, pick = m.sb("small", 128, 8, 64), m.sb("pick", 128, 8, 64)
        coeff, solved, term = m.sb("coeff", 128, 8, 8), m.sb("solved", 128, 8, 8), m.sb("term", 128, 8, 8)
        state = m.sb("state", 128, 2, DT, 64)
        z, u = m.sb("z", 128, 2, 256), m.sb("u", 128, 2, 256)
        y, y2, y3, bonus = (m.sb(x, 128, DT, 64) for x in ("y", "y2", "y3", "bonus"))
        stat = m.sb("stat", 128, 3, DT)
        gated = m.sb("gated", 128, DT, 128)
        gram_mask = m.sb("gram_mask", 128, 2, 4, 128)
        small_mask, block_mask = m.sb("small_mask", 128, 64), m.sb("block_mask", 128, 16)
        row_pick, unit8, level_mask = m.sb("row_pick", 128, 8), m.sb("unit8", 128, 8), m.sb("level_mask", 128, 3, 128)
        block_ones, ident = m.sb("block_ones", 128, 128), m.sb("ident", 128, 128)
        gn_g, gn_b = m.sb("gn_g", 128, DT, 64), m.sb("gn_b", 128, DT, 64)
        ga, gb = m.ps("ga", 128, 512), m.ps("gb", 128, 512)
        wb = m.ps("wb", 128, 2, 512)
        mb = m.ps("mb", 128, 4, 512)
        gbank = (ga, gb)
        consts_loaded = m.sem("consts_loaded")
        ops_loaded, v_loaded, gate_loaded = m.sem("ops_loaded"), m.sem("v_loaded"), m.sem("gate_loaded")
        zeroed, q_widened, k_widened = m.sem("zeroed"), m.sem("q_widened"), m.sem("k_widened")
        v_turned, v_kept = m.sem("v_turned"), m.sem("v_kept")
        rows_turned, rows_kept = m.sem("rows_turned"), m.sem("rows_kept")
        gram_made, gram_kept, gram_small = m.sem("gram_made"), m.sem("gram_kept"), m.sem("gram_small")
        coeff_made, picked, spread, solving, solved_wide = (m.sem(x) for x in ("coeff_made", "picked", "spread", "solving", "solved_wide"))
        inv_turned, inv_kept = m.sem("inv_turned"), m.sem("inv_kept")
        below_made, lm_made, lm_kept, grown, grown_kept = (m.sem(x) for x in ("below_made", "lm_made", "lm_kept", "grown", "grown_kept"))
        z_made, z_kept, u_made, u_kept, s_made, s_kept = (m.sem(x) for x in ("z_made", "z_kept", "u_made", "u_kept", "s_made", "s_kept"))
        y_made, normed, y_squared, y_rooted, y_turned, y_gated = (m.sem(x) for x in ("y_made", "normed", "y_squared", "y_rooted", "y_turned", "y_gated"))
        y_stored = m.sem("y_stored")
        pe_turns, pool_turns, act_turns = m.sem("pe_turns"), m.sem("pool_turns"), m.sem("act_turns")
        NORM = 10
        ROW_BANK = (1, 3, 0, 2)
        CHUNKS = 2 * TILES

        def steps(eng, body):
            for q in range(2):
                body(0, q, q)
            with eng.Fori(1, TILES) as t:
                for q in range(2):
                    body(t, q, 2 * t + q)
            body(TILES, 0, CHUNKS)

        def below_of(c, n):
            return isinstance(c, int) and c < n

        consts = (("gram_mask", gram_mask), ("small_mask", small_mask), ("block_mask", block_mask), ("row_pick", row_pick),
                  ("unit8", unit8), ("level_mask", level_mask), ("block_ones", block_ones), ("ident", ident),
                  ("gn_g", gn_g), ("gn_b", gn_b))
        s_sample = m.sb("s_sample", 128, 4, NB, 64)
        spread8, spread_u, spread_v = m.sb("spread8", 128, NB, 64), m.sb("spread_u", 128, NB, 64), m.sb("spread_v", 128, NB, 64)
        seq_mask = m.sb("seq_mask", 128, NB)
        s_next, yr, y_own = m.sb("s_next", 128, NB, 64), m.sb("yr", 128, 64), m.sb("y_own", 128, DT, 64)
        s_loaded, s_stored = [m.sem(f"s_loaded{k}") for k in range(4)], m.sem("s_stored")
        big_made, own_z, own_u, own_u_kept, own_spread, own_y, own_s, own_yr, own_added, own_done, chained = (m.sem(x) for x in (
            "big_made", "own_z", "own_u", "own_u_kept", "own_spread", "own_y", "own_s", "own_yr", "own_added", "own_done", "chained"))

        def widen(eng, k, s, c, done, copy):
            n = slice(0, 64) if isinstance(c, int) and c == CHUNKS else slice(64 * s, 64 * s + 64)
            for h in range(2):
                p = slice(64 * h, 64 * h + 64)
                copy(wide[p, k, 8 * s:8 * s + 8, 64 * h:64 * h + 64], ops[p, k, :, n]).then_inc(done, 1)

        with nc.Block() as block:
            @block.sync
            def _(sp):
                for name, dst in consts:
                    sp.dma_start(dst[:], a[name]).then_inc(consts_loaded, 16)
                sp.dma_start(seq_mask[:], a["seq_mask"]).then_inc(consts_loaded, 16)

                def body(t, n, first):
                    if not first:
                        sp.wait_ge(gram_made, 8 * t)
                        sp.wait_ge(q_widened, 8 * t)
                        sp.wait_ge(k_widened, 8 * t)
                    for k, name in enumerate(("kt", "rt", "bh", "kh")):
                        sp.dma_start(ops[:, k, :, 0:n], scr[name][t, :, :, 0:n]).then_inc(ops_loaded, 16)
                    if not first:
                        sp.wait_ge(v_turned, 4 * t)
                    sp.dma_start(v_in[:, :, 0:n], scr["v"][t, :, :, 0:n]).then_inc(v_loaded, 16)
                    if not first:
                        sp.wait_ge(y_gated, 2 * t)
                        sp.dma_start(scr["y"][t - 1], gated[:]).then_inc(y_stored, 16)
                    sp.dma_start(gate[:, :, 0:n], scr["g"][t, :, :, 0:n]).then_inc(gate_loaded, 16)
                body(0, 128, True)
                with sp.Fori(1, TILES) as t:
                    body(t, 128, False)
                body(TILES, 64, False)
                sp.wait_ge(s_kept, 2 * CHUNKS)
                sp.dma_start(outp["wkv_prompt"], state[:, 0]).then_inc(s_stored, 16)
                for pair in range(4):
                    sp.dma_start(s_sample[:, pair], a["s_sample"][:, pair]).then_inc(s_loaded[pair], 16)
                for pair in range(DT):
                    sp.wait_ge(own_done, pair + 1)
                    sp.dma_start(outp["wkv_sample"][:, pair], s_next[:]).then_inc(s_stored, 16)
                    if pair + 4 < DT:
                        sp.dma_start(s_sample[:, pair], a["s_sample"][:, pair + 4]).then_inc(s_loaded[pair], 16)
                sp.wait_ge(y_gated, CHUNKS + 1)
                sp.dma_start(scr["y"][TILES, :, :, 0:64], gated[:, :, 0:64]).then_inc(y_stored, 16)
                sp.wait_ge(y_stored, 16 * (TILES + 1))
                sp.wait_ge(s_stored, 16 * (DT + 1))

            @block.gpsimd
            def _(pool):
                pool.memset(wide[:], 0.0).then_inc(zeroed, 1)
                pool.memset(state[:], 0.0).then_inc(zeroed, 1)
                pool.wait_ge(consts_loaded, 176)
                pool.wait_ge(zeroed, 2)

                def body(t, s, c):
                    pool.wait_ge(ops_loaded, 64 * (t + 1))
                    if not below_of(c, 1):
                        pool.wait_ge(below_made, 3 * c)
                    if not below_of(c, 2):
                        pool.wait_ge(y_made, c - 1)
                    pool.sem_inc(pool_turns, 1)
                    for k in range(2):
                        widen(pool, k, s, c, q_widened, pool.tensor_copy)
                    pool.wait_ge(q_widened, 4 * c + 4)
                    pool.wait_ge(gram_kept, 8 * c + 8)
                    for lev in range(3):
                        pool.wait_ge(lm_made, 6 * c + 2 * lev)
                        pool.tensor_tensor(below[:], grams[:, 8 * s:8 * s + 8, 0, :],
                                           level_mask[:, lev:lev + 1, :].broadcast_to([128, 8, 128]), ALU.mult).then_inc(below_made, 1)
                steps(pool, body)

            @block.tensor
            def _(pe):
                pe.wait_ge(consts_loaded, 176)

                def inverse_begins(t, s, c):
                    pe.wait_ge(ops_loaded, 64 * (t + 1))
                    pe.wait_ge(k_widened, 4 * c + 4)
                    for n in range(4):
                        g, k = n // 2, n % 2
                        if n % 2 == 0 and not below_of(c, 1):
                            pe.wait_ge(grown_kept, 10 * c - 2 + n)
                        pe.sem_inc(pe_turns, 1)
                        for j in range(4):
                            mm = pe.transpose(mb[:, ROW_BANK[n], 128 * j:128 * j + 128], wide[:, 2 + k, 8 * s + 4 * g + j, :], ident[:])
                        mm.then_inc(rows_turned, 1)
                        if n >= 2:
                            pe.wait_ge(gram_kept, 8 * c + 2 * (n - 2) + 2)
                        elif n == 0 and not below_of(c, 2):
                            pe.wait_ge(normed, NORM * (c - 2) + 3)
                        elif n == 1 and not below_of(c, 3):
                            pe.wait_ge(y_gated, c - 2)
                        for j in range(2):
                            pair = 2 * n + j
                            rhs = ops[:, 0:2, pair, 64 * s:64 * s + 64]
                            for k in range(2):
                                mm = pe.matmul(gbank[n % 2][:, 256 * j + 128 * k:256 * j + 128 * k + 128],
                                               wide[:, 2 + k, 8 * s + pair, :], rhs, start=True, stop=True)
                        mm.then_inc(gram_made, 1)
                    pe.wait_ge(v_loaded, 16 * (t + 1))
                    pe.sem_inc(pe_turns, 1)
                    for g in range(2):
                        for j in range(4):
                            mm = pe.transpose(wb[0:64, g, 128 * j:128 * j + 128], v_in[:, 4 * g + j, 64 * s:64 * s + 64], ident[:])
                        mm.then_inc(v_turned, 1)
                    if not below_of(c, 1):
                        products_with_state(1 - s, c - 1, c)
                    pe.wait_ge(gram_kept, 8 * c + 8)
                    if not below_of(c, 2):
                        turn_y(c - 2)
                    pe.wait_ge(picked, c + 1)
                    pe.wait_ge(v_kept, 2 * c + 1)
                    pe.matmul(wb[:, 0, :], block_ones[:], pick[:], start=True, stop=True).then_inc(spread, 1)

                def inverse_ends(s, c):
                    pe.wait_ge(solved_wide, c + 1)
                    pe.wait_ge(rows_kept, 4 * c + 4)
                    for g in range(2):
                        for j in range(4):
                            mm = pe.transpose(mb[:, g, 128 * j:128 * j + 128], inv_t[:, 8 * s + 4 * g + j, :], ident[:])
                        mm.then_inc(inv_turned, 1)
                    if not below_of(c, 1):
                        pe.wait_ge(s_kept, 2 * c - 1)
                    for lev in range(3):
                        for g in range(2):
                            pe.wait_ge(below_made, 3 * c + lev + 1)
                            if lev == 0:
                                pe.wait_ge(inv_kept, 2 * c + g + 1)
                            else:
                                pe.wait_ge(grown_kept, 10 * c + 4 * (lev - 1) + 2 * g + 1)
                            for j in range(4):
                                mm = pe.matmul(wb[:, g, 128 * j:128 * j + 128], below[:, 4 * g + j, :], inv[:, 4 * g + j, :], start=True, stop=True)
                            mm.then_inc(lm_made, 1)
                        for g in range(2):
                            pe.wait_ge(lm_kept, 6 * c + 2 * lev + g + 1)
                            if lev == 0:
                                pe.wait_ge(inv_kept, 2 * c + 2)
                            else:
                                pe.wait_ge(grown_kept, 10 * c + 4 * (lev - 1) + 2 * g + 2)
                            if lev < 2:
                                for j in range(4):
                                    mm = pe.matmul(mb[:, 2 * g + 1, 128 * j:128 * j + 128], inv_t[:, 8 * s + 4 * g + j, :], lm[:, g, 128 * j:128 * j + 128], start=True, stop=True)
                                mm.then_inc(grown, 1)
                            for j in range(4):
                                mm = pe.matmul(mb[:, 2 * g, 128 * j:128 * j + 128], lm[:, g, 128 * j:128 * j + 128], inv_t[:, 8 * s + 4 * g + j, :], start=True, stop=True)
                            mm.then_inc(grown, 1)

                def products_with_state(s, c, now):
                    if below_of(c, 1):
                        pe.wait_ge(zeroed, 2)
                    else:
                        pe.wait_ge(s_kept, 2 * c)
                    pe.wait_ge(q_widened, 4 * c + 4)
                    for half in range(2):
                        pe.wait_ge(rows_kept, 4 * now + 4)
                        for j in range(4):
                            pair = 4 * half + j
                            unit, o = 8 * s + pair, mb[:, half, 64 * j:64 * j + 64]
                            pe.matmul(o, wide[:, 0, unit, :], state[:, s, pair, :], start=True, stop=False)
                            mm = pe.matmul(o, grams[:, unit, 2, :], v_rows[:, unit, :], start=False, stop=True)
                        mm.then_inc(z_made, 1)

                def chunk_behind(s, c, now):
                    for half in range(2):
                        pe.wait_ge(z_kept, 2 * c + half + 1)
                        for j in range(4):
                            unit = 8 * s + 4 * half + j
                            mm = pe.matmul(mb[:, 2 + half, 64 * j:64 * j + 64], inv_t[:, unit, :], z[:, half, 64 * j:64 * j + 64], start=True, stop=True)
                        mm.then_inc(u_made, 1)
                    pe.wait_ge(v_kept, 2 * now + 2)
                    for pair in range(8):
                        unit = 8 * s + pair
                        if pair % 4 == 0:
                            pe.wait_ge(u_kept, 2 * c + pair // 4 + 1)
                        o = wb[:, 1, 64 * pair:64 * pair + 64]
                        pe.matmul(o, rows[:, 0, unit, :], u[:, pair // 4, 64 * (pair % 4):64 * (pair % 4) + 64], start=True, stop=False)
                        mm = pe.matmul(o, rows[:, 1, unit, :], v_rows[:, unit, :], start=False, stop=True)
                    mm.then_inc(s_made, 1)
                    for pair in range(8):
                        unit, half, o = 8 * s + pair, pair // 4, ga[:, 64 * pair:64 * pair + 64]
                        pe.matmul(o, wide[:, 1, unit, :], state[:, s, pair, :], start=True, stop=False)
                        pe.matmul(o, grams[:, unit, 1, :], u[:, half, 64 * (pair % 4):64 * (pair % 4) + 64], start=False, stop=False)
                        mm = pe.matmul(o, grams[:, unit, 3, :], v_rows[:, unit, :], start=False, stop=True)
                    mm.then_inc(y_made, 1)

                def turn_y(c):
                    pe.wait_ge(normed, NORM * (c + 1))
                    if not below_of(c, 1):
                        pe.wait_ge(y_gated, c)
                    for j in range(4):
                        mm = pe.transpose(gb[:, 128 * j:128 * j + 128], y3[:, 2 * j:2 * j + 2, :], ident[:])
                    mm.then_inc(y_turned, 1)

                def body(t, s, c):
                    inverse_begins(t, s, c)
                    if not below_of(c, 1):
                        chunk_behind(1 - s, c - 1, c)
                    inverse_ends(s, c)
                steps(pe, body)

                turn_y(CHUNKS - 1)
                pe.wait_ge(grown_kept, 10 * CHUNKS + 10)
                pe.wait_ge(q_widened, 4 * CHUNKS + 4)

                def all_states(pair):
                    k = pair % 4
                    pe.wait_ge(s_loaded[k], 16 * (pair // 4 + 1))
                    if pair:
                        pe.wait_ge(own_yr, pair)
                    pe.matmul(mb[:, 0, :], wide[:, 0, pair, :], s_sample[:, k], start=True, stop=True)
                    pe.matmul(mb[:, 1, :], wide[:, 1, pair, :], s_sample[:, k], start=True, stop=True)
                    pe.matmul(mb[:, 2, 0:64], grams[:, pair, 2, :], v_rows[:, pair, :], start=True, stop=True).then_inc(big_made, 1)

                all_states(0)
                for pair in range(DT):
                    pe.wait_ge(own_z, pair + 1)
                    if pair:
                        pe.wait_ge(own_u_kept, pair)
                    pe.matmul(wb[:, 0, 0:64], inv_t[:, pair, :], z[:, 0, 0:64], start=True, stop=True).then_inc(own_u, 1)
                    pe.wait_ge(own_u_kept, pair + 1)
                    if pair:
                        pe.wait_ge(own_added, pair)
                    pe.matmul(mb[:, 3, 0:64], grams[:, pair, 1, :], u[:, 0, 0:64], start=True, stop=False)
                    pe.matmul(mb[:, 3, 0:64], grams[:, pair, 3, :], v_rows[:, pair, :], start=False, stop=True).then_inc(own_y, 1)
                    if pair < DT - 1:
                        all_states(pair + 1)
                    pe.wait_ge(own_spread, pair + 1)
                    pe.matmul(wb[:, 1, :], rows[:, 0, pair, :], spread_u[:], start=True, stop=False)
                    pe.matmul(wb[:, 1, :], rows[:, 1, pair, :], spread_v[:], start=False, stop=True).then_inc(own_s, 1)
                turn_y(CHUNKS)

            @block.scalar
            def _(act):
                def widen_next(t, s, c):
                    act.wait_ge(ops_loaded, 64 * (t + 1))
                    if not below_of(c, 2):
                        act.wait_ge(gram_made, 4 * (c - 1))
                        act.wait_ge(rows_turned, 4 * (c - 1))
                    act.sem_inc(act_turns, 1)
                    for k in (2, 3):
                        widen(act, k, s, c, k_widened, lambda dst, src: act.activation(dst, src, ACT.Copy))

                act.wait_ge(zeroed, 2)
                widen_next(0, 0, 0)

                def body(t, s, c):
                    if not below_of(c, 2):
                        act.wait_ge(s_made, c - 1)
                        act.wait_ge(y_made, c - 1)
                        act.wait_ge(normed, NORM * (c - 2) + 1)
                    for n in range(4):
                        g, k = n // 2, n % 2
                        act.wait_ge(rows_turned, 4 * c + n + 1)
                        act.activation(rows[:, k, 8 * s + 4 * g:8 * s + 4 * g + 4, :], mb[:, ROW_BANK[n], :].rearrange("p (j n) -> p j n", j=4),
                                       ACT.Copy, scale=-1.0 if k == 0 else 1.0).then_inc(rows_kept, 1)
                    for g in range(2):
                        act.wait_ge(v_turned, 2 * c + g + 1)
                        src = wb[0:64, g, :].rearrange("p (j n) -> p j n", j=4)
                        act.activation(v_rows[0:64, 8 * s + 4 * g:8 * s + 4 * g + 4, :], src[:, :, 0:64], ACT.Copy)
                        act.activation(v_rows[64:128, 8 * s + 4 * g:8 * s + 4 * g + 4, :], src[:, :, 64:128], ACT.Copy).then_inc(v_kept, 1)
                    behind = c - 1
                    if not below_of(c, 1):
                        for half in range(2):
                            act.wait_ge(z_made, 2 * behind + half + 1)
                            if not below_of(behind, 1):
                                act.wait_ge(u_made, 2 * behind)
                            act.activation(z[:, half], mb[:, half, 0:256], ACT.Copy).then_inc(z_kept, 1)
                        for half in range(2):
                            act.wait_ge(u_made, 2 * behind + half + 1)
                            if not below_of(behind, 1):
                                act.wait_ge(s_made, behind)
                                act.wait_ge(y_made, behind)
                            act.activation(u[:, half], mb[:, 2 + half, 0:256], ACT.Copy).then_inc(u_kept, 1)
                    for g in range(2):
                        act.wait_ge(inv_turned, 2 * c + g + 1)
                        if not below_of(c, 1):
                            act.wait_ge(lm_made, 6 * c)
                        act.activation(inv[:, 4 * g:4 * g + 4, :], mb[:, g, :].rearrange("p (j n) -> p j n", j=4), ACT.Copy).then_inc(inv_kept, 1)
                    for lev in range(3):
                        for g in range(2):
                            act.wait_ge(lm_made, 6 * c + 2 * lev + g + 1)
                            if lev:
                                act.wait_ge(grown, 10 * c + 4 * (lev - 1) + 2 * g + 2)
                            elif not below_of(c, 1):
                                act.wait_ge(grown, 10 * c)
                            act.activation(lm[:, g, :], wb[:, g, :], ACT.Copy).then_inc(lm_kept, 1)
                        if lev == 0 and not below_of(c, 1):
                            act.wait_ge(normed, NORM * behind + 3)
                            act.activation(y2[:], y[:], ACT.Square).then_inc(y_squared, 1)
                        if lev == 0 and not (isinstance(c, int) and c == CHUNKS):
                            widen_next(t + s, 1 - s, c + 1)
                        if lev == 1 and not below_of(c, 1):
                            act.wait_ge(normed, NORM * behind + 5)
                            act.activation(stat[:, 1], stat[:, 1], ACT.Sqrt).then_inc(y_rooted, 1)
                steps(act, body)
                act.wait_ge(s_made, CHUNKS)
                for pair in range(DT):
                    act.wait_ge(own_u, pair + 1)
                    if pair:
                        act.wait_ge(own_y, pair)
                        act.wait_ge(own_spread, pair)
                    act.activation(u[:, 0, 0:64], wb[:, 0, 0:64], ACT.Copy).then_inc(own_u_kept, 1)
                act.wait_ge(normed, NORM * CHUNKS + 3)
                act.activation(y2[:], y[:], ACT.Square).then_inc(y_squared, 1)
                act.wait_ge(normed, NORM * CHUNKS + 5)
                act.activation(stat[:, 1], stat[:, 1], ACT.Sqrt).then_inc(y_rooted, 1)

            @block.vector
            def _(dve):
                dve.wait_ge(consts_loaded, 176)

                def per(x):
                    return x[:, :].rearrange("p (j o) -> p j o", o=1).broadcast_to([128, DT, 64])

                def norm_1(s, c, y_in):
                    at = NORM * c
                    if not below_of(c, 1):
                        dve.wait_ge(normed, at)
                    by = keep["bonus"][:, ds(c, 1), :].rearrange("p o (j u) -> p (o j) u", u=1).broadcast_to([128, DT, 64])
                    dve.tensor_tensor(bonus[:], v_rows[:, 8 * s:8 * s + 8, :], by, ALU.mult).then_inc(normed, 1)
                    if y_in is None:
                        dve.wait_ge(y_made, c + 1)
                        y_in = ga[:, :].rearrange("p (j n) -> p j n", j=DT)
                    dve.tensor_reduce(stat[:, 0], y_in, AX, ALU.add).then_inc(normed, 1)
                    dve.wait_ge(normed, at + 2)
                    dve.scalar_tensor_tensor(y[:], per(stat[:, 0]), -1.0 / HD, y_in, ALU.mult, ALU.add).then_inc(normed, 1)

                def norm_2(c):
                    dve.wait_ge(y_squared, c + 1)
                    dve.tensor_reduce(stat[:, 2], y2[:], AX, ALU.add).then_inc(normed, 1)
                    dve.wait_ge(normed, NORM * c + 4)
                    dve.tensor_scalar(stat[:, 1], stat[:, 2], 1.0 / HD, GN_EPS, ALU.mult, ALU.add).then_inc(normed, 1)

                def norm_3(c):
                    dve.wait_ge(y_rooted, c + 1)
                    dve.reciprocal(stat[:, 2], stat[:, 1]).then_inc(normed, 1)
                    dve.wait_ge(normed, NORM * c + 6)
                    dve.tensor_tensor(y[:], y[:], per(stat[:, 2]), ALU.mult).then_inc(normed, 1)
                    dve.wait_ge(normed, NORM * c + 7)
                    dve.tensor_tensor(y[:], y[:], gn_g[:], ALU.mult).then_inc(normed, 1)

                def norm_4(c):
                    dve.wait_ge(normed, NORM * c + 8)
                    dve.tensor_tensor(y[:], y[:], gn_b[:], ALU.add).then_inc(normed, 1)
                    dve.wait_ge(normed, NORM * c + 9)
                    if not below_of(c, 1):
                        dve.wait_ge(y_turned, c)
                    dve.tensor_tensor(y3[:], y[:], bonus[:], ALU.add).then_inc(normed, 1)

                def gate_rows(t, s, c):
                    dve.wait_ge(y_turned, c + 1)
                    dve.wait_ge(gate_loaded, 16 * (t + 1))
                    if s == 0 and not below_of(t, 1):
                        dve.wait_ge(y_stored, 16 * t)
                    dve.tensor_tensor(gated[:, :, 64 * s:64 * s + 64], gb[:, :].rearrange("p (j n) -> p j n", j=DT),
                                      gate[:, :, 64 * s:64 * s + 64], ALU.mult).then_inc(y_gated, 1)

                def body(t, s, c):
                    kind = 1 if isinstance(c, int) and c == CHUNKS else 0
                    if not below_of(c, 2):
                        dve.wait_ge(y_made, c - 1)
                        dve.wait_ge(below_made, 3 * (c - 1))
                    if not below_of(c, 1):
                        dve.wait_ge(coeff_made, c)
                    for n in range(4):
                        dve.wait_ge(gram_made, 4 * c + n + 1)
                        two = gbank[n % 2][:, :].rearrange("p (j k n) -> p j k n", j=2, k=4)
                        dve.tensor_tensor(small[:, 2 * n:2 * n + 2, :], two[:, :, 0, :],
                                          small_mask[:, :].rearrange("p (o n) -> p o n", o=1).broadcast_to([128, 2, 64]), ALU.mult).then_inc(gram_small, 1)
                        for j in range(2):
                            src = two[:, j].rearrange("p k (o n) -> p k o n", o=1).broadcast_to([128, 4, 2, 64])
                            dve.tensor_tensor(grams[:, 8 * s + 2 * n + j].rearrange("p k (h n) -> p k h n", h=2), src,
                                              gram_mask[:, kind].rearrange("p k (h n) -> p k h n", h=2), ALU.mult).then_inc(gram_kept, 1)
                    dve.wait_ge(gram_small, 4 * c + 4)
                    dve.tensor_reduce(coeff[:], small[:].rearrange("p u (b n) -> p u n b", b=8), AX, ALU.add).then_inc(coeff_made, 1)
                    dve.wait_ge(coeff_made, c + 1)
                    src = coeff[:].rearrange("p u (o n) -> p u o n", o=1).broadcast_to([128, 8, 8, 8])
                    sel = row_pick[:, :].rearrange("p (u j n) -> p u j n", u=1, n=1).broadcast_to([128, 8, 8, 8])
                    dve.tensor_tensor(pick[:].rearrange("p u (j n) -> p u j n", j=8), src, sel, ALU.mult).then_inc(picked, 1)
                    if not below_of(c, 2):
                        gate_rows(t - 1, s, c - 2)
                    at = 15 * c
                    dve.tensor_copy(solved[:], unit8[:, :].rearrange("p (o n) -> p o n", o=1).broadcast_to([128, 8, 8])).then_inc(solving, 1)
                    dve.wait_ge(spread, c + 1)
                    blocks = wb[:, 0, :].rearrange("p (u j n) -> p u j n", u=8, j=8)
                    for j in range(7):
                        dve.wait_ge(solving, at + 2 * j + 1)
                        dve.tensor_tensor(term[:, :, 0:7 - j], solved[:, :, j:j + 1].broadcast_to([128, 8, 7 - j]), blocks[:, :, j, j + 1:8], ALU.mult).then_inc(solving, 1)
                        dve.wait_ge(solving, at + 2 * j + 2)
                        dve.tensor_tensor(solved[:, :, j + 1:8], solved[:, :, j + 1:8], term[:, :, 0:7 - j], ALU.add).then_inc(solving, 1)
                    dve.wait_ge(solving, at + 15)
                    if not below_of(c, 2):
                        dve.wait_ge(u_made, 2 * (c - 1))
                    src = solved[:].rearrange("p u (o n) -> p u o n", o=1).broadcast_to([128, 8, 16, 8])
                    sel = block_mask[:, :].rearrange("p (u b n) -> p u b n", u=1, n=1).broadcast_to([128, 8, 16, 8])
                    dve.tensor_tensor(inv_t[:, 8 * s:8 * s + 8, :].rearrange("p u (b n) -> p u b n", b=16), src, sel, ALU.mult).then_inc(solved_wide, 1)
                    behind = c - 1
                    if not below_of(c, 1):
                        new = state[:, s]
                        dve.wait_ge(s_made, behind + 1)
                        if not below_of(behind, 1):
                            dve.wait_ge(y_made, behind)
                        dve.tensor_tensor(new, state[:, 1 - s], wb[:, 1, :].rearrange("p (j n) -> p j n", j=DT), ALU.add).then_inc(s_kept, 1)
                        dve.wait_ge(s_kept, 2 * behind + 1)
                        end = keep["ends"][:, :, ds(behind, 1)].broadcast_to([128, DT, 64])
                        dve.tensor_tensor(new, new, end, ALU.mult).then_inc(s_kept, 1)
                        norm_1(1 - s, behind, None)
                    for lev in range(3):
                        each = 2 if lev < 2 else 1
                        for g in range(2):
                            for at, k in enumerate((1, 0) if lev < 2 else (0,)):
                                dve.wait_ge(grown, 10 * c + 4 * lev + each * g + at + 1)
                                dst = inv_t[:, 8 * s + 4 * g:8 * s + 4 * g + 4, :] if k == 0 else inv[:, 4 * g:4 * g + 4, :]
                                dve.tensor_tensor(dst, dst, mb[:, 2 * g + k, :].rearrange("p (j n) -> p j n", j=4), ALU.add).then_inc(grown_kept, 1)
                        if not below_of(c, 1):
                            (norm_2, norm_3, norm_4)[lev](behind)
                steps(dve, body)
                gate_rows(TILES - 1, 1, CHUNKS - 1)

                own = seq_mask[:, :].rearrange("p (b o) -> p b o", o=1).broadcast_to([128, NB, 64])
                count = [0]

                def then(ins):
                    count[0] += 1
                    ins.then_inc(chained, 1)
                    dve.wait_ge(chained, count[0])

                def own_rows(pair):
                    dve.wait_ge(big_made, pair + 1)
                    then(dve.tensor_tensor(spread8[:], mb[:, 0, :].rearrange("p (b n) -> p b n", b=NB), own, ALU.mult))
                    if pair:
                        dve.wait_ge(own_u, pair)
                    then(dve.tensor_reduce(z[:, 1, 0:64], spread8[:].rearrange("p b n -> p n b"), AX, ALU.add))
                    dve.tensor_tensor(z[:, 0, 0:64], z[:, 1, 0:64], mb[:, 2, 0:64], ALU.add).then_inc(own_z, 1)
                    then(dve.tensor_tensor(spread8[:], mb[:, 1, :].rearrange("p (b n) -> p b n", b=NB), own, ALU.mult))
                    dve.tensor_reduce(yr[:], spread8[:].rearrange("p b n -> p n b"), AX, ALU.add).then_inc(own_yr, 1)

                own_rows(0)
                for pair in range(DT):
                    if pair:
                        dve.wait_ge(own_s, pair)
                    dve.tensor_tensor(spread_v[:], v_rows[:, pair:pair + 1, :].broadcast_to([128, NB, 64]), own, ALU.mult)
                    dve.wait_ge(own_u_kept, pair + 1)
                    dve.tensor_tensor(spread_u[:], u[:, 0:1, 0:64].broadcast_to([128, NB, 64]), own, ALU.mult).then_inc(own_spread, 1)
                    dve.wait_ge(own_y, pair + 1)
                    dve.wait_ge(own_yr, pair + 1)
                    dve.tensor_tensor(y_own[:, pair, :], yr[:], mb[:, 3, 0:64], ALU.add).then_inc(own_added, 1)
                    dve.wait_ge(own_added, pair + 1)
                    if pair < DT - 1:
                        own_rows(pair + 1)
                    dve.wait_ge(own_s, pair + 1)
                    if pair:
                        dve.wait_ge(s_stored, 16 * (pair + 1))
                    then(dve.tensor_tensor(s_next[:], s_sample[:, pair % 4], wb[:, 1, :].rearrange("p (b n) -> p b n", b=NB), ALU.add))
                    end = keep["ends_sample"][:, pair, :].rearrange("p (b o) -> p b o", o=1).broadcast_to([128, NB, 64])
                    dve.tensor_tensor(s_next[:], s_next[:], end, ALU.mult).then_inc(own_done, 1)
                dve.wait_ge(chained, count[0])
                norm_1(0, CHUNKS, y_own[:])
                norm_2(CHUNKS)
                norm_3(CHUNKS)
                norm_4(CHUNKS)
                gate_rows(TILES, 0, CHUNKS)


def three_passes(pe, out, w_high, w_low, r_high, r_low, columns):
    for d in range(DT):
        for k, (w, r) in enumerate(((w_high, r_high), (w_high, r_low), (w_low, r_high))):
            mm = pe.matmul(out, w[:, d, :], r[:, d, columns], start=d == 0 and k == 0, stop=d == DT - 1 and k == 2)
    return mm


def project_and_norm(nc, a, stage, weights, gain, shift, rhs, load_rhs, x, load_residual, store):
    with Tensors(nc, stage) as m:
        wt = m.sb("wt", 128, 2, DT, 128)
        w_high, w_low = (m.sb(x, 128, 2, DT, 128, dtype=F32R) for x in ("w_high", "w_low"))
        r_high, r_low = (m.sb(x, 128, DT, N, dtype=F32R) for x in ("r_high", "r_low"))
        square = rhs
        channel_sum, rstd = m.sb("channel_sum", 128, N), m.sb("rstd", 128, N)
        g, b, mean_ones = m.sb("g", 128, DT), m.sb("b", 128, DT), m.sb("mean_ones", 128, 128)
        acc = m.ps("acc", 128, 2, 3, 512)
        small_loaded, rhs_loaded, res_loaded = m.sem("small_loaded"), m.sem("rhs_loaded"), m.sem("res_loaded")
        w_loaded = [m.sem(f"w_loaded{i}") for i in range(2)]
        r_rounded, r_split, w_rounded, w_split, column_summed = (m.sem(x) for x in ("r_rounded", "r_split", "w_rounded", "w_split", "column_summed"))
        acc_made, added, mean_made, centred, squared, halved, var_made = (m.sem(x) for x in (
            "acc_made", "added", "mean_made", "centred", "squared", "halved", "var_made"))
        shifted, rooted, inverted, scaled, finished, stored = (m.sem(x) for x in ("shifted", "rooted", "inverted", "scaled", "finished", "stored"))
        act_turns, pool_turns = m.sem("act_turns"), m.sem("pool_turns")

        def jobs(eng, body):
            body(0, True)
            with eng.Fori(1, DT // 2) as i:
                body(i, False)

        with nc.Block() as block:
            @block.sync
            def _(sp):
                load_rhs(sp, rhs_loaded)

                def body(i, first):
                    for s in range(2):
                        if not first:
                            sp.wait_ge(acc_made, 3 * (2 * i + s - 1))
                        sp.dma_start(wt[:, s], weights[2 * i + s]).then_inc(w_loaded[s], 16)
                    if first:
                        load_residual(sp, res_loaded)
                        for dst, src in ((g, gain), (b, shift), (mean_ones, a["mean_ones"])):
                            sp.dma_start(dst[:], src).then_inc(small_loaded, 16)
                jobs(sp, body)
                if store is not None:
                    for k in range(3):
                        sp.wait_ge(finished, DT * (k + 1))
                        store(sp, k, stored)
                    sp.wait_ge(stored, 48)

            @block.tensor
            def _(pe):
                pe.wait_ge(r_split, DT)

                def body(i, first):
                    for s in range(2):
                        pe.wait_ge(w_split, 2 * i + s + 1)
                        for k, (n0, n) in enumerate(PARTS):
                            if not first:
                                pe.wait_ge(added, 3 * (2 * i + s - 2) + k + 1)
                            three_passes(pe, acc[:, s, k, 0:n], w_high[:, s], w_low[:, s], r_high, r_low, slice(n0, n0 + n)).then_inc(acc_made, 1)
                jobs(pe, body)
                pe.wait_ge(small_loaded, 48)
                pe.wait_ge(added, 3 * DT)
                pe.wait_ge(column_summed, DT)
                for k, (n0, n) in enumerate(PARTS):
                    pe.matmul(acc[:, 0, k, 0:n], mean_ones[:], channel_sum[:, n0:n0 + n], start=True, stop=True).then_inc(mean_made, 1)
                for k, (n0, n) in enumerate(PARTS):
                    pe.wait_ge(halved, k + 1)
                    for d in range(DT // 2):
                        mm = pe.matmul(acc[:, 1, k, 0:n], mean_ones[:], square[:, d, n0:n0 + n], start=d == 0, stop=d == DT // 2 - 1)
                    mm.then_inc(var_made, 1)

            @block.gpsimd
            def _(pool):
                for first, j in ((True, 0), (False, None)):
                    def add(j):
                        pool.wait_ge(added, 3 * j + 3)
                        pool.wait_ge(column_summed, j)
                        pool.sem_inc(pool_turns, 1)
                        pool.tensor_tensor(channel_sum[:], channel_sum[:], x[:, ds(j, 1), :].rearrange("p o n -> p (o n)"), ALU.add).then_inc(column_summed, 1)
                    if first:
                        pool.wait_ge(added, 3)
                        pool.tensor_copy(channel_sum[:], x[:, 0, :]).then_inc(column_summed, 1)
                    else:
                        with pool.Fori(1, DT) as i:
                            add(i)

            @block.vector
            def _(dve):
                dve.wait_ge(rhs_loaded, rhs_count(load_rhs)) if load_rhs.count else None
                for d in range(DT):
                    dve.wait_ge(r_rounded, d + 1)
                    dve.tensor_tensor(r_low[:, d, :], rhs[:, d, :], r_high[:, d, :].bitcast(F32), ALU.subtract).then_inc(r_split, 1)

                def add(job, s):
                    for k, (n0, n) in enumerate(PARTS):
                        dve.wait_ge(acc_made, 3 * job + k + 1)
                        row = x[:, ds(job, 1), n0:n0 + n].rearrange("p o n -> p (o n)")
                        dve.scalar_tensor_tensor(row, row, ALPHA, acc[:, s, k, 0:n], ALU.mult, ALU.add).then_inc(added, 1)

                def body(i, first):
                    for s in range(2):
                        dve.wait_ge(w_rounded, 2 * i + s + 1)
                        dve.tensor_tensor(w_low[:, s], wt[:, s], w_high[:, s].bitcast(F32), ALU.subtract).then_inc(w_split, 1)
                        if first and s == 0:
                            dve.wait_ge(res_loaded, rhs_count(load_residual)) if load_residual.count else None
                        else:
                            add(2 * i + s - 1, 1 - s)
                jobs(dve, body)
                add(DT - 1, 1)
                dve.wait_ge(added, 3 * DT)
                for k, (n0, n) in enumerate(PARTS):
                    dve.wait_ge(mean_made, k + 1)
                    mean = acc[:, 0, k:k + 1, 0:n].broadcast_to([128, DT, n])
                    dve.tensor_tensor(x[:, :, n0:n0 + n], x[:, :, n0:n0 + n], mean, ALU.subtract).then_inc(centred, 1)
                for k, (n0, n) in enumerate(PARTS):
                    dve.wait_ge(squared, k + 1)
                    low, high = square[:, 0:DT // 2, n0:n0 + n], square[:, DT // 2:DT, n0:n0 + n]
                    dve.tensor_tensor(low, low, high, ALU.add).then_inc(halved, 1)
                for k, (n0, n) in enumerate(PARTS):
                    dve.wait_ge(var_made, k + 1)
                    dve.tensor_scalar(rstd[:, n0:n0 + n], acc[:, 1, k, 0:n], LN_EPS, None, ALU.add).then_inc(shifted, 1)
                for k, (n0, n) in enumerate(PARTS):
                    dve.wait_ge(rooted, k + 1)
                    dve.reciprocal(rstd[:, n0:n0 + n], rstd[:, n0:n0 + n]).then_inc(inverted, 1)
                    dve.wait_ge(inverted, k + 1)
                    inv = rstd[:, n0:n0 + n].rearrange("p (o n) -> p o n", o=1).broadcast_to([128, DT, n])
                    dve.tensor_tensor(x[:, :, n0:n0 + n], x[:, :, n0:n0 + n], inv, ALU.mult).then_inc(scaled, 1)

            @block.scalar
            def _(act):
                act.wait_ge(rhs_loaded, rhs_count(load_rhs)) if load_rhs.count else None
                for d in range(DT):
                    act.activation(r_high[:, d, :], rhs[:, d, :], ACT.Copy).then_inc(r_rounded, 1)

                def body(i, first):
                    for s in range(2):
                        act.wait_ge(w_loaded[s], 16 * (i + 1))
                        act.sem_inc(act_turns, 1)
                        act.activation(w_high[:, s], wt[:, s], ACT.Copy).then_inc(w_rounded, 1)
                jobs(act, body)
                act.wait_ge(small_loaded, 48)
                for k, (n0, n) in enumerate(PARTS):
                    act.wait_ge(centred, k + 1)
                    act.activation(square[:, :, n0:n0 + n], x[:, :, n0:n0 + n], ACT.Square).then_inc(squared, 1)
                for k, (n0, n) in enumerate(PARTS):
                    act.wait_ge(shifted, k + 1)
                    act.activation(rstd[:, n0:n0 + n], rstd[:, n0:n0 + n], ACT.Sqrt).then_inc(rooted, 1)
                for k, (n0, n) in enumerate(PARTS):
                    act.wait_ge(scaled, k + 1)
                    for d in range(DT):
                        act.activation(x[:, d, n0:n0 + n], x[:, d, n0:n0 + n], ACT.Identity, scale=g[:, d:d + 1], bias=b[:, d:d + 1]).then_inc(finished, 1)


def rhs_count(load):
    return 16 * load.count


def attention_projections(nc, a, scr, x):
    with Tensors(nc, "qkvg") as m:
        wt = m.sb("wt", 128, 2, DT, 128)
        w_high, w_low = (m.sb(x, 128, 2, DT, 128, dtype=F32R) for x in ("w_high", "w_low"))
        r_high, r_low = (m.sb(x, 128, DT, N, dtype=F32R) for x in ("r_high", "r_low"))
        out = m.sb("out", 128, 2, N)
        acc = m.ps("acc", 128, 2, 3, 512)
        w_loaded = [m.sem(f"w_loaded{i}") for i in range(2)]
        stored = [m.sem(f"stored{i}") for i in range(2)]
        r_rounded, r_split, w_rounded, w_split = (m.sem(x) for x in ("r_rounded", "r_split", "w_rounded", "w_split"))
        acc_made, evacuated = m.sem("acc_made"), m.sem("evacuated")
        dve_turns = m.sem("dve_turns")
        phases = (("aq", 0, DT), ("ak", DT, 2), ("av", DT + 2, 2), ("ag", DT + 4, DT))
        JOBS = 2 * DT + 4

        def pairs(eng, p, body):
            if p == 0:
                body(0, 0, True)
            start = 1 if p == 0 else 0
            with eng.Fori(start, phases[p][2] // 2) as i:
                body(i, phases[p][1] + 2 * i, False)

        def all_pairs(eng, body):
            body(0, 0, True)
            with eng.Fori(1, JOBS // 2) as i:
                body(i, 2 * i, False)

        with nc.Block() as block:
            @block.sync
            def _(sp):
                def body(i, job, first):
                    for s in range(2):
                        if not first:
                            sp.wait_ge(acc_made, 3 * (job + s - 1))
                        sp.dma_start(wt[:, s], a["w_att"][job + s]).then_inc(w_loaded[s], 16)
                all_pairs(sp, body)

            @block.vector
            def _(dve):
                for d in range(DT):
                    dve.wait_ge(r_rounded, d + 1)
                    dve.tensor_tensor(r_low[:, d, :], x[:, d, :], r_high[:, d, :].bitcast(F32), ALU.subtract).then_inc(r_split, 1)

                def body(i, job, first):
                    for s in range(2):
                        dve.wait_ge(w_loaded[s], 16 * (i + 1))
                        dve.sem_inc(dve_turns, 1)
                        dve.tensor_copy(w_high[:, s], wt[:, s]).then_inc(w_rounded, 1)
                        dve.wait_ge(w_rounded, job + s + 1)
                        dve.tensor_tensor(w_low[:, s], wt[:, s], w_high[:, s].bitcast(F32), ALU.subtract).then_inc(w_split, 1)
                all_pairs(dve, body)

            @block.tensor
            def _(pe):
                pe.wait_ge(r_split, DT)

                def body(i, job, first):
                    for s in range(2):
                        pe.wait_ge(w_split, job + s + 1)
                        for k, (n0, n) in enumerate(PARTS):
                            if not first:
                                pe.wait_ge(evacuated, 3 * (job + s - 2) + k + 1)
                            three_passes(pe, acc[:, s, k, 0:n], w_high[:, s], w_low[:, s], r_high, r_low, slice(n0, n0 + n)).then_inc(acc_made, 1)
                all_pairs(pe, body)

            @block.scalar
            def _(act):
                for d in range(DT):
                    act.activation(r_high[:, d, :], x[:, d, :], ACT.Copy).then_inc(r_rounded, 1)
                for p, (name, job0, _) in enumerate(phases):
                    def body(i, job, first, name=name, job0=job0):
                        for s in range(2):
                            if not first:
                                act.wait_ge(stored[s], 32 * (job0 // 2 + i))
                            for k, (n0, n) in enumerate(PARTS):
                                act.wait_ge(acc_made, 3 * (job + s) + k + 1)
                                act.activation(out[:, s, n0:n0 + n], acc[:, s, k, 0:n], ACT.Silu if name == "ag" else ACT.Copy).then_inc(evacuated, 1)
                            act.wait_ge(evacuated, 3 * (job + s) + 3)
                            store_tiles(act, scr[name], 2 * i + s, out[:, s], stored[s])
                    pairs(act, p, body)
                for s in range(2):
                    act.wait_ge(stored[s], 32 * 10)


def attention(nc, a, scr, outp, o):
    with Tensors(nc, "att") as m:
        q_in, k_in = m.sb("q_in", 128, 2, DT, 128), m.sb("k_in", 128, 2, 2, 128)
        v_in, gate = m.sb("v_in", 128, 2, 2, 128), m.sb("gate", 128, 2, DT, 128)
        keys = m.sb("keys", 128, KVH, 2, 2, 128)
        v_rows = m.sb("v_rows", 128, 2, 256)
        bias = m.sb("bias", 128, H, 3, 128)
        score = m.sb("score", 128, 2, H, 256)
        prob_t = m.sb("prob_t", 128, 2, 2, 512)
        sink, ident = m.sb("sink", 128, H), m.sb("ident", 128, 128)
        top, low, sums, extra, recip = (m.sb(x, 128, H) for x in ("top", "low", "sums", "extra", "recip"))
        sc = m.ps("sc", 128, 2, 512)
        turn = m.ps("turn", 128, 4, 512)
        pv = m.ps("pv", 128, 2, 512)
        small_loaded, zeroed = m.sem("small_loaded"), m.sem("zeroed")
        loaded = [m.sem(f"loaded{i}") for i in range(2)]
        gate_loaded = [m.sem(f"gate_loaded{i}") for i in range(2)]
        v_turned, v_kept, widened = m.sem("v_turned"), m.sem("v_kept"), m.sem("widened")
        scored, biased, topped, lowered, sunk = (m.sem(x) for x in ("scored", "biased", "topped", "lowered", "sunk"))
        raised, totalled, inverted, normed = (m.sem(x) for x in ("raised", "totalled", "inverted", "normed"))
        p_turned, p_kept, mixed, gated = (m.sem(x) for x in ("p_turned", "p_kept", "mixed", "gated"))
        copied = m.sem("copied")
        dve_turns, pool_turns, sp_turns, pe_turns = m.sem("dve_turns"), m.sem("pool_turns"), m.sem("sp_turns"), m.sem("pe_turns")

        def steps(eng, body):
            body(0, 0)
            body(1, 1)
            with eng.Fori(1, TILES // 2) as i:
                body(2 * i, 0)
                body(2 * i + 1, 1)

        def under(t, n):
            return isinstance(t, int) and t < n

        def slots(t):
            return (0,) if under(t, 1) else (0, 1)

        with nc.Block() as block:
            @block.sync
            def _(sp):
                def body(t, slot):
                    if not under(t, 2):
                        held(sp, scored, 8 * (t - 1), sp_turns)
                        held(sp, widened, 8 * (t - 1), sp_turns)
                        held(sp, v_turned, t - 1, sp_turns)
                    for dst, name in ((q_in, "aq"), (k_in, "ak"), (v_in, "av")):
                        sp.dma_start(dst[:, slot], scr[name][t]).then_inc(loaded[slot], 16)
                    if under(t, 1):
                        for dst, name in ((bias, "bias"), (sink, "sink"), (ident, "ident")):
                            sp.dma_start(dst[:], a[name]).then_inc(small_loaded, 16)
                    if not under(t, 2):
                        held(sp, gated, 8 * (t - 1), sp_turns)
                    sp.dma_start(gate[:, slot], scr["ag"][t]).then_inc(gate_loaded[slot], 16)
                steps(sp, body)
                sp.dma_start(outp["k_prompt"], scr["ak"][TILES - 1]).then_inc(copied, 16)
                sp.dma_start(outp["v_prompt"], scr["av"][TILES - 1]).then_inc(copied, 16)
                sp.wait_ge(copied, 32)

            @block.gpsimd
            def _(pool):
                pool.memset(keys[:], 0.0).then_inc(zeroed, 1)
                pool.wait_ge(zeroed, 1)

                def body(t, slot):
                    pool.wait_ge(loaded[slot], 24 * (t - slot) + 48)
                    for n in range(KVH):
                        if not under(t, 1):
                            pool.wait_ge(scored, 8 * (t - 1) + 2 * n + 2)
                        pool.sem_inc(pool_turns, 1)
                        for h in range(2):
                            pool.tensor_copy(keys[64 * h:64 * h + 64, n, h, slot, :],
                                             k_in[64 * (n % 2):64 * (n % 2) + 64, slot, n // 2, :]).then_inc(widened, 1)
                steps(pool, body)

            @block.tensor
            def _(pe):
                pe.wait_ge(small_loaded, 48)

                def turn_probs(b, slot, g):
                    pe.wait_ge(normed, 16 * b + 4 * g + 4)
                    if g == 0:
                        pe.wait_ge(v_kept, b + 1)
                    if not under(b, 1) or g >= 2:
                        pe.wait_ge(p_kept, 8 * b + 2 * (g - 1))
                    for s in slots(b):
                        for h in range(4):
                            mm = pe.transpose(turn[:, 2 * (g % 2) + s, 128 * h:128 * h + 128], score[:, slot, 4 * g + h, 128 * s:128 * s + 128], ident[:])
                        mm.then_inc(p_turned, 2 // len(slots(b)))

                def values(b, g):
                    pe.wait_ge(p_kept, 8 * b + 2 * g + 2)
                    if not under(b, 1) or g >= 2:
                        pe.wait_ge(gated, 8 * b + 2 * (g - 1))
                    for s in slots(b):
                        mm = pe.matmul(pv[0:64, g % 2, :], v_rows[:, s, 64 * g:64 * g + 64], prob_t[:, g % 2, s, :],
                                       start=s == 0, stop=s == len(slots(b)) - 1)
                    mm.then_inc(mixed, 1)

                def body(t, slot):
                    pe.wait_ge(loaded[slot], 24 * (t - slot) + 48)
                    for g in range(KVH):
                        if not under(t, 1):
                            turn_probs(t - 1, 1 - slot, g)
                        pe.wait_ge(widened, 8 * t + 2 * g + 2)
                        for pair in (2 * g, 2 * g + 1):
                            if not under(t, 1) or pair >= 2:
                                pe.wait_ge(biased, 16 * t + 2 * (pair - 1))
                            rhs = keys[:, g, :, 0, :] if under(t, 1) else keys[:, g]
                            pe.matmul(sc[:, pair % 2, 0:256 * len(slots(t))], q_in[:, slot, pair, :], rhs, start=True, stop=True).then_inc(scored, 1)
                        if not under(t, 1):
                            values(t - 1, g)
                    if not under(t, 1):
                        pe.wait_ge(p_kept, 8 * t)
                    for j in range(2):
                        mm = pe.transpose(turn[:, 0, 128 * j:128 * j + 128], v_in[:, slot, j, :], ident[:])
                    mm.then_inc(v_turned, 1)
                steps(pe, body)
                for g in range(KVH):
                    turn_probs(TILES - 1, 1, g)
                    values(TILES - 1, g)

            @block.scalar
            def _(act):
                def keep_probs(b, g):
                    for s in slots(b):
                        act.wait_ge(p_turned, 8 * b + 2 * g + s + 2 // len(slots(b)))
                        if not under(b, 1) or g >= 2:
                            act.wait_ge(mixed, 4 * b + g - 1)
                        act.activation(prob_t[:, g % 2, s, :], turn[:, 2 * (g % 2) + s, :], ACT.Copy).then_inc(p_kept, 2 // len(slots(b)))

                def raise_group(t, slot, g):
                    act.wait_ge(lowered, 4 * t + g + 1)
                    width = 128 * len(slots(t))
                    for h in range(4 * g, 4 * g + 4):
                        act.activation(score[:, slot, h, 0:width], score[:, slot, h, 0:width], ACT.Exp, bias=low[:, h:h + 1],
                                       accum_out=sums[:, h:h + 1]).then_inc(raised, 1)
                    act.wait_ge(sunk, 4 * t + g + 1)
                    act.activation(extra[:, 4 * g:4 * g + 4], extra[:, 4 * g:4 * g + 4], ACT.Exp).then_inc(raised, 1)

                def body(t, slot):
                    for g in range(KVH):
                        if not under(t, 1):
                            keep_probs(t - 1, g)
                        if g:
                            raise_group(t, slot, g - 1)
                    raise_group(t, slot, KVH - 1)
                    act.wait_ge(v_turned, t + 1)
                    if not under(t, 1):
                        act.wait_ge(mixed, 4 * t)
                    act.activation(v_rows[:, slot, :], turn[:, 0, 0:256], ACT.Copy).then_inc(v_kept, 1)
                steps(act, body)
                for g in range(KVH):
                    keep_probs(TILES - 1, g)

            @block.vector
            def _(dve):
                dve.wait_ge(small_loaded, 48)

                def bias_group(t, slot, g):
                    width = 128 * len(slots(t))
                    for pair in (2 * g, 2 * g + 1):
                        held(dve, scored, 8 * t + pair + 1, dve_turns)
                        for h in range(2):
                            head = 2 * pair + h
                            table = bias[:, head, 1:2] if under(t, 1) else bias[:, head, 1 - slot:3 - slot]
                            src = sc[:, pair % 2, width * h:width * h + width].rearrange("p (s n) -> p s n", n=128)
                            dve.tensor_tensor_reduce(score[:, slot, head, 0:width].rearrange("p (s n) -> p s n", n=128), src, table,
                                                     SCALE, -1e30, ALU.add, ALU.max, top[:, head:head + 1]).then_inc(biased, 1)
                    hs = slice(4 * g, 4 * g + 4)
                    dve.wait_ge(biased, 16 * t + 4 * g + 4)
                    dve.tensor_tensor(low[:, hs], top[:, hs], sink[:, hs], ALU.max).then_inc(topped, 1)
                    dve.wait_ge(topped, 4 * t + g + 1)
                    dve.tensor_scalar(low[:, hs], low[:, hs], -1.0, None, ALU.mult).then_inc(lowered, 1)
                    dve.wait_ge(lowered, 4 * t + g + 1)
                    dve.tensor_tensor(extra[:, hs], low[:, hs], sink[:, hs], ALU.add).then_inc(sunk, 1)

                def norm_group(t, slot, g):
                    hs, width = slice(4 * g, 4 * g + 4), 128 * len(slots(t))
                    dve.wait_ge(raised, 20 * t + 5 * g + 5)
                    dve.tensor_tensor(sums[:, hs], sums[:, hs], extra[:, hs], ALU.add).then_inc(totalled, 1)
                    dve.wait_ge(totalled, 4 * t + g + 1)
                    dve.reciprocal(recip[:, hs], sums[:, hs]).then_inc(inverted, 1)
                    dve.wait_ge(inverted, 4 * t + g + 1)
                    for h in range(4 * g, 4 * g + 4):
                        dve.tensor_scalar(score[:, slot, h, 0:width], score[:, slot, h, 0:width], recip[:, h:h + 1], None, ALU.mult).then_inc(normed, 1)

                def gate_group(b, slot, g):
                    if g == 0:
                        dve.wait_ge(gate_loaded[slot], 8 * (b - slot) + 16)
                    dve.wait_ge(mixed, 4 * b + g + 1)
                    for h in range(2):
                        p = slice(64 * h, 64 * h + 64)
                        src = pv[0:64, g % 2, :].rearrange("p (j h n) -> p j h n", j=2, h=2)[:, :, h, :]
                        dve.tensor_tensor(o[p, 2 * g:2 * g + 2, ds(128 * b, 128)], src, gate[p, slot, 2 * g:2 * g + 2, :], ALU.mult).then_inc(gated, 1)

                def body(t, slot):
                    if not under(t, 2):
                        dve.wait_ge(p_turned, 8 * (t - 1))
                    if not under(t, 1):
                        dve.wait_ge(normed, 16 * t)
                    for g in range(KVH):
                        bias_group(t, slot, g)
                        if g:
                            norm_group(t, slot, g - 1)
                        if not under(t, 1):
                            gate_group(t - 1, 1 - slot, g)
                    norm_group(t, slot, KVH - 1)
                steps(dve, body)
                for g in range(KVH):
                    gate_group(TILES - 1, 1, g)


def sample_attention(nc, a, scr, outp, o):
    ROWS, NEW = 128, NB * NT
    with Tensors(nc, "smp") as m:
        q_half = m.sb("q_half", 128, H, NEW)
        wide = m.sb("wide", 128, 2, NB, 128)
        k_all = m.sb("k_all", 128, NB, 2, WIN)
        k_new, v_new = m.sb("k_new", 128, 2, NEW), m.sb("v_new", 128, 2, NEW)
        v_all, v_rows = m.sb("v_all", 128, NB, 256), m.sb("v_rows", NEW, 256)
        gate = m.sb("gate", 128, DT, NEW)
        bias = m.sb("bias", 128, NB, WIN + NEW)
        score = m.sb("score", 128, NB, WIN + NEW)
        prob_t = m.sb("prob_t", 128, 2, 2, 128)
        sink, ident = m.sb("sink", 128, 1), m.sb("ident", 128, 128)
        top, low, sums, extra, recip = (m.sb(x, 128, NB) for x in ("top", "low", "sums", "extra", "recip"))
        sc, turn = m.ps("sc", 128, 2, 512), m.ps("turn", 128, 2, 512)
        pv = m.ps("pv", 128, 4, 512)
        loaded, zeroed, widened, v_turned, v_kept = (m.sem(x) for x in ("loaded", "zeroed", "widened", "v_turned", "v_kept"))
        scored, biased, vec, raised, p_turned, p_kept, mixed, gated = (m.sem(x) for x in (
            "scored", "biased", "vec", "raised", "p_turned", "p_kept", "mixed", "gated"))
        stored = m.sem("stored")

        with nc.Block() as block:
            @block.sync
            def _(sp):
                q = scr["aq"][TILES, :, :, 0:NEW]
                for half in range(2):
                    for h in range(2):
                        dst = q_half[64 * half:64 * half + 64].rearrange("p (j h) n -> p j h n", h=2)[:, :, h, :]
                        sp.dma_start(dst, q[64 * h:64 * h + 64]).then_inc(loaded, 16)
                for dst, src in ((k_new[:], scr["ak"][TILES, :, :, 0:NEW]), (v_new[:], scr["av"][TILES, :, :, 0:NEW]),
                                 (gate[:], scr["ag"][TILES, :, :, 0:NEW]), (k_all[:], a["k_cache"]), (v_all[:], a["v_cache"]),
                                 (bias[:], a["bias_sample"]), (sink[:], a["sink_sample"]), (ident[:], a["ident"])):
                    sp.dma_start(dst, src).then_inc(loaded, 16)
                sp.wait_ge(loaded, 16 * 12)
                for j in range(2):
                    sp.dma_start(outp["k_sample"][:, :, j, 0:WIN - NT], k_all[:, :, j, NT:WIN]).then_inc(stored, 16)
                    sp.dma_start(outp["k_sample"][:, :, j, WIN - NT:WIN], k_new[:, j, :].rearrange("p (b t) -> p b t", b=NB)).then_inc(stored, 16)
                sp.dma_start(outp["v_sample"][0:WIN - NT], v_all[NT:WIN]).then_inc(stored, 16)
                sp.wait_ge(v_kept, 1)
                for b in range(NB):
                    sp.dma_start(outp["v_sample"][WIN - NT:WIN, b, :], v_rows[NT * b:NT * b + NT, :]).then_inc(stored, 16)
                sp.wait_ge(stored, 16 * (5 + NB))

            @block.gpsimd
            def _(pool):
                pool.memset(wide[:], 0.0).then_inc(zeroed, 1)
                pool.wait_ge(zeroed, 1)
                pool.wait_ge(loaded, 16 * 12)
                for n in range(KVH):
                    p = slice(64 * (n % 2), 64 * (n % 2) + 64)
                    for b in range(NB):
                        pool.tensor_copy(wide[p, n // 2, b, 32 * n:32 * n + 32].rearrange("p (g t) -> p g t", g=G),
                                         q_half[p, G * n:G * n + G, NT * b:NT * b + NT]).then_inc(widened, 1)

            @block.tensor
            def _(pe):
                pe.wait_ge(loaded, 16 * 12)
                for j in range(2):
                    mm = pe.transpose(turn[0:NEW, 0, 128 * j:128 * j + 128], v_new[:, j, :], ident[:])
                mm.then_inc(v_turned, 1)
                pe.wait_ge(widened, KVH * NB)
                for b in range(NB):
                    if b >= 2:
                        pe.wait_ge(biased, b - 1)
                    for j in range(2):
                        pe.matmul(sc[:, b % 2, 0:WIN], wide[:, j, b, :], k_all[:, b, j, :], start=j == 0, stop=j == 1)
                    for j in range(2):
                        mm = pe.matmul(sc[:, b % 2, WIN:WIN + NEW], wide[:, j, b, :], k_new[:, j, :], start=j == 0, stop=j == 1)
                    mm.then_inc(scored, 1)
                pe.wait_ge(v_kept, 1)
                pe.wait_ge(vec, 5)
                for b in range(NB):
                    if b >= 2:
                        pe.wait_ge(p_kept, b - 1)
                    pe.transpose(turn[:, b % 2, 0:128], score[:, b, 0:WIN], ident[:])
                    pe.transpose(turn[0:NEW, b % 2, 128:256], score[:, b, WIN:WIN + NEW], ident[:]).then_inc(p_turned, 1)
                    pe.wait_ge(p_kept, b + 1)
                    for j in range(2):
                        out = pv[:, 2 * j + b // 4, 128 * (b % 4):128 * (b % 4) + 128]
                        pe.matmul(out, v_all[:, b, 128 * j:128 * j + 128], prob_t[:, b % 2, 0, :], start=True, stop=False)
                        mm = pe.matmul(out, v_rows[:, 128 * j:128 * j + 128], prob_t[0:NEW, b % 2, 1, :], start=False, stop=True)
                    mm.then_inc(mixed, 1)

            @block.scalar
            def _(act):
                act.wait_ge(v_turned, 1)
                act.activation(v_rows[:], turn[0:NEW, 0, 0:256], ACT.Copy).then_inc(v_kept, 1)
                act.wait_ge(vec, 2)
                for b in range(NB):
                    act.activation(score[:, b, :], score[:, b, :], ACT.Exp, bias=low[:, b:b + 1], accum_out=sums[:, b:b + 1]).then_inc(raised, 1)
                act.activation(extra[:], low[:], ACT.Exp, bias=sink[:]).then_inc(raised, 1)
                for b in range(NB):
                    act.wait_ge(p_turned, b + 1)
                    if b >= 2:
                        act.wait_ge(mixed, b - 1)
                    act.activation(prob_t[:, b % 2, 0, :], turn[:, b % 2, 0:128], ACT.Copy)
                    act.activation(prob_t[0:NEW, b % 2, 1, :], turn[0:NEW, b % 2, 128:256], ACT.Copy).then_inc(p_kept, 1)

            @block.vector
            def _(dve):
                dve.wait_ge(loaded, 16 * 12)
                for b in range(NB):
                    dve.wait_ge(scored, b + 1)
                    dve.tensor_tensor_reduce(score[:, b, :], sc[:, b % 2, 0:WIN + NEW], bias[:, b, :], SCALE, -1e30,
                                             ALU.add, ALU.max, top[:, b:b + 1]).then_inc(biased, 1)
                dve.wait_ge(biased, NB)
                dve.tensor_scalar(low[:], top[:], sink[:], None, ALU.max).then_inc(vec, 1)
                dve.wait_ge(vec, 1)
                dve.tensor_scalar(low[:], low[:], -1.0, None, ALU.mult).then_inc(vec, 1)
                dve.wait_ge(raised, NB + 1)
                dve.tensor_tensor(sums[:], sums[:], extra[:], ALU.add).then_inc(vec, 1)
                dve.wait_ge(vec, 3)
                dve.reciprocal(recip[:], sums[:]).then_inc(vec, 1)
                dve.wait_ge(vec, 4)
                scale = recip[:, :].rearrange("p (b o) -> p b o", o=1).broadcast_to([128, NB, WIN + NEW])
                dve.tensor_tensor(score[:], score[:], scale, ALU.mult).then_inc(vec, 1)
                dve.wait_ge(mixed, NB)
                for n in range(KVH):
                    for h in range(2):
                        src = pv[64 * (n % 2):64 * (n % 2) + 64, 2 * (n // 2):2 * (n // 2) + 2, :]
                        src = src.rearrange("p c (b r) -> p (c b) r", b=4)[:, :, 32 * n:32 * n + 32].rearrange("p b (i h t) -> p i h b t", i=2, h=2)[:, :, h]
                        for i in range(2):
                            p = slice(64 * h, 64 * h + 64)
                            dve.tensor_tensor(o[p, 2 * n + i, SEQ:N].rearrange("p (b t) -> p b t", b=NB), src[:, i],
                                              gate[p, 2 * n + i, :].rearrange("p (b t) -> p b t", b=NB), ALU.mult).then_inc(gated, 1)


_INS = {
    "xpad": (128, DT, XPAD), "mu": (128, 6, DT), "w0": (128, DT), "a0": (128, DT), "lora1": (128, 2, DT, 64),
    "lora2": (DT, 64, 2, 128), "w_in": (4, DT, 128, DT, 128), "k_k": (128, DT), "k_a": (128, DT), "r_k": (128, DT),
    "gn_g": (128, DT, 64), "gn_b": (128, DT, 64), "s_sample": (128, DT, NB, 64), "w_out": (DT, 128, DT, 128),
    "ln_g": (2, 128, DT), "ln_b": (2, 128, DT), "w_att": (20, 128, DT, 128), "w_att_out": (DT, 128, DT, 128),
    "sink": (128, H), "sink_sample": (128, 1), "k_cache": (128, NB, 2, WIN), "v_cache": (128, NB, 256),
}
_OUTS = {
    "y": (128, DT, N), "wkv_prompt": (128, DT, 64), "wkv_sample": (128, DT, NB, 64), "shift": (NB + 1, D),
    "k_prompt": (128, 2, 128), "v_prompt": (128, 2, 128), "k_sample": (128, NB, 2, WIN), "v_sample": (WIN, NB, 256),
}


def constants():
    r = np.arange(128)
    head, tok = r // 64, r % 64
    same = head[:, None] == head[None, :]
    before, upto = tok[:, None] < tok[None, :], tok[:, None] <= tok[None, :]
    seq = tok[:, None] // NT == tok[None, :] // NT
    gram = np.stack([np.stack([-1.0 * (same & before & part), -1.0 * (same & upto & part),
                               1.0 * (same & before & part), 1.0 * (same & upto & part)], 1) for part in (np.ones_like(seq), seq)], 1)
    c = np.arange(64)
    small = -1.0 * ((tok[:, None] // 8 == c // 8) & (tok[:, None] < c))
    levels = np.stack([(r[:, None] // (2 * b) == r // (2 * b)) & (r[:, None] // b % 2 == 0) & (r // b % 2 == 1) for b in (8, 16, 32)], 1)
    slopes = 2.0 ** (-8.0 * np.arange(1, H + 1) / H)
    dead = -1e31
    q, k = r[:, None], r[None, :]
    far, own = q - k + 128, q - k
    tables = [np.where(far < WIN, far, np.nan), np.where(own >= 0, own, np.nan)]
    bias = np.stack([np.stack([np.where(np.isnan(t), dead, -s * np.nan_to_num(t) / SCALE) for t in (tables[0], tables[1], tables[0])], 1)
                     for s in slopes], 1)
    row_t, row_head = r % NT, r // NT
    key = np.arange(WIN)
    cached = row_t[:, None] + WIN - key
    cached = np.where(cached < WIN, cached, np.nan)[:, None, :].repeat(NB, 1)
    c = np.arange(NB * NT)
    new = (row_t[:, None] - c % NT)[:, None, :].repeat(NB, 1).astype(float)
    new = np.where((c // NT == np.arange(NB)[:, None])[None] & (new >= 0), new, np.nan)
    dist = np.concatenate([cached, new], 2)
    bias_s = np.where(np.isnan(dist), dead, -slopes[row_head][:, None, None] * np.nan_to_num(dist) / SCALE)
    reset = np.ones(N)
    reset[0:SEQ:C] = 0
    reset[SEQ::NT] = 0
    return {k: np.ascontiguousarray(v, dtype=np.float32) for k, v in {
        "reset": np.broadcast_to(reset, (128, N)), "headsum": same, "headpick": head[:, None] == np.arange(2),
        "gram_mask": gram, "small_mask": small, "block_mask": r[:, None] // 8 == np.arange(16), "row_pick": r[:, None] % 8 == np.arange(8),
        "unit8": r[:, None] % 8 == np.arange(8), "level_mask": levels, "block_ones": r[:, None] // 8 == r // 8,
        "ident": np.eye(128), "seq_mask": tok[:, None] // NT == np.arange(NB), "mean_ones": np.full((128, 128), 1.0 / D),
        "bias": bias, "bias_sample": bias_s,
    }.items()}


def program(nc, a, outp):
    scr = {}
    for name, tiles in (("v", DT), ("g", DT), ("kt", DT), ("rt", DT), ("bh", DT), ("kh", DT), ("y", DT),
                        ("aq", DT), ("ak", 2), ("av", 2), ("ag", DT)):
        scr[name] = nc.dram_tensor(f"scr_{name}", (TILES + 1, 128, tiles, 128), F32, kind="Internal").ap()

    with Tensors(nc, "shift") as m:
        copied = m.sem("copied")
        with nc.Block() as block:
            @block.sync
            def _(sp):
                sp.dma_start(outp["shift"], a["x_last"]).then_inc(copied, 16)
                sp.wait_ge(copied, 16)

    with Tensors(nc, "rwkv") as m:
        keep = {"bonus": m.sb("bonus", 128, 2 * TILES + 1, DT), "ends": m.sb("ends", 128, DT, SEQ // C),
                "ends_sample": m.sb("ends_sample", 128, DT, NB)}
        mixed_projections(nc, a, scr, keep)
        delta_rule(nc, a, scr, keep, outp)

    with Tensors(nc, "both") as m:
        x = m.sb("x", 128, DT, N)
        with Tensors(nc, "one") as m1:
            rhs = m1.sb("rhs", 128, DT, N)

            def load_y(sp, sem):
                for t in range(TILES + 1):
                    n = min(128, N - 128 * t)
                    sp.dma_start(rhs[:, :, 128 * t:128 * t + n], scr["y"][t, :, :, 0:n]).then_inc(sem, 16)
            load_y.count = TILES + 1

            def load_x(sp, sem):
                sp.dma_start(x[:, :, 0:SEQ], a["xpad"][:, :, 1:1 + SEQ]).then_inc(sem, 16)
                for d in range(DT):
                    pad = a["xpad"][:, d, 1 + SEQ:].rearrange("p (b t) -> p b t", b=NB)
                    sp.dma_start(x[:, d, SEQ:N].rearrange("p (b t) -> p b t", b=NB), pad[:, :, 1:]).then_inc(sem, 16)
            load_x.count = DT + 1
            project_and_norm(nc, a, "out1", a["w_out"], a["ln_g"][0], a["ln_b"][0], rhs, load_y, x, load_x, None)
        attention_projections(nc, a, scr, x)
        with Tensors(nc, "two") as m2:
            o = m2.sb("o", 128, DT, N)
            attention(nc, a, scr, outp, o)
            sample_attention(nc, a, scr, outp, o)

            def nothing(sp, sem):
                return None
            nothing.count = 0

            def store_y(sp, part, sem):
                n0, n = PARTS[part]
                sp.dma_start(outp["y"][:, :, n0:n0 + n], x[:, :, n0:n0 + n]).then_inc(sem, 16)
            project_and_norm(nc, a, "out2", a["w_att_out"], a["ln_g"][1], a["ln_b"][1], o, nothing, x, nothing, store_y)


def laid_out(i):
    i = {k: np.asarray(v) for k, v in i.items()}

    def channels(v):
        return np.moveaxis(v.reshape(*v.shape[:-1], DT, 128), -1, 0)

    def weight_tiles(w):
        return w.reshape(DT, 128, -1, 128).transpose(2, 1, 0, 3)

    perm = np.concatenate([np.arange(64) + 64 * (4 * f + 2 * p + h) for f in range(4) for h in range(2) for p in range(2)])
    token_rows = np.concatenate([np.zeros((1, D), np.float32), i["x_prompt"][0]] + [
        r for b in range(NB) for r in (i["state_shift"][0, b][None], i["x_sample"][b])])
    w = i["rwkv_w_in"][0]
    pairs = lambda v: np.repeat(v.reshape(DT, 2, 1, 64).transpose(1, 2, 0, 3), 64, 1).reshape(128, DT, 64)
    arrays = {
        "xpad": channels(token_rows).transpose(0, 2, 1), "mu": channels(i["rwkv_mu"][0]), "w0": channels(i["rwkv_w0"][0]),
        "a0": channels(i["rwkv_a0"][0]),
        "lora1": np.stack([i["rwkv_w1"][0], i["rwkv_a1"][0]]).reshape(2, DT, 128, 64).transpose(2, 0, 1, 3),
        "lora2": np.stack([i["rwkv_w2"][0], i["rwkv_a2"][0]]).reshape(2, 64, DT, 128).transpose(2, 1, 0, 3),
        "w_in": np.stack([weight_tiles(x) for x in (w[1], w[0], w[2], w[3][:, perm])]),
        "k_k": channels(i["rwkv_k_k"][0]), "k_a": channels(i["rwkv_k_a"][0]), "r_k": channels(i["rwkv_r_k"][0].reshape(D)),
        "gn_g": pairs(i["rwkv_gn_g"][0]), "gn_b": pairs(i["rwkv_gn_b"][0]),
        "s_sample": i["state_wkv"][0].reshape(NB, DT, 2, 64, 64).transpose(2, 4, 1, 0, 3).reshape(128, DT, NB, 64),
        "w_out": weight_tiles(i["rwkv_w_out"][0][perm]), "ln_g": np.stack([channels(x) for x in i["ln_g"]]),
        "ln_b": np.stack([channels(x) for x in i["ln_b"]]), "w_att": weight_tiles(i["att_w_in"][0]),
        "w_att_out": weight_tiles(i["att_w_out"][0]), "sink": np.broadcast_to(i["att_sinks"][0], (128, H)),
        "sink_sample": np.repeat(i["att_sinks"][0], NT).reshape(128, 1),
        "k_cache": i["cache_win_k"][0].reshape(NB, WIN, 2, 128).transpose(3, 0, 2, 1),
        "v_cache": i["cache_win_v"][0].reshape(NB, WIN, 256).transpose(1, 0, 2),
    }
    arrays = {k: np.ascontiguousarray(v) for k, v in {**arrays, **constants()}.items()}
    arrays["x_last"] = np.ascontiguousarray(np.concatenate([i["x_prompt"][:, -1], i["x_sample"][:, -1]]))
    return arrays


def kernel(**inputs):
    import concourse.bacc as _bacc
    from concourse.bass_utils import run_bass_kernel_spmd as _run

    arrays = laid_out(inputs)
    nc = _bacc.Bacc("TRN2", target_bir_lowering=False, num_devices=1)
    a = {k: nc.dram_tensor(f"in_{k}", v.shape, F32, kind="ExternalInput").ap() for k, v in arrays.items()}
    outp = {k: nc.dram_tensor(f"out_{k}", shape, F32, kind="ExternalOutput").ap() for k, shape in _OUTS.items()}
    program(nc, a, outp)
    r = _run(nc, [{f"in_{k}": v for k, v in arrays.items()}], core_ids=[0]).results[0]
    got = {k: r[f"out_{k}"] for k in _OUTS}
    y = got["y"].transpose(2, 1, 0).reshape(N, D)
    window = lambda v: v.transpose(2, 1, 0).reshape(1, 1, WIN, KVH, HD)
    return (y[None, :SEQ], y[SEQ:].reshape(NB, NT, D),
            got["wkv_prompt"].reshape(2, 64, DT, 64).transpose(2, 0, 3, 1).reshape(1, 1, H, HD, HD),
            got["shift"][None, :1], window(got["k_prompt"]), window(got["v_prompt"]),
            got["wkv_sample"].reshape(2, 64, DT, NB, 64).transpose(3, 2, 0, 4, 1).reshape(1, NB, H, HD, HD),
            got["shift"][None, 1:],
            got["k_sample"].transpose(1, 3, 2, 0).reshape(1, NB, WIN, KVH, HD),
            got["v_sample"].transpose(1, 0, 2).reshape(1, NB, WIN, KVH, HD))
```

```python
from contextlib import ExitStack

import numpy as np

import concourse.bass as bass
from concourse import mybir

F32 = mybir.dt.float32
F32R = mybir.dt.float32r
ALU = mybir.AluOpType
ACT = mybir.ActivationFunctionType
AX = mybir.AxisListType.X

D = 1024
DT = D // 128
SEQ, NB, NT = 1024, 8, 8
N = SEQ + NB * NT
TILES = SEQ // 128
H, HD = 16, 64
C = 64
KVH, G = 4, 4
WIN = 128
DECAY = -float(np.exp(-0.5))
ALPHA = 4.0 ** 0.25
SCALE = HD ** -0.5
LN_EPS, GN_EPS = 1e-5, 64e-5
PARTS = ((0, 364), (364, 364), (728, 360))
XPAD = 1 + SEQ + NB * (NT + 1)


def ds(i, n):
    return bass.ds(i, n)


class Tensors:

    def __init__(self, nc, stage, group=None):
        self.nc, self.stage, self.stack, self.sems = nc, stage, ExitStack(), []
        self.group = group

    def __enter__(self):
        return self

    def __exit__(self, *e):
        if self.group is not None:
            self.group.sems += self.sems
        elif self.sems:
            self.nc.clear_and_free_semaphores(self.sems)
            self.nc.all_engine_barrier()
        self.stack.close()

    def sb(self, name, *shape, dtype=F32):
        return self.stack.enter_context(self.nc.sbuf_tensor(f"{self.stage}_{name}", list(shape), dtype))

    def ps(self, name, *shape):
        return self.stack.enter_context(self.nc.psum_tensor(f"{self.stage}_{name}", list(shape), F32))

    def sem(self, name):
        self.sems.append(self.nc.alloc_semaphore(f"{self.stage}_{name}"))
        return self.sems[-1]


def held(eng, sem, value, turns):
    eng.wait_ge(sem, value)
    eng.sem_inc(turns, 1)


def both(ap):
    return ap[:, 0:SEQ], ap[:, SEQ:N].rearrange("p (b t) -> p b t", b=NB)


def mixed_projections(nc, group, a, scr, keep, outp):
    with Tensors(nc, "mix", group) as m:
        xs_odd = m.sb("xs_odd", 128, DT, N)
        mu, w0, a0 = m.sb("mu", 128, 6, DT), m.sb("w0", 128, DT), m.sb("a0", 128, DT)
        k_k, k_a, r_k = m.sb("k_k", 128, DT), m.sb("k_a", 128, DT), m.sb("r_k", 128, DT)
        headsum, headpick = m.sb("headsum", 128, 128), m.sb("headpick", 128, 2)
        wt, out = m.sb("wt", 128, 2, DT, 128), m.sb("out", 128, 2, N)
        dots = m.sb("dots", 128, TILES + 1, H)
        with Tensors(nc, "turns") as early:
            xs_even = early.sb("xs_even", 128, DT, N)
            xpad = early.sb("xpad", 128, DT, XPAD)
            lora1, lora2 = early.sb("lora1", 128, 2, DT, 64), early.sb("lora2", 64, 2, 2, 128)
            hidden, reset = early.sb("hidden", 64, 2, N), early.sb("reset", 128, N)
            sigma, step_size = early.sb("sigma", 128, N), early.sb("step_size", 128, 2, N)
            norm, bonus = early.sb("norm", 128, N), early.sb("bonus", 128, N)
            work = early.sb("work", 128, DT, N)
            outs = work[:, 0:4]
            decay = work[:, 4:7]
            square = work[:, 7]
        xs = (xs_even, xs_odd)
        g_high, g_low = (m.sb(x, 128, DT, N, dtype=F32R) for x in ("g_high", "g_low"))
        m.sb("rest_of_xpad", 128, DT * (XPAD - N))
        v_high, v_low = (m.sb(x, 128, DT, N, dtype=F32R) for x in ("v_high", "v_low"))
        w_high, w_low = (m.sb(x, 128, 2, DT, 128, dtype=F32R) for x in ("w_high", "w_low"))
        acc = m.ps("acc", 128, 2, 3, 512)
        side = m.ps("side", 128, 2, 512)
        x_loaded = [m.sem(f"x_loaded{i}") for i in range(DT)]
        small_loaded = m.sem("small_loaded")
        w_loaded = [m.sem(f"w_loaded{i}") for i in range(2)]
        l_loaded = [m.sem(f"l_loaded{i}") for i in range(2)]
        stored = [m.sem(f"stored{i}") for i in range(2)]
        shifted, mix_made, hid_acc, hid_made = (m.sem(x) for x in ("shifted", "mix_made", "hid_acc", "hid_made"))
        acc_made, evacuated, lora_made, lora_kept = (m.sem(x) for x in ("acc_made", "evacuated", "lora_made", "lora_kept"))
        summed_up, decayed, ones_set, keyed, squared = (m.sem(x) for x in ("summed_up", "decayed", "ones_set", "keyed", "squared"))
        summed, clamped, rooted, vec, bonused = (m.sem(x) for x in ("summed", "clamped", "rooted", "vec", "bonused"))
        dotted, ends_kept, dots_kept, ops_stored = (m.sem(x) for x in ("dotted", "ends_kept", "dots_kept", "ops_stored"))
        act_turns, sp_turns, pool_turns = m.sem("act_turns"), m.sem("sp_turns"), m.sem("pool_turns")
        shift_copied = m.sem("shift_copied")
        r_rounded, r_split, w_rounded, w_split = (m.sem(x) for x in ("r_rounded", "r_split", "w_rounded", "w_split"))
        dve_turns = m.sem("dve_turns")
        VEC = 9
        MU = (4, 5, 1, 0, 2, 3)
        smalls = (("mu", mu), ("lora1", lora1), ("w0", w0), ("a0", a0), ("reset", reset), ("k_k", k_k), ("k_a", k_a), ("r_k", r_k),
                  ("headsum", headsum), ("headpick", headpick))

        def turns(eng, body, last=False):
            body(0, 0, True)
            body(1, 1, False)
            with eng.Fori(1, DT // 2 - (1 if last else 0)) as i:
                body(2 * i, 0, False)
                body(2 * i + 1, 1, False)
            if last:
                body(DT - 2, 0, False)
                body(DT - 1, 1, False)

        def pairs(eng, p, body):
            if p == 0:
                body(0, True)
            with eng.Fori(1 if p == 0 else 0, DT // 2) as i:
                body(i, False)

        def known(j):
            return isinstance(j, int)

        with nc.Block() as block:
            @block.sync
            def _(sp):
                for name, dst in smalls[0:2]:
                    sp.dma_start(dst[:], a[name]).then_inc(small_loaded, 16)
                for d in range(DT):
                    sp.dma_start(xpad[:, d, :], a["xpad"][:, d, :]).then_inc(x_loaded[d], 16)
                for name, dst in smalls[2:]:
                    sp.dma_start(dst[:], a[name]).then_inc(small_loaded, 16)

                def store_ops(j):
                    held(sp, vec, VEC * (j + 1), sp_turns)
                    for k, name in enumerate(("kt", "rt", "bh", "kh")):
                        store_tiles(sp, scr[name], j, outs[:, k], ops_stored)

                def body(j, s, first):
                    if not (known(j) and j < 2):
                        held(sp, lora_made, 6 * (j - 1), sp_turns)
                    sp.dma_start(lora2[:, s], a["lora2"][j]).then_inc(l_loaded[s], 16)
                    for k in range(2):
                        if not first:
                            held(sp, acc_made, 3 * (2 * j + k - 1), sp_turns)
                        sp.dma_start(wt[:, k], a["w_in"][k][j]).then_inc(w_loaded[k], 16)
                    if not first:
                        store_ops(j - 1)
                turns(sp, body)
                for p in range(2):
                    def job(i, first, p=p):
                        for s in range(2):
                            sp.wait_ge(acc_made, 3 * (16 + 8 * p + 2 * i + s - 1))
                            sp.dma_start(wt[:, s], a["w_in"][2 + p][2 * i + s]).then_inc(w_loaded[s], 16)
                        if first:
                            store_ops(DT - 1)
                            sp.dma_start(outp["shift"], a["x_last"]).then_inc(shift_copied, 16)
                    pairs(sp, p, job)
                sp.wait_ge(ops_stored, 128 * DT)
                sp.wait_ge(shift_copied, 16)

            @block.gpsimd
            def _(pool):
                def body(j, s, first):
                    held(pool, decayed, 3 * j + 1, pool_turns)
                    prompt, sample = both(decay[:, 1])
                    pool.memset(prompt.rearrange("p (c t) -> p c t", t=C)[:, :, 0:1], 1.0).then_inc(ones_set, 1)
                    pool.memset(sample[:, :, 0:1], 1.0).then_inc(ones_set, 1)
                turns(pool, body)

            @block.tensor
            def _(pe):
                pe.wait_ge(small_loaded, 16 * len(smalls))
                for p in range(2):
                    for d in range(DT):
                        pe.wait_ge(mix_made, 2 * (DT * p + d + 1))
                        for k, (n0, n) in enumerate(PARTS):
                            mm = pe.matmul(acc[0:64, p, k, 0:n], lora1[:, p, d, :], xs[p][:, d, n0:n0 + n], start=d == 0, stop=d == DT - 1)
                            if d == DT - 1:
                                mm.then_inc(hid_acc, 1)
                pe.wait_ge(hid_made, 6)

                def part(j_job, s, k, wait):
                    n0, n = PARTS[k]
                    if wait:
                        pe.wait_ge(evacuated, 3 * (j_job - 2) + k + 1)
                    for d in range(DT):
                        mm = pe.matmul(acc[:, s, k, 0:n], wt[:, s, d, :], xs[s][:, d, n0:n0 + n], start=d == 0, stop=d == DT - 1)
                    mm.then_inc(acc_made, 1)

                def dot_products(j):
                    pe.wait_ge(bonused, j + 1)
                    for t in range(TILES + 1):
                        n = min(128, N - 128 * t)
                        mm = pe.matmul(side[0:n, 1, 2 * t:2 * t + 2], bonus[:, 128 * t:128 * t + n], headpick[:], start=True, stop=True)
                    mm.then_inc(dotted, 1)

                def body(j, s, first):
                    pe.wait_ge(l_loaded[s], 8 * (j - s) + 16)
                    if not first:
                        pe.wait_ge(clamped, 3 * j)
                        if not (known(j) and j == 1):
                            pe.wait_ge(dots_kept, j - 1)
                    for k in range(3):
                        for turn in (2 * k, 2 * k + 1):
                            l, (n0, n) = turn // 3, PARTS[turn % 3]
                            if turn >= 2:
                                pe.wait_ge(lora_kept, 6 * j + turn - 1)
                            pe.matmul(side[:, turn % 2, 0:n], lora2[:, s, l, :], hidden[:, l, n0:n0 + n], start=True, stop=True).then_inc(lora_made, 1)
                        if k == 0:
                            if first:
                                pe.wait_ge(mix_made, 2 * DT * 3)
                            pe.wait_ge(w_loaded[0], 16 * (j + 1))
                        part(2 * j, 0, k, not first)
                    pe.wait_ge(lora_kept, 6 * j + 6)
                    if not first:
                        dot_products(j - 1)
                    if first:
                        pe.wait_ge(mix_made, 2 * DT * 4)
                    pe.wait_ge(w_loaded[1], 16 * (j + 1))
                    part(2 * j + 1, 1, 0, not first)
                    last = known(j) and j == DT - 1
                    if last:
                        part(2 * j + 1, 1, 1, True)
                        part(2 * j + 1, 1, 2, True)
                    pe.wait_ge(squared, j + 1)
                    for k, (n0, n) in enumerate(PARTS):
                        if k == 1 and not first:
                            pe.wait_ge(dots_kept, j)
                        if k == 2:
                            pe.wait_ge(clamped, 3 * j + 1)
                        pe.matmul(side[:, k % 2, 0:n], headsum[:], square[:, n0:n0 + n], start=True, stop=True).then_inc(summed, 1)
                    if not last:
                        part(2 * j + 1, 1, 1, not first)
                        part(2 * j + 1, 1, 2, not first)
                turns(pe, body, last=True)
                for p in range(2):
                    if p == 0:
                        pe.wait_ge(mix_made, 2 * DT * 5)
                    else:
                        pe.wait_ge(r_split, 2 * DT)

                    def job(i, first, p=p):
                        for s in range(2):
                            if first:
                                pe.wait_ge(w_loaded[s], 16 * (DT + 1))
                            else:
                                pe.wait_ge(w_split, 8 * p + 2 * i + s - 1)
                                pe.wait_ge(r_split, DT * (p + 1))
                            for k in range(3):
                                part_of(p, i, s, k, first)
                                if first and s == 0 and k == 1:
                                    pe.wait_ge(clamped, 3 * DT)
                                    dot_products(DT - 1)

                    def part_of(p, i, s, k, first):
                        n0, n = PARTS[k]
                        pe.wait_ge(evacuated, 3 * (16 + 8 * p + 2 * i + s - 2) + k + 1)
                        if first:
                            for d in range(DT):
                                mm = pe.matmul(acc[:, s, k, 0:n], wt[:, s, d, :], xs[0][:, d, n0:n0 + n], start=d == 0, stop=d == DT - 1)
                        else:
                            mm = three_passes(pe, acc[:, s, k, 0:n], w_high[:, s], w_low[:, s], (v_high, g_high)[p], (v_low, g_low)[p], slice(n0, n0 + n))
                        mm.then_inc(acc_made, 1)
                    pairs(pe, p, job)

            @block.scalar
            def _(act):
                act.wait_ge(small_loaded, 16 * len(smalls))
                for p in range(2):
                    for k, (n0, n) in enumerate(PARTS):
                        turn = 3 * p + k
                        act.wait_ge(hid_acc, turn + 1)
                        act.activation(hidden[:, p, n0:n0 + n], acc[0:64, p, k, 0:n], ACT.Tanh if p == 0 else ACT.Copy).then_inc(hid_made, 1)

                def body(j, s, first):
                    if not first:
                        act.wait_ge(summed_up, j)
                    if not (known(j) and j < 2):
                        act.wait_ge(vec, VEC * (j - 1))
                    for l in range(2):
                        for k, (n0, n) in enumerate(PARTS):
                            held(act, lora_made, 6 * j + 3 * l + k + 1, act_turns)
                            dst = (sigma[:, n0:n0 + n], step_size[:, s, n0:n0 + n])[l]
                            act.activation(dst, side[:, (3 * l + k) % 2, 0:n], ACT.Sigmoid, bias=(w0, a0)[l][:, ds(j, 1)]).then_inc(lora_kept, 1)
                    if not first:
                        act.wait_ge(vec, VEC * j)
                        act.wait_ge(bonused, j)
                        act.wait_ge(ones_set, 2 * j)
                    act.wait_ge(summed_up, j + 1)
                    if first:
                        act.wait_ge(mix_made, 2 * DT * 4)
                    act.activation(decay[:, 1, 1:N], decay[:, 0, 0:N - 1], ACT.Exp, scale=DECAY).then_inc(decayed, 1)
                    act.activation(decay[:, 2], decay[:, 0], ACT.Exp, scale=-DECAY).then_inc(decayed, 1)
                    act.wait_ge(decayed, 3 * j + 2)
                    act.activation(decay[:, 0], decay[:, 0], ACT.Exp, scale=DECAY).then_inc(decayed, 1)
                    for k, (n0, n) in enumerate(PARTS):
                        act.wait_ge(acc_made, 6 * j + k + 1)
                        act.activation(out[:, 0, n0:n0 + n], acc[:, 0, k, 0:n], ACT.Copy).then_inc(evacuated, 1)
                    if not first:
                        act.wait_ge(ops_stored, 128 * j)
                        act.wait_ge(summed, 3 * j)
                    held(act, evacuated, 6 * j + 3, act_turns)
                    act.activation(square, out[:, 0], ACT.Square, scale=k_k[:, ds(j, 1)]).then_inc(squared, 1)
                    act.activation(outs[:, 0], out[:, 0], ACT.Copy, scale=k_k[:, ds(j, 1)]).then_inc(keyed, 1)
                    act.wait_ge(clamped, 3 * j + 3)
                    act.activation(norm[:], norm[:], ACT.Sqrt).then_inc(rooted, 1)
                    for k, (n0, n) in enumerate(PARTS):
                        act.wait_ge(acc_made, 6 * j + 3 + k + 1)
                        act.activation(out[:, 1, n0:n0 + n], acc[:, 1, k, 0:n], ACT.Copy).then_inc(evacuated, 1)
                turns(act, body)
                act.wait_ge(vec, VEC * DT)
                act.wait_ge(bonused, DT)
                act.wait_ge(keyed, DT)
                for p, name in enumerate(("v", "g")):
                    def job(i, first, p=p, name=name):
                        for s in range(2):
                            n = 16 + 8 * p + 2 * i + s
                            if not first:
                                act.wait_ge(stored[s], 32 * (4 * p + i))
                            for k, (n0, width) in enumerate(PARTS):
                                act.wait_ge(acc_made, 3 * n + k + 1)
                                act.activation(out[:, s, n0:n0 + width], acc[:, s, k, 0:width], ACT.Silu if name == "g" else ACT.Copy).then_inc(evacuated, 1)
                            act.wait_ge(evacuated, 3 * n + 3)
                            store_tiles(act, scr[name], 2 * i + s, out[:, s], stored[s])
                    pairs(act, p, job)
                for s in range(2):
                    act.wait_ge(stored[s], 32 * DT)

            @block.vector
            def _(dve):
                dve.wait_ge(small_loaded, 32)

                def mix(p, tiles=range(DT)):
                    for d in tiles:
                        if p == 0:
                            dve.wait_ge(x_loaded[d], 16)
                        pad = xpad[:, d, 1 + SEQ:].rearrange("p (b t) -> p b t", b=NB)
                        o, x = both(xs[p % 2][:, d, :]), (xpad[:, d, 1:1 + SEQ], pad[:, :, 1:1 + NT])
                        scale = mu[:, MU[p], d:d + 1]
                        diff = both(work[:, d, :]) if p < 4 else o
                        if p == 0 or p >= 4:
                            dve.tensor_tensor(diff[0], xpad[:, d, 0:SEQ], x[0], ALU.subtract).then_inc(shifted, 1)
                            dve.tensor_tensor(diff[1], pad[:, :, 0:NT], x[1], ALU.subtract).then_inc(shifted, 1)
                        for k in range(2):
                            dve.wait_ge(shifted, 2 * DT * max(p - 3, 0) + 2 * d + k + 1)
                            dve.scalar_tensor_tensor(o[k], diff[k], scale, x[k], ALU.mult, ALU.add).then_inc(mix_made, 1)

                def split_high(src, high):
                    for d in range(DT):
                        dve.tensor_copy(high[:, d, :], src[:, d, :]).then_inc(r_rounded, 1)

                def split_low(src, low, high, before, tiles):
                    for d in tiles:
                        dve.wait_ge(r_rounded, before + d + 1)
                        dve.tensor_tensor(low[:, d, :], src[:, d, :], high[:, d, :].bitcast(F32), ALU.subtract).then_inc(r_split, 1)

                def split_weights(n, s, loaded):
                    dve.wait_ge(w_loaded[s], loaded)
                    dve.sem_inc(dve_turns, 1)
                    dve.tensor_copy(w_high[:, s], wt[:, s]).then_inc(w_rounded, 1)
                    dve.wait_ge(w_rounded, n + 1)
                    dve.tensor_tensor(w_low[:, s], wt[:, s], w_high[:, s].bitcast(F32), ALU.subtract).then_inc(w_split, 1)

                mix(0)
                mix(1)
                dve.wait_ge(hid_acc, 3)
                mix(2)
                dve.wait_ge(hid_acc, 6)
                mix(3)
                dve.wait_ge(mix_made, 2 * DT * 4)
                dve.wait_ge(small_loaded, 16 * len(smalls))

                def keep_dots(j):
                    dve.wait_ge(dotted, j + 1)
                    full = dots[:, 0:TILES, ds(2 * j, 2)]
                    dve.tensor_copy(full, side[:, 1, 0:2 * TILES].rearrange("p (t h) -> p t h", h=2))
                    dve.tensor_copy(dots[0:NB * NT, TILES:TILES + 1, ds(2 * j, 2)],
                                    side[0:NB * NT, 1, 2 * TILES:2 * TILES + 2].rearrange("p (t h) -> p t h", h=2)).then_inc(dots_kept, 1)

                def body(j, s, first):
                    k_in, r_in, a_in = out[:, 0], out[:, 1], step_size[:, s]
                    p_now, p_before, p_inverse = (decay[:, k] for k in range(3))
                    kt, rt, bh, kh = (outs[:, k] for k in range(4))
                    step = VEC * j
                    dve.wait_ge(lora_kept, 6 * j + 3)
                    if not first:
                        dve.wait_ge(vec, step)
                        dve.wait_ge(ends_kept, 2 * j)
                    dve.tensor_tensor_scan(p_now, reset[:], sigma[:], 0.0, ALU.mult, ALU.add).then_inc(summed_up, 1)
                    if not first:
                        keep_dots(j - 1)
                        dve.wait_ge(ops_stored, 128 * j)
                    dve.wait_ge(lora_kept, 6 * j + 6)
                    dve.tensor_scalar(kh, a_in, -1.0, k_a[:, ds(j, 1)], ALU.add, ALU.mult).then_inc(vec, 1)
                    dve.wait_ge(evacuated, 6 * j + 3)
                    dve.wait_ge(vec, step + 1)
                    dve.scalar_tensor_tensor(kh, kh, 1.0, k_in, ALU.add, ALU.mult).then_inc(vec, 1)
                    if known(j) and j == DT - 1:
                        dve.wait_ge(acc_made, 3 * (2 * DT - 1))
                        mix(4)
                    for k, (n0, n) in enumerate(PARTS):
                        dve.wait_ge(summed, 3 * j + k + 1)
                        dve.tensor_scalar(norm[:, n0:n0 + n], side[:, k % 2, 0:n], 1e-24, None, ALU.max).then_inc(clamped, 1)
                    dve.wait_ge(rooted, j + 1)
                    dve.reciprocal(norm[:], norm[:]).then_inc(vec, 1)
                    dve.wait_ge(keyed, j + 1)
                    dve.wait_ge(vec, step + 3)
                    dve.tensor_tensor(kt, kt, norm[:], ALU.mult).then_inc(vec, 1)
                    dve.wait_ge(vec, step + 4)
                    dve.tensor_tensor(bh, kt, a_in, ALU.mult).then_inc(vec, 1)
                    dve.wait_ge(ones_set, 2 * j + 2)
                    dve.wait_ge(vec, step + 5)
                    dve.tensor_tensor(kt, kt, p_before, ALU.mult).then_inc(vec, 1)
                    dve.wait_ge(decayed, 3 * j + 3)
                    dve.tensor_tensor(bh, bh, p_inverse, ALU.mult).then_inc(vec, 1)
                    prompt, sample = both(p_now)
                    dve.tensor_copy(keep["ends"][:, ds(j, 1), :],
                                    prompt.rearrange("p (o c t) -> p o c t", o=1, t=C)[:, :, :, C - 1]).then_inc(ends_kept, 1)
                    dve.tensor_copy(keep["ends_sample"][:, ds(j, 1), :],
                                    sample.rearrange("p (o b) t -> p o b t", o=1)[:, :, :, NT - 1]).then_inc(ends_kept, 1)
                    dve.wait_ge(evacuated, 6 * j + 6)
                    dve.scalar_tensor_tensor(bonus[:], r_in, r_k[:, ds(j, 1)], kh, ALU.mult, ALU.mult).then_inc(bonused, 1)
                    dve.tensor_tensor(rt, r_in, p_now, ALU.mult).then_inc(vec, 1)
                    dve.wait_ge(bonused, j + 1)
                    dve.tensor_tensor(kh, kh, p_inverse, ALU.mult).then_inc(vec, 1)
                turns(dve, body, last=True)
                keep_dots(DT - 1)
                dve.wait_ge(dots_kept, DT)
                chunks = keep["bonus"][:, 0:2 * TILES, :].rearrange("p (t q) j -> p t q j", q=2)
                for q in range(2):
                    for h in range(2):
                        src = dots[64 * q:64 * q + 64, 0:TILES, :].rearrange("p t (j h) -> p t j h", h=2)[:, :, :, h]
                        dve.tensor_copy(chunks[64 * h:64 * h + 64, :, q, :], src).then_inc(dots_kept, 1)
                for h in range(2):
                    src = dots[0:64, TILES:TILES + 1, :].rearrange("p t (j h) -> p t j h", h=2)[:, :, :, h]
                    dve.tensor_copy(keep["bonus"][64 * h:64 * h + 64, 2 * TILES:2 * TILES + 1, :], src).then_inc(dots_kept, 1)
                dve.wait_ge(ops_stored, 128 * DT)
                split_high(xs_even, v_high)
                split_low(xs_even, v_low, v_high, 0, range(DT))
                split_weights(0, 0, 16 * (DT + 2))
                dve.wait_ge(acc_made, 6 * DT)
                mix(5, range(DT // 2))
                split_weights(1, 1, 16 * (DT + 2))
                mix(5, range(DT // 2, DT))
                split_weights(2, 0, 16 * (DT + 3))
                dve.wait_ge(acc_made, 3 * (2 * DT + 2))
                dve.wait_ge(mix_made, 2 * DT * 6)
                split_high(xs_odd, g_high)
                split_weights(3, 1, 16 * (DT + 3))
                split_low(xs_odd, g_low, g_high, DT, range(DT // 2))
                split_weights(4, 0, 16 * (DT + 4))
                split_low(xs_odd, g_low, g_high, DT, range(DT // 2, DT))
                split_weights(5, 1, 16 * (DT + 4))
                with dve.Fori(0, DT // 2) as i:
                    for s in range(2):
                        split_weights(6 + 2 * i + s, s, 16 * (DT + 4 + i + 1))


def store_tiles(eng, dram, j, row, stored):
    tiles = dram.shape[2]
    eng.dma_start(dram[0:TILES].rearrange("t p j n -> p t j n")[:, :, j, :],
                  row[:, 0:SEQ].rearrange("p (t n) -> p t n", t=TILES)).then_inc(stored, 16)
    eng.dma_start(dram[TILES, :, j, 0:NB * NT], row[:, SEQ:N]).then_inc(stored, 16)


def delta_rule(nc, group, a, scr, keep, outp):
    with Tensors(nc, "delta", group) as m:
        ops, v_in, gate = m.sb("ops", 128, 4, DT, 128), m.sb("v_in", 128, DT, 128), m.sb("gate", 128, DT, 128)
        wide = m.sb("wide", 128, 4, 16, 128)
        grams = m.sb("grams", 128, 16, 4, 128)
        below = m.sb("below", 128, 8, 128)
        inv_t, inv = m.sb("inv_t", 128, 16, 128), m.sb("inv", 128, 8, 128)
        lm = m.sb("lm", 128, 2, 512)
        rows = m.sb("rows", 128, 2, 16, 128)
        v_rows = m.sb("v_rows", 128, 16, 64)
        small, pick = m.sb("small", 128, 8, 64), m.sb("pick", 128, 8, 64)
        coeff, solved, term = m.sb("coeff", 128, 8, 8), m.sb("solved", 128, 8, 8), m.sb("term", 128, 8, 8)
        state = m.sb("state", 128, 2, DT, 64)
        z, u = m.sb("z", 128, 2, 256), m.sb("u", 128, 2, 256)
        y, y2, y3, bonus = (m.sb(x, 128, DT, 64) for x in ("y", "y2", "y3", "bonus"))
        stat = m.sb("stat", 128, 3, DT)
        gated = m.sb("gated", 128, DT, 128)
        gram_mask = m.sb("gram_mask", 128, 2, 4, 128)
        small_mask, block_mask = m.sb("small_mask", 128, 64), m.sb("block_mask", 128, 16)
        row_pick, unit8, level_mask = m.sb("row_pick", 128, 8), m.sb("unit8", 128, 8), m.sb("level_mask", 128, 3, 128)
        block_ones, ident = m.sb("block_ones", 128, 128), m.sb("ident", 128, 128)
        gn_g, gn_b = m.sb("gn_g", 128, DT, 64), m.sb("gn_b", 128, DT, 64)
        ga, gb = m.ps("ga", 128, 512), m.ps("gb", 128, 512)
        wb = m.ps("wb", 128, 2, 512)
        mb = m.ps("mb", 128, 4, 512)
        gbank = (ga, gb)
        consts_loaded = m.sem("consts_loaded")
        v_loaded, gate_loaded = m.sem("v_loaded"), m.sem("gate_loaded")
        ops_loaded = m.sem("q_ops_loaded"), m.sem("k_ops_loaded")
        zeroed, k_zeroed, q_widened, k_widened = m.sem("zeroed"), m.sem("k_zeroed"), m.sem("q_widened"), m.sem("k_widened")
        v_turned, v_kept = m.sem("v_turned"), m.sem("v_kept")
        rows_turned, rows_kept = m.sem("rows_turned"), m.sem("rows_kept")
        gram_made, gram_kept, gram_small = m.sem("gram_made"), m.sem("gram_kept"), m.sem("gram_small")
        coeff_made, picked, spread, solving, solved_wide = (m.sem(x) for x in ("coeff_made", "picked", "spread", "solving", "solved_wide"))
        inv_turned, inv_kept = m.sem("inv_turned"), m.sem("inv_kept")
        below_made, lm_made, lm_kept, grown, grown_kept = (m.sem(x) for x in ("below_made", "lm_made", "lm_kept", "grown", "grown_kept"))
        z_made, z_kept, u_made, u_kept, s_made, s_kept = (m.sem(x) for x in ("z_made", "z_kept", "u_made", "u_kept", "s_made", "s_kept"))
        y_made, normed, y_squared, y_rooted, y_turned, y_gated = (m.sem(x) for x in ("y_made", "normed", "y_squared", "y_rooted", "y_turned", "y_gated"))
        y_stored = m.sem("y_stored")
        pe_turns, pool_turns, act_turns = m.sem("pe_turns"), m.sem("pool_turns"), m.sem("act_turns")
        NORM = 10
        ROW_BANK = (1, 3, 0, 2)
        CHUNKS = 2 * TILES

        def steps(eng, body):
            for q in range(2):
                body(0, q, q)
            with eng.Fori(1, TILES) as t:
                for q in range(2):
                    body(t, q, 2 * t + q)
            body(TILES, 0, CHUNKS)

        def below_of(c, n):
            return isinstance(c, int) and c < n

        consts = (("gram_mask", gram_mask), ("small_mask", small_mask), ("block_mask", block_mask), ("row_pick", row_pick),
                  ("unit8", unit8), ("level_mask", level_mask), ("block_ones", block_ones), ("ident", ident),
                  ("gn_g", gn_g), ("gn_b", gn_b))
        s_sample = m.sb("s_sample", 128, 4, NB, 64)
        spread8, spread_u, spread_v = m.sb("spread8", 128, NB, 64), m.sb("spread_u", 128, NB, 64), m.sb("spread_v", 128, NB, 64)
        seq_mask = m.sb("seq_mask", 128, NB)
        s_next, yr, y_own = m.sb("s_next", 128, NB, 64), m.sb("yr", 128, 64), m.sb("y_own", 128, DT, 64)
        s_loaded, s_stored = [m.sem(f"s_loaded{k}") for k in range(4)], m.sem("s_stored")
        big_made, own_z, own_u, own_u_kept, own_spread, own_y, own_s, own_yr, own_added, own_done, chained = (m.sem(x) for x in (
            "big_made", "own_z", "own_u", "own_u_kept", "own_spread", "own_y", "own_s", "own_yr", "own_added", "own_done", "chained"))

        def widen(eng, k, s, c, done, copy):
            n = slice(0, 64) if isinstance(c, int) and c == CHUNKS else slice(64 * s, 64 * s + 64)
            for h in range(2):
                p = slice(64 * h, 64 * h + 64)
                copy(wide[p, k, 8 * s:8 * s + 8, 64 * h:64 * h + 64], ops[p, k, :, n]).then_inc(done, 1)

        with nc.Block() as block:
            @block.sync
            def _(sp):
                def body(t, n, first):
                    if not first:
                        sp.wait_ge(gram_made, 8 * t)
                        sp.wait_ge(q_widened, 8 * t)
                        sp.wait_ge(k_widened, 8 * t)
                    for k, name in ((2, "bh"), (3, "kh"), (0, "kt"), (1, "rt")):
                        sp.dma_start(ops[:, k, :, 0:n], scr[name][t, :, :, 0:n]).then_inc(ops_loaded[k // 2], 16)
                    if first:
                        for name, dst in consts + (("seq_mask", seq_mask),):
                            sp.dma_start(dst[:], a[name]).then_inc(consts_loaded, 16)
                    if not first:
                        sp.wait_ge(v_turned, 4 * t)
                    sp.dma_start(v_in[:, :, 0:n], scr["v"][t, :, :, 0:n]).then_inc(v_loaded, 16)
                    if not first:
                        sp.wait_ge(y_gated, 2 * t)
                        sp.dma_start(scr["y"][t - 1], gated[:]).then_inc(y_stored, 16)
                    sp.dma_start(gate[:, :, 0:n], scr["g"][t, :, :, 0:n]).then_inc(gate_loaded, 16)
                body(0, 128, True)
                for pair in range(4):
                    sp.dma_start(s_sample[:, pair], a["s_sample"][:, pair]).then_inc(s_loaded[pair], 16)
                with sp.Fori(1, TILES) as t:
                    body(t, 128, False)
                body(TILES, 64, False)
                sp.wait_ge(s_kept, 2 * CHUNKS)
                sp.dma_start(outp["wkv_prompt"], state[:, 0]).then_inc(s_stored, 16)
                for pair in range(DT):
                    sp.wait_ge(own_done, pair + 1)
                    sp.dma_start(outp["wkv_sample"][:, pair], s_next[:]).then_inc(s_stored, 16)
                    if pair + 4 < DT:
                        sp.dma_start(s_sample[:, pair], a["s_sample"][:, pair + 4]).then_inc(s_loaded[pair], 16)
                sp.wait_ge(y_gated, CHUNKS + 1)
                sp.dma_start(scr["y"][TILES, :, :, 0:64], gated[:, :, 0:64]).then_inc(y_stored, 16)
                sp.wait_ge(y_stored, 16 * (TILES + 1))
                sp.wait_ge(s_stored, 16 * (DT + 1))

            @block.gpsimd
            def _(pool):
                pool.memset(wide[:, 0], 0.0).then_inc(zeroed, 1)
                pool.memset(state[:], 0.0).then_inc(zeroed, 1)
                pool.wait_ge(consts_loaded, 176)
                pool.wait_ge(zeroed, 2)
                pool.wait_ge(k_zeroed, 3)

                def body(t, s, c):
                    pool.wait_ge(ops_loaded[0], 32 * (t + 1))
                    if not below_of(c, 1):
                        pool.wait_ge(below_made, 3 * c)
                    if not below_of(c, 2):
                        pool.wait_ge(y_made, c - 1)
                    pool.sem_inc(pool_turns, 1)
                    for k in range(2):
                        widen(pool, k, s, c, q_widened, pool.tensor_copy)
                    pool.wait_ge(q_widened, 4 * c + 4)
                    pool.wait_ge(gram_kept, 8 * c + 8)
                    for lev in range(3):
                        pool.wait_ge(lm_made, 6 * c + 2 * lev)
                        pool.tensor_tensor(below[:], grams[:, 8 * s:8 * s + 8, 0, :],
                                           level_mask[:, lev:lev + 1, :].broadcast_to([128, 8, 128]), ALU.mult).then_inc(below_made, 1)
                steps(pool, body)

            @block.tensor
            def _(pe):
                pe.wait_ge(consts_loaded, 176)

                def inverse_begins(t, s, c):
                    pe.wait_ge(ops_loaded[0], 32 * (t + 1))
                    pe.wait_ge(k_widened, 4 * c + 4)
                    for n in range(4):
                        g, k = n // 2, n % 2
                        if n % 2 == 0 and not below_of(c, 1):
                            pe.wait_ge(grown_kept, 10 * c - 2 + n)
                        pe.sem_inc(pe_turns, 1)
                        for j in range(4):
                            mm = pe.transpose(mb[:, ROW_BANK[n], 128 * j:128 * j + 128], wide[:, 2 + k, 8 * s + 4 * g + j, :], ident[:])
                        mm.then_inc(rows_turned, 1)
                        if n >= 2:
                            pe.wait_ge(gram_kept, 8 * c + 2 * (n - 2) + 2)
                        elif n == 0 and not below_of(c, 2):
                            pe.wait_ge(normed, NORM * (c - 2) + 3)
                        elif n == 1 and not below_of(c, 3):
                            pe.wait_ge(y_gated, c - 2)
                        for j in range(2):
                            pair = 2 * n + j
                            rhs = ops[:, 0:2, pair, 64 * s:64 * s + 64]
                            for k in range(2):
                                mm = pe.matmul(gbank[n % 2][:, 256 * j + 128 * k:256 * j + 128 * k + 128],
                                               wide[:, 2 + k, 8 * s + pair, :], rhs, start=True, stop=True)
                        mm.then_inc(gram_made, 1)
                    pe.wait_ge(v_loaded, 16 * (t + 1))
                    pe.sem_inc(pe_turns, 1)
                    for g in range(2):
                        for j in range(4):
                            mm = pe.transpose(wb[0:64, g, 128 * j:128 * j + 128], v_in[:, 4 * g + j, 64 * s:64 * s + 64], ident[:])
                        mm.then_inc(v_turned, 1)
                    if not below_of(c, 1):
                        products_with_state(1 - s, c - 1, c)
                    pe.wait_ge(gram_kept, 8 * c + 8)
                    if not below_of(c, 2):
                        turn_y(c - 2)
                    pe.wait_ge(picked, c + 1)
                    pe.wait_ge(v_kept, 2 * c + 1)
                    pe.matmul(wb[:, 0, :], block_ones[:], pick[:], start=True, stop=True).then_inc(spread, 1)

                def inverse_ends(s, c):
                    pe.wait_ge(solved_wide, c + 1)
                    pe.wait_ge(rows_kept, 4 * c + 4)
                    for g in range(2):
                        for j in range(4):
                            mm = pe.transpose(mb[:, g, 128 * j:128 * j + 128], inv_t[:, 8 * s + 4 * g + j, :], ident[:])
                        mm.then_inc(inv_turned, 1)
                    if not below_of(c, 1):
                        pe.wait_ge(s_kept, 2 * c - 1)
                    for lev in range(3):
                        for g in range(2):
                            pe.wait_ge(below_made, 3 * c + lev + 1)
                            if lev == 0:
                                pe.wait_ge(inv_kept, 2 * c + g + 1)
                            else:
                                pe.wait_ge(grown_kept, 10 * c + 4 * (lev - 1) + 2 * g + 1)
                            for j in range(4):
                                mm = pe.matmul(wb[:, g, 128 * j:128 * j + 128], below[:, 4 * g + j, :], inv[:, 4 * g + j, :], start=True, stop=True)
                            mm.then_inc(lm_made, 1)
                        for g in range(2):
                            pe.wait_ge(lm_kept, 6 * c + 2 * lev + g + 1)
                            if lev == 0:
                                pe.wait_ge(inv_kept, 2 * c + 2)
                            else:
                                pe.wait_ge(grown_kept, 10 * c + 4 * (lev - 1) + 2 * g + 2)
                            if lev < 2:
                                for j in range(4):
                                    mm = pe.matmul(mb[:, 2 * g + 1, 128 * j:128 * j + 128], inv_t[:, 8 * s + 4 * g + j, :], lm[:, g, 128 * j:128 * j + 128], start=True, stop=True)
                                mm.then_inc(grown, 1)
                            for j in range(4):
                                mm = pe.matmul(mb[:, 2 * g, 128 * j:128 * j + 128], lm[:, g, 128 * j:128 * j + 128], inv_t[:, 8 * s + 4 * g + j, :], start=True, stop=True)
                            mm.then_inc(grown, 1)

                def products_with_state(s, c, now):
                    if below_of(c, 1):
                        pe.wait_ge(zeroed, 2)
                    else:
                        pe.wait_ge(s_kept, 2 * c)
                    pe.wait_ge(q_widened, 4 * c + 4)
                    for half in range(2):
                        pe.wait_ge(rows_kept, 4 * now + 4)
                        for j in range(4):
                            pair = 4 * half + j
                            unit, o = 8 * s + pair, mb[:, half, 64 * j:64 * j + 64]
                            pe.matmul(o, wide[:, 0, unit, :], state[:, s, pair, :], start=True, stop=False)
                            mm = pe.matmul(o, grams[:, unit, 2, :], v_rows[:, unit, :], start=False, stop=True)
                        mm.then_inc(z_made, 1)

                def chunk_behind(s, c, now):
                    for half in range(2):
                        pe.wait_ge(z_kept, 2 * c + half + 1)
                        for j in range(4):
                            unit = 8 * s + 4 * half + j
                            mm = pe.matmul(mb[:, 2 + half, 64 * j:64 * j + 64], inv_t[:, unit, :], z[:, half, 64 * j:64 * j + 64], start=True, stop=True)
                        mm.then_inc(u_made, 1)
                    pe.wait_ge(v_kept, 2 * now + 2)
                    for pair in range(8):
                        unit = 8 * s + pair
                        if pair % 4 == 0:
                            pe.wait_ge(u_kept, 2 * c + pair // 4 + 1)
                        o = wb[:, 1, 64 * pair:64 * pair + 64]
                        pe.matmul(o, rows[:, 0, unit, :], u[:, pair // 4, 64 * (pair % 4):64 * (pair % 4) + 64], start=True, stop=False)
                        mm = pe.matmul(o, rows[:, 1, unit, :], v_rows[:, unit, :], start=False, stop=True)
                    mm.then_inc(s_made, 1)
                    for pair in range(8):
                        unit, half, o = 8 * s + pair, pair // 4, ga[:, 64 * pair:64 * pair + 64]
                        pe.matmul(o, wide[:, 1, unit, :], state[:, s, pair, :], start=True, stop=False)
                        pe.matmul(o, grams[:, unit, 1, :], u[:, half, 64 * (pair % 4):64 * (pair % 4) + 64], start=False, stop=False)
                        mm = pe.matmul(o, grams[:, unit, 3, :], v_rows[:, unit, :], start=False, stop=True)
                    mm.then_inc(y_made, 1)

                def turn_y(c):
                    pe.wait_ge(normed, NORM * (c + 1))
                    if not below_of(c, 1):
                        pe.wait_ge(y_gated, c)
                    for j in range(4):
                        mm = pe.transpose(gb[:, 128 * j:128 * j + 128], y3[:, 2 * j:2 * j + 2, :], ident[:])
                    mm.then_inc(y_turned, 1)

                def body(t, s, c):
                    inverse_begins(t, s, c)
                    if not below_of(c, 1):
                        chunk_behind(1 - s, c - 1, c)
                    inverse_ends(s, c)
                steps(pe, body)

                turn_y(CHUNKS - 1)
                pe.wait_ge(grown_kept, 10 * CHUNKS + 10)
                pe.wait_ge(q_widened, 4 * CHUNKS + 4)

                def all_states(pair):
                    k = pair % 4
                    pe.wait_ge(s_loaded[k], 16 * (pair // 4 + 1))
                    if pair:
                        pe.wait_ge(own_yr, pair)
                    pe.matmul(mb[:, 0, :], wide[:, 0, pair, :], s_sample[:, k], start=True, stop=True)
                    pe.matmul(mb[:, 1, :], wide[:, 1, pair, :], s_sample[:, k], start=True, stop=True)
                    pe.matmul(mb[:, 2, 0:64], grams[:, pair, 2, :], v_rows[:, pair, :], start=True, stop=True).then_inc(big_made, 1)

                all_states(0)
                for pair in range(DT):
                    pe.wait_ge(own_z, pair + 1)
                    if pair:
                        pe.wait_ge(own_u_kept, pair)
                    pe.matmul(wb[:, 0, 0:64], inv_t[:, pair, :], z[:, 0, 0:64], start=True, stop=True).then_inc(own_u, 1)
                    pe.wait_ge(own_u_kept, pair + 1)
                    if pair:
                        pe.wait_ge(own_added, pair)
                    pe.matmul(mb[:, 3, 0:64], grams[:, pair, 1, :], u[:, 0, 0:64], start=True, stop=False)
                    pe.matmul(mb[:, 3, 0:64], grams[:, pair, 3, :], v_rows[:, pair, :], start=False, stop=True).then_inc(own_y, 1)
                    if pair < DT - 1:
                        all_states(pair + 1)
                    pe.wait_ge(own_spread, pair + 1)
                    pe.matmul(wb[:, 1, :], rows[:, 0, pair, :], spread_u[:], start=True, stop=False)
                    pe.matmul(wb[:, 1, :], rows[:, 1, pair, :], spread_v[:], start=False, stop=True).then_inc(own_s, 1)
                turn_y(CHUNKS)

            @block.scalar
            def _(act):
                def widen_next(t, s, c):
                    act.wait_ge(ops_loaded[1], 32 * (t + 1))
                    if not below_of(c, 2):
                        act.wait_ge(gram_made, 4 * (c - 1))
                        act.wait_ge(rows_turned, 4 * (c - 1))
                    act.sem_inc(act_turns, 1)
                    for k in (2, 3):
                        widen(act, k, s, c, k_widened, lambda dst, src: act.activation(dst, src, ACT.Copy))

                act.wait_ge(k_zeroed, 2)
                widen_next(0, 0, 0)

                def body(t, s, c):
                    if not below_of(c, 2):
                        act.wait_ge(s_made, c - 1)
                        act.wait_ge(y_made, c - 1)
                        act.wait_ge(normed, NORM * (c - 2) + 1)
                    for n in range(4):
                        g, k = n // 2, n % 2
                        act.wait_ge(rows_turned, 4 * c + n + 1)
                        act.activation(rows[:, k, 8 * s + 4 * g:8 * s + 4 * g + 4, :], mb[:, ROW_BANK[n], :].rearrange("p (j n) -> p j n", j=4),
                                       ACT.Copy, scale=-1.0 if k == 0 else 1.0).then_inc(rows_kept, 1)
                    for g in range(2):
                        act.wait_ge(v_turned, 2 * c + g + 1)
                        src = wb[0:64, g, :].rearrange("p (j n) -> p j n", j=4)
                        act.activation(v_rows[0:64, 8 * s + 4 * g:8 * s + 4 * g + 4, :], src[:, :, 0:64], ACT.Copy)
                        act.activation(v_rows[64:128, 8 * s + 4 * g:8 * s + 4 * g + 4, :], src[:, :, 64:128], ACT.Copy).then_inc(v_kept, 1)
                    behind = c - 1
                    if not below_of(c, 1):
                        for half in range(2):
                            act.wait_ge(z_made, 2 * behind + half + 1)
                            if not below_of(behind, 1):
                                act.wait_ge(u_made, 2 * behind)
                            act.activation(z[:, half], mb[:, half, 0:256], ACT.Copy).then_inc(z_kept, 1)
                        for half in range(2):
                            act.wait_ge(u_made, 2 * behind + half + 1)
                            if not below_of(behind, 1):
                                act.wait_ge(s_made, behind)
                                act.wait_ge(y_made, behind)
                            act.activation(u[:, half], mb[:, 2 + half, 0:256], ACT.Copy).then_inc(u_kept, 1)
                    for g in range(2):
                        act.wait_ge(inv_turned, 2 * c + g + 1)
                        if not below_of(c, 1):
                            act.wait_ge(lm_made, 6 * c)
                        act.activation(inv[:, 4 * g:4 * g + 4, :], mb[:, g, :].rearrange("p (j n) -> p j n", j=4), ACT.Copy).then_inc(inv_kept, 1)
                    for lev in range(3):
                        for g in range(2):
                            act.wait_ge(lm_made, 6 * c + 2 * lev + g + 1)
                            if lev:
                                act.wait_ge(grown, 10 * c + 4 * (lev - 1) + 2 * g + 2)
                            elif not below_of(c, 1):
                                act.wait_ge(grown, 10 * c)
                            act.activation(lm[:, g, :], wb[:, g, :], ACT.Copy).then_inc(lm_kept, 1)
                        if lev == 0 and not below_of(c, 1):
                            act.wait_ge(normed, NORM * behind + 3)
                            act.activation(y2[:], y[:], ACT.Square).then_inc(y_squared, 1)
                        if lev == 0 and not (isinstance(c, int) and c == CHUNKS):
                            widen_next(t + s, 1 - s, c + 1)
                        if lev == 1 and not below_of(c, 1):
                            act.wait_ge(normed, NORM * behind + 5)
                            act.activation(stat[:, 1], stat[:, 1], ACT.Sqrt).then_inc(y_rooted, 1)
                steps(act, body)
                act.wait_ge(s_made, CHUNKS)
                for pair in range(DT):
                    act.wait_ge(own_u, pair + 1)
                    if pair:
                        act.wait_ge(own_y, pair)
                        act.wait_ge(own_spread, pair)
                    act.activation(u[:, 0, 0:64], wb[:, 0, 0:64], ACT.Copy).then_inc(own_u_kept, 1)
                act.wait_ge(normed, NORM * CHUNKS + 3)
                act.activation(y2[:], y[:], ACT.Square).then_inc(y_squared, 1)
                act.wait_ge(normed, NORM * CHUNKS + 5)
                act.activation(stat[:, 1], stat[:, 1], ACT.Sqrt).then_inc(y_rooted, 1)

            @block.vector
            def _(dve):
                for k in (2, 3, 1):
                    dve.memset(wide[:, k], 0.0).then_inc(k_zeroed, 1)
                dve.wait_ge(consts_loaded, 176)

                def per(x):
                    return x[:, :].rearrange("p (j o) -> p j o", o=1).broadcast_to([128, DT, 64])

                def norm_1(s, c, y_in):
                    at = NORM * c
                    if not below_of(c, 1):
                        dve.wait_ge(normed, at)
                    by = keep["bonus"][:, ds(c, 1), :].rearrange("p o (j u) -> p (o j) u", u=1).broadcast_to([128, DT, 64])
                    dve.tensor_tensor(bonus[:], v_rows[:, 8 * s:8 * s + 8, :], by, ALU.mult).then_inc(normed, 1)
                    if y_in is None:
                        dve.wait_ge(y_made, c + 1)
                        y_in = ga[:, :].rearrange("p (j n) -> p j n", j=DT)
                    dve.tensor_reduce(stat[:, 0], y_in, AX, ALU.add).then_inc(normed, 1)
                    dve.wait_ge(normed, at + 2)
                    dve.scalar_tensor_tensor(y[:], per(stat[:, 0]), -1.0 / HD, y_in, ALU.mult, ALU.add).then_inc(normed, 1)

                def norm_2(c):
                    dve.wait_ge(y_squared, c + 1)
                    dve.tensor_reduce(stat[:, 2], y2[:], AX, ALU.add).then_inc(normed, 1)
                    dve.wait_ge(normed, NORM * c + 4)
                    dve.tensor_scalar(stat[:, 1], stat[:, 2], 1.0 / HD, GN_EPS, ALU.mult, ALU.add).then_inc(normed, 1)

                def norm_3(c):
                    dve.wait_ge(y_rooted, c + 1)
                    dve.reciprocal(stat[:, 2], stat[:, 1]).then_inc(normed, 1)
                    dve.wait_ge(normed, NORM * c + 6)
                    dve.tensor_tensor(y[:], y[:], per(stat[:, 2]), ALU.mult).then_inc(normed, 1)
                    dve.wait_ge(normed, NORM * c + 7)
                    dve.tensor_tensor(y[:], y[:], gn_g[:], ALU.mult).then_inc(normed, 1)

                def norm_4(c):
                    dve.wait_ge(normed, NORM * c + 8)
                    dve.tensor_tensor(y[:], y[:], gn_b[:], ALU.add).then_inc(normed, 1)
                    dve.wait_ge(normed, NORM * c + 9)
                    if not below_of(c, 1):
                        dve.wait_ge(y_turned, c)
                    dve.tensor_tensor(y3[:], y[:], bonus[:], ALU.add).then_inc(normed, 1)

                def gate_rows(t, s, c):
                    dve.wait_ge(y_turned, c + 1)
                    dve.wait_ge(gate_loaded, 16 * (t + 1))
                    if s == 0 and not below_of(t, 1):
                        dve.wait_ge(y_stored, 16 * t)
                    dve.tensor_tensor(gated[:, :, 64 * s:64 * s + 64], gb[:, :].rearrange("p (j n) -> p j n", j=DT),
                                      gate[:, :, 64 * s:64 * s + 64], ALU.mult).then_inc(y_gated, 1)

                def body(t, s, c):
                    kind = 1 if isinstance(c, int) and c == CHUNKS else 0
                    if not below_of(c, 2):
                        dve.wait_ge(y_made, c - 1)
                        dve.wait_ge(below_made, 3 * (c - 1))
                    if not below_of(c, 1):
                        dve.wait_ge(coeff_made, c)
                    for n in range(4):
                        dve.wait_ge(gram_made, 4 * c + n + 1)
                        two = gbank[n % 2][:, :].rearrange("p (j k n) -> p j k n", j=2, k=4)
                        dve.tensor_tensor(small[:, 2 * n:2 * n + 2, :], two[:, :, 0, :],
                                          small_mask[:, :].rearrange("p (o n) -> p o n", o=1).broadcast_to([128, 2, 64]), ALU.mult).then_inc(gram_small, 1)
                        for j in range(2):
                            src = two[:, j].rearrange("p k (o n) -> p k o n", o=1).broadcast_to([128, 4, 2, 64])
                            dve.tensor_tensor(grams[:, 8 * s + 2 * n + j].rearrange("p k (h n) -> p k h n", h=2), src,
                                              gram_mask[:, kind].rearrange("p k (h n) -> p k h n", h=2), ALU.mult).then_inc(gram_kept, 1)
                    dve.wait_ge(gram_small, 4 * c + 4)
                    dve.tensor_reduce(coeff[:], small[:].rearrange("p u (b n) -> p u n b", b=8), AX, ALU.add).then_inc(coeff_made, 1)
                    dve.wait_ge(coeff_made, c + 1)
                    src = coeff[:].rearrange("p u (o n) -> p u o n", o=1).broadcast_to([128, 8, 8, 8])
                    sel = row_pick[:, :].rearrange("p (u j n) -> p u j n", u=1, n=1).broadcast_to([128, 8, 8, 8])
                    dve.tensor_tensor(pick[:].rearrange("p u (j n) -> p u j n", j=8), src, sel, ALU.mult).then_inc(picked, 1)
                    if not below_of(c, 2):
                        gate_rows(t - 1, s, c - 2)
                    at = 15 * c
                    dve.tensor_copy(solved[:], unit8[:, :].rearrange("p (o n) -> p o n", o=1).broadcast_to([128, 8, 8])).then_inc(solving, 1)
                    dve.wait_ge(spread, c + 1)
                    blocks = wb[:, 0, :].rearrange("p (u j n) -> p u j n", u=8, j=8)
                    for j in range(7):
                        dve.wait_ge(solving, at + 2 * j + 1)
                        dve.tensor_tensor(term[:, :, 0:7 - j], solved[:, :, j:j + 1].broadcast_to([128, 8, 7 - j]), blocks[:, :, j, j + 1:8], ALU.mult).then_inc(solving, 1)
                        dve.wait_ge(solving, at + 2 * j + 2)
                        dve.tensor_tensor(solved[:, :, j + 1:8], solved[:, :, j + 1:8], term[:, :, 0:7 - j], ALU.add).then_inc(solving, 1)
                    dve.wait_ge(solving, at + 15)
                    if not below_of(c, 2):
                        dve.wait_ge(u_made, 2 * (c - 1))
                    src = solved[:].rearrange("p u (o n) -> p u o n", o=1).broadcast_to([128, 8, 16, 8])
                    sel = block_mask[:, :].rearrange("p (u b n) -> p u b n", u=1, n=1).broadcast_to([128, 8, 16, 8])
                    dve.tensor_tensor(inv_t[:, 8 * s:8 * s + 8, :].rearrange("p u (b n) -> p u b n", b=16), src, sel, ALU.mult).then_inc(solved_wide, 1)
                    behind = c - 1
                    if not below_of(c, 1):
                        new = state[:, s]
                        dve.wait_ge(s_made, behind + 1)
                        if not below_of(behind, 1):
                            dve.wait_ge(y_made, behind)
                        dve.tensor_tensor(new, state[:, 1 - s], wb[:, 1, :].rearrange("p (j n) -> p j n", j=DT), ALU.add).then_inc(s_kept, 1)
                        dve.wait_ge(s_kept, 2 * behind + 1)
                        end = keep["ends"][:, :, ds(behind, 1)].broadcast_to([128, DT, 64])
                        dve.tensor_tensor(new, new, end, ALU.mult).then_inc(s_kept, 1)
                        norm_1(1 - s, behind, None)
                    for lev in range(3):
                        each = 2 if lev < 2 else 1
                        for g in range(2):
                            for at, k in enumerate((1, 0) if lev < 2 else (0,)):
                                dve.wait_ge(grown, 10 * c + 4 * lev + each * g + at + 1)
                                dst = inv_t[:, 8 * s + 4 * g:8 * s + 4 * g + 4, :] if k == 0 else inv[:, 4 * g:4 * g + 4, :]
                                dve.tensor_tensor(dst, dst, mb[:, 2 * g + k, :].rearrange("p (j n) -> p j n", j=4), ALU.add).then_inc(grown_kept, 1)
                        if not below_of(c, 1):
                            (norm_2, norm_3, norm_4)[lev](behind)
                steps(dve, body)
                gate_rows(TILES - 1, 1, CHUNKS - 1)

                own = seq_mask[:, :].rearrange("p (b o) -> p b o", o=1).broadcast_to([128, NB, 64])
                count = [0]

                def then(ins):
                    count[0] += 1
                    ins.then_inc(chained, 1)
                    dve.wait_ge(chained, count[0])

                def own_rows(pair):
                    dve.wait_ge(big_made, pair + 1)
                    then(dve.tensor_tensor(spread8[:], mb[:, 0, :].rearrange("p (b n) -> p b n", b=NB), own, ALU.mult))
                    if pair:
                        dve.wait_ge(own_u, pair)
                    then(dve.tensor_reduce(z[:, 1, 0:64], spread8[:].rearrange("p b n -> p n b"), AX, ALU.add))
                    dve.tensor_tensor(z[:, 0, 0:64], z[:, 1, 0:64], mb[:, 2, 0:64], ALU.add).then_inc(own_z, 1)
                    then(dve.tensor_tensor(spread8[:], mb[:, 1, :].rearrange("p (b n) -> p b n", b=NB), own, ALU.mult))
                    dve.tensor_reduce(yr[:], spread8[:].rearrange("p b n -> p n b"), AX, ALU.add).then_inc(own_yr, 1)

                own_rows(0)
                for pair in range(DT):
                    if pair:
                        dve.wait_ge(own_s, pair)
                    dve.tensor_tensor(spread_v[:], v_rows[:, pair:pair + 1, :].broadcast_to([128, NB, 64]), own, ALU.mult)
                    dve.wait_ge(own_u_kept, pair + 1)
                    dve.tensor_tensor(spread_u[:], u[:, 0:1, 0:64].broadcast_to([128, NB, 64]), own, ALU.mult).then_inc(own_spread, 1)
                    dve.wait_ge(own_y, pair + 1)
                    dve.wait_ge(own_yr, pair + 1)
                    dve.tensor_tensor(y_own[:, pair, :], yr[:], mb[:, 3, 0:64], ALU.add).then_inc(own_added, 1)
                    dve.wait_ge(own_added, pair + 1)
                    if pair < DT - 1:
                        own_rows(pair + 1)
                    dve.wait_ge(own_s, pair + 1)
                    if pair:
                        dve.wait_ge(s_stored, 16 * (pair + 1))
                    then(dve.tensor_tensor(s_next[:], s_sample[:, pair % 4], wb[:, 1, :].rearrange("p (b n) -> p b n", b=NB), ALU.add))
                    end = keep["ends_sample"][:, pair, :].rearrange("p (b o) -> p b o", o=1).broadcast_to([128, NB, 64])
                    dve.tensor_tensor(s_next[:], s_next[:], end, ALU.mult).then_inc(own_done, 1)
                dve.wait_ge(chained, count[0])
                norm_1(0, CHUNKS, y_own[:])
                norm_2(CHUNKS)
                norm_3(CHUNKS)
                norm_4(CHUNKS)
                gate_rows(TILES, 0, CHUNKS)


def weights_buffer(m, name, wt):
    return {"wt": wt, "loaded": [m.sem(f"{name}_w_loaded{i}") for i in range(2)]}


def load_ahead(sp, buffer, weights, slots=(0, 1)):
    for s in slots:
        sp.dma_start(buffer["wt"][:, s], weights[s]).then_inc(buffer["loaded"][s], 16)


def three_passes(pe, out, w_high, w_low, r_high, r_low, columns):
    for d in range(DT):
        for k, (w, r) in enumerate(((w_high, r_high), (w_high, r_low), (w_low, r_high))):
            mm = pe.matmul(out, w[:, d, :], r[:, d, columns], start=d == 0 and k == 0, stop=d == DT - 1 and k == 2)
    return mm


def project_and_norm(nc, group, a, stage, weights, gain, shift, rhs, load_rhs, x, load_residual, store,
                     buffer, ahead):
    with Tensors(nc, stage, group) as m:
        wt, w_loaded = buffer["wt"], buffer["loaded"]
        w_high, w_low = (m.sb(x, 128, 2, DT, 128, dtype=F32R) for x in ("w_high", "w_low"))
        r_high, r_low = (m.sb(x, 128, DT, N, dtype=F32R) for x in ("r_high", "r_low"))
        square = rhs
        channel_sum, rstd = m.sb("channel_sum", 128, N), m.sb("rstd", 128, N)
        g, b, mean_ones = m.sb("g", 128, DT), m.sb("b", 128, DT), m.sb("mean_ones", 128, 128)
        acc = m.ps("acc", 128, 2, 3, 512)
        small_loaded, res_loaded = m.sem("small_loaded"), m.sem("res_loaded")
        rhs_loaded = [m.sem(f"rhs_loaded{k}") for k in range(3)]
        r_rounded, r_split, w_rounded, w_split, column_summed = (m.sem(x) for x in ("r_rounded", "r_split", "w_rounded", "w_split", "column_summed"))
        acc_made, added, mean_made, centred, squared, halved, var_made = (m.sem(x) for x in (
            "acc_made", "added", "mean_made", "centred", "squared", "halved", "var_made"))
        shifted, rooted, inverted, scaled, finished, stored = (m.sem(x) for x in ("shifted", "rooted", "inverted", "scaled", "finished", "stored"))
        act_turns, pool_turns = m.sem("act_turns"), m.sem("pool_turns")

        def jobs(eng, body):
            body(0, True)
            with eng.Fori(1, DT // 2) as i:
                body(i, False)

        with nc.Block() as block:
            @block.sync
            def _(sp):
                def body(i, first):
                    for s in range(2):
                        if not first:
                            sp.wait_ge(acc_made, 3 * (2 * i + s - 1))
                            sp.dma_start(wt[:, s], weights[2 * i + s]).then_inc(w_loaded[s], 16)
                        if first and s == 0:
                            load_rhs(sp, rhs_loaded)
                    if first:
                        load_residual(sp, res_loaded)
                        for dst, src in ((g, gain), (b, shift), (mean_ones, a["mean_ones"])):
                            sp.dma_start(dst[:], src).then_inc(small_loaded, 16)
                jobs(sp, body)
                if ahead is not None:
                    sp.wait_ge(acc_made, 3 * DT)
                    ahead(sp)
                if store is not None:
                    for k in range(3):
                        sp.wait_ge(finished, DT * (k + 1))
                        store(sp, k, stored)
                    sp.wait_ge(stored, 48)

            @block.tensor
            def _(pe):
                def body(i, first):
                    for s in range(2):
                        pe.wait_ge(w_split, 2 * i + s + 1)
                        for k, (n0, n) in enumerate(PARTS):
                            if first and s == 0:
                                pe.wait_ge(r_split, k + 1)
                            if not first:
                                pe.wait_ge(added, 3 * (2 * i + s - 2) + k + 1)
                            three_passes(pe, acc[:, s, k, 0:n], w_high[:, s], w_low[:, s], r_high, r_low, slice(n0, n0 + n)).then_inc(acc_made, 1)
                jobs(pe, body)
                pe.wait_ge(small_loaded, 48)
                pe.wait_ge(added, 3 * DT)
                pe.wait_ge(column_summed, DT - 1)
                for k, (n0, n) in enumerate(PARTS):
                    pe.matmul(acc[:, 0, k, 0:n], mean_ones[:], channel_sum[:, n0:n0 + n], start=True, stop=False)
                    pe.matmul(acc[:, 0, k, 0:n], mean_ones[:], x[:, DT - 1, n0:n0 + n], start=False, stop=True).then_inc(mean_made, 1)
                for k, (n0, n) in enumerate(PARTS):
                    tiles = DT if k < 2 else DT // 2
                    if k < 2:
                        pe.wait_ge(squared, k + 1)
                    else:
                        pe.wait_ge(halved, 1)
                    for d in range(tiles):
                        mm = pe.matmul(acc[:, 1, k, 0:n], mean_ones[:], square[:, d, n0:n0 + n], start=d == 0, stop=d == tiles - 1)
                    mm.then_inc(var_made, 1)

            @block.gpsimd
            def _(pool):
                pool.wait_ge(added, 3)
                pool.tensor_copy(channel_sum[:], x[:, 0, :]).then_inc(column_summed, 1)
                with pool.Fori(1, DT - 1) as j:
                    pool.wait_ge(added, 3 * j + 3)
                    pool.wait_ge(column_summed, j)
                    pool.sem_inc(pool_turns, 1)
                    pool.tensor_tensor(channel_sum[:], channel_sum[:], x[:, ds(j, 1), :].rearrange("p o n -> p (o n)"), ALU.add).then_inc(column_summed, 1)

            @block.vector
            def _(dve):
                def split_part(k):
                    at = slice(PARTS[k][0], PARTS[k][0] + PARTS[k][1])
                    dve.wait_ge(r_rounded, k + 1)
                    dve.tensor_tensor(r_low[:, :, at], rhs[:, :, at], r_high[:, :, at].bitcast(F32), ALU.subtract).then_inc(r_split, 1)

                def add(job, s):
                    for k, (n0, n) in enumerate(PARTS):
                        dve.wait_ge(acc_made, 3 * job + k + 1)
                        row = x[:, ds(job, 1), n0:n0 + n].rearrange("p o n -> p (o n)")
                        dve.scalar_tensor_tensor(row, row, ALPHA, acc[:, s, k, 0:n], ALU.mult, ALU.add).then_inc(added, 1)

                def body(i, first):
                    for s in range(2):
                        dve.wait_ge(w_rounded, 2 * i + s + 1)
                        dve.tensor_tensor(w_low[:, s], wt[:, s], w_high[:, s].bitcast(F32), ALU.subtract).then_inc(w_split, 1)
                        if first and s == 0:
                            for k in range(3):
                                split_part(k)
                        else:
                            if first and load_residual.count:
                                dve.wait_ge(res_loaded, rhs_count(load_residual))
                            add(2 * i + s - 1, 1 - s)
                jobs(dve, body)
                add(DT - 1, 1)
                dve.wait_ge(added, 3 * DT)
                def centre(k):
                    n0, n = PARTS[k]
                    dve.wait_ge(mean_made, k + 1)
                    mean = acc[:, 0, k:k + 1, 0:n].broadcast_to([128, DT, n])
                    dve.tensor_tensor(x[:, :, n0:n0 + n], x[:, :, n0:n0 + n], mean, ALU.subtract).then_inc(centred, 1)

                for k in range(3):
                    centre(k)
                n0, n = PARTS[2]
                dve.wait_ge(squared, 3)
                low, high = square[:, 0:DT // 2, n0:n0 + n], square[:, DT // 2:DT, n0:n0 + n]
                dve.tensor_tensor(low, low, high, ALU.add).then_inc(halved, 1)
                def shift(k):
                    n0, n = PARTS[k]
                    dve.wait_ge(var_made, k + 1)
                    dve.tensor_scalar(rstd[:, n0:n0 + n], acc[:, 1, k, 0:n], LN_EPS, None, ALU.add).then_inc(shifted, 1)

                shift(0)
                for k, (n0, n) in enumerate(PARTS):
                    dve.wait_ge(rooted, k + 1)
                    dve.reciprocal(rstd[:, n0:n0 + n], rstd[:, n0:n0 + n]).then_inc(inverted, 1)
                    dve.wait_ge(inverted, k + 1)
                    inv = rstd[:, n0:n0 + n].rearrange("p (o n) -> p o n", o=1).broadcast_to([128, DT, n])
                    if k < 2:
                        shift(k + 1)
                    dve.tensor_tensor(x[:, :, n0:n0 + n], x[:, :, n0:n0 + n], inv, ALU.mult).then_inc(scaled, 1)

            @block.scalar
            def _(act):
                def body(i, first):
                    for s in range(2):
                        act.wait_ge(w_loaded[s], 16 * (i + 1))
                        act.sem_inc(act_turns, 1)
                        act.activation(w_high[:, s], wt[:, s], ACT.Copy).then_inc(w_rounded, 1)
                        if first and s == 0:
                            for k, (n0, n) in enumerate(PARTS):
                                if load_rhs.count:
                                    act.wait_ge(rhs_loaded[k], 16 * load_rhs.count)
                                act.activation(r_high[:, :, n0:n0 + n], rhs[:, :, n0:n0 + n], ACT.Copy).then_inc(r_rounded, 1)
                jobs(act, body)
                act.wait_ge(small_loaded, 48)
                for k, (n0, n) in enumerate(PARTS):
                    act.wait_ge(centred, k + 1)
                    act.activation(square[:, :, n0:n0 + n], x[:, :, n0:n0 + n], ACT.Square).then_inc(squared, 1)
                for k, (n0, n) in enumerate(PARTS):
                    act.wait_ge(shifted, k + 1)
                    act.activation(rstd[:, n0:n0 + n], rstd[:, n0:n0 + n], ACT.Sqrt).then_inc(rooted, 1)
                for k, (n0, n) in enumerate(PARTS):
                    act.wait_ge(scaled, k + 1)
                    for d in range(DT):
                        act.activation(x[:, d, n0:n0 + n], x[:, d, n0:n0 + n], ACT.Identity, scale=g[:, d:d + 1], bias=b[:, d:d + 1]).then_inc(finished, 1)


def rhs_count(load):
    return 16 * load.count


def attention_projections(nc, group, a, scr, x, tables, buffer):
    with Tensors(nc, "qkvg", group) as m:
        wt, w_loaded = buffer["wt"], buffer["loaded"]
        w_high, w_low = (m.sb(x, 128, 2, DT, 128, dtype=F32R) for x in ("w_high", "w_low"))
        r_high, r_low = (m.sb(x, 128, DT, N, dtype=F32R) for x in ("r_high", "r_low"))
        out = m.sb("out", 128, 2, N)
        acc = m.ps("acc", 128, 2, 3, 512)
        stored = [m.sem(f"stored{i}") for i in range(2)]
        r_rounded, r_split, w_rounded, w_split = (m.sem(x) for x in ("r_rounded", "r_split", "w_rounded", "w_split"))
        acc_made, evacuated = m.sem("acc_made"), m.sem("evacuated")
        dve_turns = m.sem("dve_turns")
        phases = (("aq", 0, DT), ("ak", DT, 2), ("av", DT + 2, 2), ("ag", DT + 4, DT))
        JOBS = 2 * DT + 4

        def pairs(eng, p, body):
            if p == 0:
                body(0, 0, True)
            start = 1 if p == 0 else 0
            with eng.Fori(start, phases[p][2] // 2) as i:
                body(i, phases[p][1] + 2 * i, False)

        def all_pairs(eng, body):
            body(0, 0, True)
            with eng.Fori(1, JOBS // 2) as i:
                body(i, 2 * i, False)

        with nc.Block() as block:
            @block.sync
            def _(sp):
                def body(i, job, first):
                    for s in range(2):
                        if not first:
                            sp.wait_ge(acc_made, 3 * (job + s - 1))
                            sp.dma_start(wt[:, s], a["w_att"][job + s]).then_inc(w_loaded[s], 16)
                    if first:
                        for name in ("bias", "sink", "ident"):
                            sp.dma_start(tables[name][:], a[name]).then_inc(tables["loaded"], 16)
                all_pairs(sp, body)

            @block.vector
            def _(dve):
                def body(i, job, first):
                    for s in range(2):
                        dve.wait_ge(w_loaded[s], 16 * (i + 1))
                        dve.sem_inc(dve_turns, 1)
                        dve.tensor_copy(w_high[:, s], wt[:, s]).then_inc(w_rounded, 1)
                        dve.wait_ge(w_rounded, job + s + 1)
                        dve.tensor_tensor(w_low[:, s], wt[:, s], w_high[:, s].bitcast(F32), ALU.subtract).then_inc(w_split, 1)
                        for k, (n0, n) in enumerate(PARTS) if first and s == 0 else ():
                            at = slice(n0, n0 + n)
                            dve.wait_ge(r_rounded, k + 1)
                            dve.tensor_tensor(r_low[:, :, at], x[:, :, at], r_high[:, :, at].bitcast(F32), ALU.subtract).then_inc(r_split, 1)
                all_pairs(dve, body)

            @block.tensor
            def _(pe):
                def body(i, job, first):
                    for s in range(2):
                        pe.wait_ge(w_split, job + s + 1)
                        for k, (n0, n) in enumerate(PARTS):
                            if first and s == 0:
                                pe.wait_ge(r_split, k + 1)
                            if not first:
                                pe.wait_ge(evacuated, 3 * (job + s - 2) + k + 1)
                            three_passes(pe, acc[:, s, k, 0:n], w_high[:, s], w_low[:, s], r_high, r_low, slice(n0, n0 + n)).then_inc(acc_made, 1)
                all_pairs(pe, body)

            @block.scalar
            def _(act):
                for k, (n0, n) in enumerate(PARTS):
                    act.activation(r_high[:, :, n0:n0 + n], x[:, :, n0:n0 + n], ACT.Copy).then_inc(r_rounded, 1)
                for p, (name, job0, _) in enumerate(phases):
                    def body(i, job, first, name=name, job0=job0):
                        for s in range(2):
                            if not first:
                                act.wait_ge(stored[s], 32 * (job0 // 2 + i))
                            for k, (n0, n) in enumerate(PARTS):
                                act.wait_ge(acc_made, 3 * (job + s) + k + 1)
                                act.activation(out[:, s, n0:n0 + n], acc[:, s, k, 0:n], ACT.Silu if name == "ag" else ACT.Copy).then_inc(evacuated, 1)
                            act.wait_ge(evacuated, 3 * (job + s) + 3)
                            store_tiles(act, scr[name], 2 * i + s, out[:, s], stored[s])
                    pairs(act, p, body)
                for s in range(2):
                    act.wait_ge(stored[s], 32 * 10)


def attention(nc, group, a, scr, outp, o, tables, sample):
    with Tensors(nc, "att", group) as m:
        q_in, k_in = m.sb("q_in", 128, 2, DT, 128), m.sb("k_in", 128, 2, 2, 128)
        v_in, gate = m.sb("v_in", 128, 2, 2, 128), m.sb("gate", 128, 2, DT, 128)
        keys = m.sb("keys", 128, KVH, 2, 2, 128)
        v_rows = m.sb("v_rows", 128, 2, 256)
        bias, sink, ident, small_loaded = (tables[x] for x in ("bias", "sink", "ident", "loaded"))
        score = m.sb("score", 128, 2, H, 256)
        prob_t = m.sb("prob_t", 128, 2, 2, 512)
        top, low, sums, extra = (m.sb(x, 128, H) for x in ("top", "low", "sums", "extra"))
        sc = m.ps("sc", 128, 2, 512)
        turn = m.ps("turn", 128, 4, 512)
        pv = m.ps("pv", 128, 2, 512)
        zeroed = m.sem("zeroed")
        loaded = [m.sem(f"loaded{i}") for i in range(2)]
        gate_loaded = [m.sem(f"gate_loaded{i}") for i in range(2)]
        v_turned, v_kept, widened = m.sem("v_turned"), m.sem("v_kept"), m.sem("widened")
        scored, biased, topped, lowered, sunk = (m.sem(x) for x in ("scored", "biased", "topped", "lowered", "sunk"))
        raised, totalled, inverted, normed = (m.sem(x) for x in ("raised", "totalled", "inverted", "normed"))
        p_turned, p_kept, mixed, gated = (m.sem(x) for x in ("p_turned", "p_kept", "mixed", "gated"))
        copied = m.sem("copied")
        dve_turns, pool_turns, sp_turns = m.sem("dve_turns"), m.sem("pool_turns"), m.sem("sp_turns")

        def steps(eng, body):
            body(0, 0)
            body(1, 1)
            with eng.Fori(1, TILES // 2) as i:
                body(2 * i, 0)
                body(2 * i + 1, 1)

        def under(t, n):
            return isinstance(t, int) and t < n

        def slots(t):
            return (0,) if under(t, 1) else (0, 1)

        with nc.Block() as block:
            @block.sync
            def _(sp):
                def body(t, slot):
                    if not under(t, 2):
                        held(sp, scored, 8 * (t - 1), sp_turns)
                        held(sp, widened, 8 * (t - 1), sp_turns)
                        held(sp, v_turned, t - 1, sp_turns)
                    for dst, name in ((q_in, "aq"), (k_in, "ak"), (v_in, "av")):
                        sp.dma_start(dst[:, slot], scr[name][t]).then_inc(loaded[slot], 16)
                    if not under(t, 2):
                        held(sp, gated, 8 * (t - 1), sp_turns)
                    sp.dma_start(gate[:, slot], scr["ag"][t]).then_inc(gate_loaded[slot], 16)
                steps(sp, body)
                load_sample(sp, a, scr, sample)
                sp.dma_start(outp["k_prompt"], scr["ak"][TILES - 1]).then_inc(copied, 16)
                sp.dma_start(outp["v_prompt"], scr["av"][TILES - 1]).then_inc(copied, 16)
                sp.wait_ge(copied, 32)

            @block.gpsimd
            def _(pool):
                pool.memset(keys[:], 0.0).then_inc(zeroed, 1)
                pool.wait_ge(zeroed, 1)

                def body(t, slot):
                    pool.wait_ge(loaded[slot], 24 * (t - slot) + 48)
                    for n in range(KVH):
                        if not under(t, 1):
                            pool.wait_ge(scored, 8 * (t - 1) + 2 * n + 2)
                        pool.sem_inc(pool_turns, 1)
                        for h in range(2):
                            pool.tensor_copy(keys[64 * h:64 * h + 64, n, h, slot, :],
                                             k_in[64 * (n % 2):64 * (n % 2) + 64, slot, n // 2, :]).then_inc(widened, 1)
                steps(pool, body)
                pool.wait_ge(widened, 8 * TILES)
                widen_sample(pool, sample)

            @block.tensor
            def _(pe):
                pe.wait_ge(small_loaded, 48)

                def turn_probs(b, slot, g):
                    pe.wait_ge(normed, 16 * b + 4 * g + 4)
                    if g == 0:
                        pe.wait_ge(v_kept, b + 1)
                    if not under(b, 1) or g >= 2:
                        pe.wait_ge(p_kept, 8 * b + 2 * (g - 1))
                    for s in slots(b):
                        for h in range(4):
                            mm = pe.transpose(turn[:, 2 * (g % 2) + s, 128 * h:128 * h + 128], score[:, slot, 4 * g + h, 128 * s:128 * s + 128], ident[:])
                        mm.then_inc(p_turned, 2 // len(slots(b)))

                def values(b, g):
                    pe.wait_ge(p_kept, 8 * b + 2 * g + 2)
                    if not under(b, 1) or g >= 2:
                        pe.wait_ge(gated, 8 * b + 2 * (g - 1))
                    for s in slots(b):
                        mm = pe.matmul(pv[0:64, g % 2, :], v_rows[:, s, 64 * g:64 * g + 64], prob_t[:, g % 2, s, :],
                                       start=s == 0, stop=s == len(slots(b)) - 1)
                    mm.then_inc(mixed, 1)

                def body(t, slot):
                    pe.wait_ge(loaded[slot], 24 * (t - slot) + 48)
                    for g in range(KVH):
                        if not under(t, 1):
                            turn_probs(t - 1, 1 - slot, g)
                        pe.wait_ge(widened, 8 * t + 2 * g + 2)
                        for pair in (2 * g, 2 * g + 1):
                            if not under(t, 1) or pair >= 2:
                                pe.wait_ge(biased, 16 * t + 2 * (pair - 1))
                            rhs = keys[:, g, :, 0, :] if under(t, 1) else keys[:, g]
                            pe.matmul(sc[:, pair % 2, 0:256 * len(slots(t))], q_in[:, slot, pair, :], rhs, start=True, stop=True).then_inc(scored, 1)
                        if not under(t, 1):
                            values(t - 1, g)
                    if not under(t, 1):
                        pe.wait_ge(p_kept, 8 * t - 2)
                    for j in range(2):
                        mm = pe.transpose(turn[:, 0, 128 * j:128 * j + 128], v_in[:, slot, j, :], ident[:])
                    mm.then_inc(v_turned, 1)
                steps(pe, body)
                turn_probs(TILES - 1, 1, 0)
                for g in range(KVH):
                    if g + 1 < KVH:
                        turn_probs(TILES - 1, 1, g + 1)
                    values(TILES - 1, g)

            @block.scalar
            def _(act):
                def keep_probs(b, g):
                    for s in slots(b):
                        act.wait_ge(p_turned, 8 * b + 2 * g + s + 2 // len(slots(b)))
                        if not under(b, 1) or g >= 2:
                            act.wait_ge(mixed, 4 * b + g - 1)
                        act.activation(prob_t[:, g % 2, s, :], turn[:, 2 * (g % 2) + s, :], ACT.Copy).then_inc(p_kept, 2 // len(slots(b)))

                def raise_group(t, slot, g):
                    act.wait_ge(lowered, 4 * t + g + 1)
                    width = 128 * len(slots(t))
                    for h in range(4 * g, 4 * g + 4):
                        act.activation(score[:, slot, h, 0:width], score[:, slot, h, 0:width], ACT.Exp, bias=low[:, h:h + 1],
                                       accum_out=sums[:, h:h + 1]).then_inc(raised, 1)
                    act.wait_ge(sunk, 4 * t + g + 1)
                    act.activation(extra[:, 4 * g:4 * g + 4], extra[:, 4 * g:4 * g + 4], ACT.Exp).then_inc(raised, 1)

                def body(t, slot):
                    for g in range(KVH):
                        if not under(t, 1):
                            keep_probs(t - 1, g)
                        if g:
                            raise_group(t, slot, g - 1)
                    act.wait_ge(v_turned, t + 1)
                    if not under(t, 1):
                        act.wait_ge(mixed, 4 * t)
                    act.activation(v_rows[:, slot, :], turn[:, 0, 0:256], ACT.Copy).then_inc(v_kept, 1)
                    raise_group(t, slot, KVH - 1)
                steps(act, body)
                for g in range(KVH):
                    keep_probs(TILES - 1, g)

            @block.vector
            def _(dve):
                dve.wait_ge(small_loaded, 48)

                def bias_group(t, slot, g):
                    width = 128 * len(slots(t))
                    for pair in (2 * g, 2 * g + 1):
                        held(dve, scored, 8 * t + pair + 1, dve_turns)
                        for h in range(2):
                            head = 2 * pair + h
                            table = bias[:, head, 1:2] if under(t, 1) else bias[:, head, 1 - slot:3 - slot]
                            src = sc[:, pair % 2, width * h:width * h + width].rearrange("p (s n) -> p s n", n=128)
                            dve.tensor_tensor_reduce(score[:, slot, head, 0:width].rearrange("p (s n) -> p s n", n=128), src, table,
                                                     SCALE, -1e30, ALU.add, ALU.max, top[:, head:head + 1]).then_inc(biased, 1)
                    hs = slice(4 * g, 4 * g + 4)
                    dve.wait_ge(biased, 16 * t + 4 * g + 4)
                    dve.tensor_tensor(low[:, hs], top[:, hs], sink[:, hs], ALU.max).then_inc(topped, 1)
                    dve.wait_ge(topped, 4 * t + g + 1)
                    dve.tensor_scalar(low[:, hs], low[:, hs], -1.0, None, ALU.mult).then_inc(lowered, 1)
                    dve.wait_ge(lowered, 4 * t + g + 1)
                    dve.tensor_tensor(extra[:, hs], low[:, hs], sink[:, hs], ALU.add).then_inc(sunk, 1)

                def norm_group(t, slot, g):
                    hs, width = slice(4 * g, 4 * g + 4), 128 * len(slots(t))
                    dve.wait_ge(raised, 20 * t + 5 * g + 5)
                    dve.tensor_tensor(sums[:, hs], sums[:, hs], extra[:, hs], ALU.add).then_inc(totalled, 1)
                    dve.wait_ge(totalled, 4 * t + g + 1)
                    dve.reciprocal(sums[:, hs], sums[:, hs]).then_inc(inverted, 1)
                    dve.wait_ge(inverted, 4 * t + g + 1)
                    for h in range(4 * g, 4 * g + 4):
                        dve.tensor_scalar(score[:, slot, h, 0:width], score[:, slot, h, 0:width], sums[:, h:h + 1], None, ALU.mult).then_inc(normed, 1)

                def gate_group(b, slot, g):
                    if g == 0:
                        dve.wait_ge(gate_loaded[slot], 8 * (b - slot) + 16)
                    dve.wait_ge(mixed, 4 * b + g + 1)
                    for h in range(2):
                        p = slice(64 * h, 64 * h + 64)
                        src = pv[0:64, g % 2, :].rearrange("p (j h n) -> p j h n", j=2, h=2)[:, :, h, :]
                        dve.tensor_tensor(o[p, 2 * g:2 * g + 2, ds(128 * b, 128)], src, gate[p, slot, 2 * g:2 * g + 2, :], ALU.mult).then_inc(gated, 1)

                def body(t, slot):
                    if not under(t, 2):
                        dve.wait_ge(p_turned, 8 * (t - 1))
                    if not under(t, 1):
                        dve.wait_ge(normed, 16 * t)
                    for g in range(KVH):
                        bias_group(t, slot, g)
                        if g:
                            norm_group(t, slot, g - 1)
                        if not under(t, 1):
                            gate_group(t - 1, 1 - slot, g)
                    norm_group(t, slot, KVH - 1)
                steps(dve, body)
                for g in range(KVH):
                    gate_group(TILES - 1, 1, g)


NEW = NB * NT


def sample_buffers(m):
    t = {
        "q_half": m.sb("q_half", 128, H, NEW),
        "wide": m.sb("wide", 128, 2, NB, 128),
        "k_all": m.sb("k_all", 128, NB, 2, WIN), "k_new": m.sb("k_new", 128, 2, NEW), "v_new": m.sb("v_new", 128, 2, NEW),
        "v_all": m.sb("v_all", 128, NB, 256), "gate": m.sb("gate", 128, DT, NEW), "bias": m.sb("bias", 128, NB, WIN + NEW),
        "sink": m.sb("sink", 128, 1),
    }
    return {**t, **{name: m.sem(f"sample_{name}") for name in ("loaded", "zeroed", "widened")}}


SAMPLE_LOADS = 11


def load_sample(sp, a, scr, t):
    q = scr["aq"][TILES, :, :, 0:NEW]
    for half in range(2):
        for h in range(2):
            dst = t["q_half"][64 * half:64 * half + 64].rearrange("p (j h) n -> p j h n", h=2)[:, :, h, :]
            sp.dma_start(dst, q[64 * h:64 * h + 64]).then_inc(t["loaded"], 16)
    for name, src in (("k_new", scr["ak"][TILES, :, :, 0:NEW]), ("v_new", scr["av"][TILES, :, :, 0:NEW]),
                      ("gate", scr["ag"][TILES, :, :, 0:NEW]), ("k_all", a["k_cache"]), ("v_all", a["v_cache"]),
                      ("bias", a["bias_sample"]), ("sink", a["sink_sample"])):
        sp.dma_start(t[name][:], src).then_inc(t["loaded"], 16)


def widen_sample(pool, t):
    pool.memset(t["wide"][:], 0.0).then_inc(t["zeroed"], 1)
    pool.wait_ge(t["zeroed"], 1)
    pool.wait_ge(t["loaded"], 16 * SAMPLE_LOADS)
    for n in range(KVH):
        p = slice(64 * (n % 2), 64 * (n % 2) + 64)
        for b in range(NB):
            pool.tensor_copy(t["wide"][p, n // 2, b, 32 * n:32 * n + 32].rearrange("p (g t) -> p g t", g=G),
                             t["q_half"][p, G * n:G * n + G, NT * b:NT * b + NT]).then_inc(t["widened"], 1)


def sample_attention(nc, group, a, scr, outp, o, tables, t, ahead):
    wide, k_all, k_new, v_new, v_all, gate, bias, sink, loaded, widened = (t[x] for x in (
        "wide", "k_all", "k_new", "v_new", "v_all", "gate", "bias", "sink", "loaded", "widened"))
    with Tensors(nc, "smp", group) as m:
        v_rows = m.sb("v_rows", NEW, 256)
        score = m.sb("score", 128, NB, WIN + NEW)
        prob_t = m.sb("prob_t", 128, 2, 2, 128)
        ident, ident_loaded = tables["ident"], tables["loaded"]
        top, low, sums, extra, recip = (m.sb(x, 128, NB) for x in ("top", "low", "sums", "extra", "recip"))
        sc, turn = m.ps("sc", 128, 2, 512), m.ps("turn", 128, 2, 512)
        pv = m.ps("pv", 128, 4, 512)
        v_turned, v_kept = m.sem("v_turned"), m.sem("v_kept")
        scored, biased, vec, raised, p_turned, p_kept, mixed, gated = (m.sem(x) for x in (
            "scored", "biased", "vec", "raised", "p_turned", "p_kept", "mixed", "gated"))
        stored = m.sem("stored")

        with nc.Block() as block:
            @block.sync
            def _(sp):
                ahead(sp)
                sp.wait_ge(loaded, 16 * SAMPLE_LOADS)
                for j in range(2):
                    sp.dma_start(outp["k_sample"][:, :, j, 0:WIN - NT], k_all[:, :, j, NT:WIN]).then_inc(stored, 16)
                    sp.dma_start(outp["k_sample"][:, :, j, WIN - NT:WIN], k_new[:, j, :].rearrange("p (b t) -> p b t", b=NB)).then_inc(stored, 16)
                sp.dma_start(outp["v_sample"][0:WIN - NT], v_all[NT:WIN]).then_inc(stored, 16)
                sp.wait_ge(v_kept, 1)
                for b in range(NB):
                    sp.dma_start(outp["v_sample"][WIN - NT:WIN, b, :], v_rows[NT * b:NT * b + NT, :]).then_inc(stored, 16)
                sp.wait_ge(stored, 16 * (5 + NB))

            @block.tensor
            def _(pe):
                pe.wait_ge(loaded, 16 * SAMPLE_LOADS)
                pe.wait_ge(ident_loaded, 48)
                for j in range(2):
                    mm = pe.transpose(turn[0:NEW, 0, 128 * j:128 * j + 128], v_new[:, j, :], ident[:])
                mm.then_inc(v_turned, 1)
                pe.wait_ge(widened, KVH * NB)
                for b in range(NB):
                    if b >= 2:
                        pe.wait_ge(biased, b - 1)
                    for j in range(2):
                        pe.matmul(sc[:, b % 2, 0:WIN], wide[:, j, b, :], k_all[:, b, j, :], start=j == 0, stop=j == 1)
                    for j in range(2):
                        mm = pe.matmul(sc[:, b % 2, WIN:WIN + NEW], wide[:, j, b, :], k_new[:, j, :], start=j == 0, stop=j == 1)
                    mm.then_inc(scored, 1)
                pe.wait_ge(v_kept, 1)
                pe.wait_ge(vec, 5)

                def turn_probs(b):
                    if b >= 2:
                        pe.wait_ge(p_kept, b - 1)
                    pe.transpose(turn[:, b % 2, 0:128], score[:, b, 0:WIN], ident[:])
                    pe.transpose(turn[0:NEW, b % 2, 128:256], score[:, b, WIN:WIN + NEW], ident[:]).then_inc(p_turned, 1)

                turn_probs(0)
                for b in range(NB):
                    if b + 1 < NB:
                        turn_probs(b + 1)
                    pe.wait_ge(p_kept, b + 1)
                    for j in range(2):
                        out = pv[:, 2 * j + b // 4, 128 * (b % 4):128 * (b % 4) + 128]
                        pe.matmul(out, v_all[:, b, 128 * j:128 * j + 128], prob_t[:, b % 2, 0, :], start=True, stop=False)
                        mm = pe.matmul(out, v_rows[:, 128 * j:128 * j + 128], prob_t[0:NEW, b % 2, 1, :], start=False, stop=True)
                    mm.then_inc(mixed, 1)

            @block.scalar
            def _(act):
                act.wait_ge(v_turned, 1)
                act.activation(v_rows[:], turn[0:NEW, 0, 0:256], ACT.Copy).then_inc(v_kept, 1)
                act.wait_ge(vec, 2)
                for b in range(NB):
                    act.activation(score[:, b, :], score[:, b, :], ACT.Exp, bias=low[:, b:b + 1], accum_out=sums[:, b:b + 1]).then_inc(raised, 1)
                act.activation(extra[:], low[:], ACT.Exp, bias=sink[:]).then_inc(raised, 1)
                for b in range(NB):
                    act.wait_ge(p_turned, b + 1)
                    if b >= 2:
                        act.wait_ge(mixed, b - 1)
                    act.activation(prob_t[:, b % 2, 0, :], turn[:, b % 2, 0:128], ACT.Copy)
                    act.activation(prob_t[0:NEW, b % 2, 1, :], turn[0:NEW, b % 2, 128:256], ACT.Copy).then_inc(p_kept, 1)

            @block.vector
            def _(dve):
                dve.wait_ge(loaded, 16 * SAMPLE_LOADS)
                for b in range(NB):
                    dve.wait_ge(scored, b + 1)
                    dve.tensor_tensor_reduce(score[:, b, :], sc[:, b % 2, 0:WIN + NEW], bias[:, b, :], SCALE, -1e30,
                                             ALU.add, ALU.max, top[:, b:b + 1]).then_inc(biased, 1)
                dve.wait_ge(biased, NB)
                dve.tensor_scalar(low[:], top[:], sink[:], None, ALU.max).then_inc(vec, 1)
                dve.wait_ge(vec, 1)
                dve.tensor_scalar(low[:], low[:], -1.0, None, ALU.mult).then_inc(vec, 1)
                dve.wait_ge(raised, NB + 1)
                dve.tensor_tensor(sums[:], sums[:], extra[:], ALU.add).then_inc(vec, 1)
                dve.wait_ge(vec, 3)
                dve.reciprocal(recip[:], sums[:]).then_inc(vec, 1)
                dve.wait_ge(vec, 4)
                scale = recip[:, :].rearrange("p (b o) -> p b o", o=1).broadcast_to([128, NB, WIN + NEW])
                dve.tensor_tensor(score[:], score[:], scale, ALU.mult).then_inc(vec, 1)
                dve.wait_ge(mixed, NB)
                for n in range(KVH):
                    for h in range(2):
                        src = pv[64 * (n % 2):64 * (n % 2) + 64, 2 * (n // 2):2 * (n // 2) + 2, :]
                        src = src.rearrange("p c (b r) -> p (c b) r", b=4)[:, :, 32 * n:32 * n + 32].rearrange("p b (i h t) -> p i h b t", i=2, h=2)[:, :, h]
                        for i in range(2):
                            p = slice(64 * h, 64 * h + 64)
                            dve.tensor_tensor(o[p, 2 * n + i, SEQ:N].rearrange("p (b t) -> p b t", b=NB), src[:, i],
                                              gate[p, 2 * n + i, :].rearrange("p (b t) -> p b t", b=NB), ALU.mult).then_inc(gated, 1)


_INS = {
    "xpad": (128, DT, XPAD), "mu": (128, 6, DT), "w0": (128, DT), "a0": (128, DT), "lora1": (128, 2, DT, 64),
    "lora2": (DT, 64, 2, 128), "w_in": (4, DT, 128, DT, 128), "k_k": (128, DT), "k_a": (128, DT), "r_k": (128, DT),
    "gn_g": (128, DT, 64), "gn_b": (128, DT, 64), "s_sample": (128, DT, NB, 64), "w_out": (DT, 128, DT, 128),
    "ln_g": (2, 128, DT), "ln_b": (2, 128, DT), "w_att": (20, 128, DT, 128), "w_att_out": (DT, 128, DT, 128),
    "sink": (128, H), "sink_sample": (128, 1), "k_cache": (128, NB, 2, WIN), "v_cache": (128, NB, 256),
}
_OUTS = {
    "y": (128, DT, N), "wkv_prompt": (128, DT, 64), "wkv_sample": (128, DT, NB, 64), "shift": (NB + 1, D),
    "k_prompt": (128, 2, 128), "v_prompt": (128, 2, 128), "k_sample": (128, NB, 2, WIN), "v_sample": (WIN, NB, 256),
}


def constants():
    r = np.arange(128)
    head, tok = r // 64, r % 64
    same = head[:, None] == head[None, :]
    before, upto = tok[:, None] < tok[None, :], tok[:, None] <= tok[None, :]
    seq = tok[:, None] // NT == tok[None, :] // NT
    gram = np.stack([np.stack([-1.0 * (same & before & part), -1.0 * (same & upto & part),
                               1.0 * (same & before & part), 1.0 * (same & upto & part)], 1) for part in (np.ones_like(seq), seq)], 1)
    c = np.arange(64)
    small = -1.0 * ((tok[:, None] // 8 == c // 8) & (tok[:, None] < c))
    levels = np.stack([(r[:, None] // (2 * b) == r // (2 * b)) & (r[:, None] // b % 2 == 0) & (r // b % 2 == 1) for b in (8, 16, 32)], 1)
    slopes = 2.0 ** (-8.0 * np.arange(1, H + 1) / H)
    dead = -1e31
    q, k = r[:, None], r[None, :]
    far, own = q - k + 128, q - k
    tables = [np.where(far < WIN, far, np.nan), np.where(own >= 0, own, np.nan)]
    bias = np.stack([np.stack([np.where(np.isnan(t), dead, -s * np.nan_to_num(t) / SCALE) for t in (tables[0], tables[1], tables[0])], 1)
                     for s in slopes], 1)
    row_t, row_head = r % NT, r // NT
    key = np.arange(WIN)
    cached = row_t[:, None] + WIN - key
    cached = np.where(cached < WIN, cached, np.nan)[:, None, :].repeat(NB, 1)
    c = np.arange(NB * NT)
    new = (row_t[:, None] - c % NT)[:, None, :].repeat(NB, 1).astype(float)
    new = np.where((c // NT == np.arange(NB)[:, None])[None] & (new >= 0), new, np.nan)
    dist = np.concatenate([cached, new], 2)
    bias_s = np.where(np.isnan(dist), dead, -slopes[row_head][:, None, None] * np.nan_to_num(dist) / SCALE)
    reset = np.ones(N)
    reset[0:SEQ:C] = 0
    reset[SEQ::NT] = 0
    return {k: np.ascontiguousarray(v, dtype=np.float32) for k, v in {
        "reset": np.broadcast_to(reset, (128, N)), "headsum": same, "headpick": head[:, None] == np.arange(2),
        "gram_mask": gram, "small_mask": small, "block_mask": r[:, None] // 8 == np.arange(16), "row_pick": r[:, None] % 8 == np.arange(8),
        "unit8": r[:, None] % 8 == np.arange(8), "level_mask": levels, "block_ones": r[:, None] // 8 == r // 8,
        "ident": np.eye(128), "seq_mask": tok[:, None] // NT == np.arange(NB), "mean_ones": np.full((128, 128), 1.0 / D),
        "bias": bias, "bias_sample": bias_s,
    }.items()}


def program(nc, a, outp):
    scr = {}
    for name, tiles in (("v", DT), ("g", DT), ("kt", DT), ("rt", DT), ("bh", DT), ("kh", DT), ("y", DT),
                        ("aq", DT), ("ak", 2), ("av", 2), ("ag", DT)):
        scr[name] = nc.dram_tensor(f"scr_{name}", (TILES + 1, 128, tiles, 128), F32, kind="Internal").ap()

    with Tensors(nc, "rwkv") as m:
        keep = {"bonus": m.sb("bonus", 128, 2 * TILES + 1, DT), "ends": m.sb("ends", 128, DT, SEQ // C),
                "ends_sample": m.sb("ends_sample", 128, DT, NB)}
        mixed_projections(nc, m, a, scr, keep, outp)
        delta_rule(nc, m, a, scr, keep, outp)

    with Tensors(nc, "both") as m:
        x = m.sb("x", 128, DT, N)
        wt = m.sb("wt", 128, 2, DT, 128)
        buffers = [weights_buffer(m, name, wt) for name in ("out1", "qkvg", "out2")]
        with Tensors(nc, "one", m) as m1:
            rhs = m1.sb("rhs", 128, DT, N)

            def load_y(sp, sem):
                load_ahead(sp, buffers[0], a["w_out"], (0,))
                for t in range(TILES + 1):
                    if t == 3:
                        load_ahead(sp, buffers[0], a["w_out"], (1,))
                    n = min(128, N - 128 * t)
                    sp.dma_start(rhs[:, :, 128 * t:128 * t + n], scr["y"][t, :, :, 0:n]).then_inc(sem[t // 3], 16)
            load_y.count = 3

            def load_x(sp, sem):
                sp.dma_start(x[:, :, 0:SEQ], a["xpad"][:, :, 1:1 + SEQ]).then_inc(sem, 16)
                for d in range(DT):
                    pad = a["xpad"][:, d, 1 + SEQ:].rearrange("p (b t) -> p b t", b=NB)
                    sp.dma_start(x[:, d, SEQ:N].rearrange("p (b t) -> p b t", b=NB), pad[:, :, 1:]).then_inc(sem, 16)
            load_x.count = DT + 1
            project_and_norm(nc, m, a, "out1", a["w_out"], a["ln_g"][0], a["ln_b"][0], rhs, load_y, x, load_x, None,
                             buffers[0], lambda sp: load_ahead(sp, buffers[1], a["w_att"]))
        tables = {
            "bias": m.sb("bias", 128, H, 3, 128),
            "sink": m.sb("sink", 128, H), "ident": m.sb("ident", 128, 128), "loaded": m.sem("tables_loaded"),
        }
        attention_projections(nc, m, a, scr, x, tables, buffers[1])
        with Tensors(nc, "two", m) as m2:
            o = m2.sb("o", 128, DT, N)
            with Tensors(nc, "sample", m) as m3:
                sample = sample_buffers(m3)
                attention(nc, m, a, scr, outp, o, tables, sample)
                sample_attention(nc, m, a, scr, outp, o, tables, sample,
                                 lambda sp: load_ahead(sp, buffers[2], a["w_att_out"]))

            def nothing(sp, sem):
                return None
            nothing.count = 0

            def store_y(sp, part, sem):
                n0, n = PARTS[part]
                sp.dma_start(outp["y"][:, :, n0:n0 + n], x[:, :, n0:n0 + n]).then_inc(sem, 16)
            project_and_norm(nc, m, a, "out2", a["w_att_out"], a["ln_g"][1], a["ln_b"][1], o, nothing, x, nothing, store_y,
                             buffers[2], None)


def laid_out(i):
    i = {k: np.asarray(v) for k, v in i.items()}

    def channels(v):
        return np.moveaxis(v.reshape(*v.shape[:-1], DT, 128), -1, 0)

    def weight_tiles(w):
        return w.reshape(DT, 128, -1, 128).transpose(2, 1, 0, 3)

    perm = np.concatenate([np.arange(64) + 64 * (4 * f + 2 * p + h) for f in range(4) for h in range(2) for p in range(2)])
    token_rows = np.concatenate([np.zeros((1, D), np.float32), i["x_prompt"][0]] + [
        r for b in range(NB) for r in (i["state_shift"][0, b][None], i["x_sample"][b])])
    w = i["rwkv_w_in"][0]
    pairs = lambda v: np.repeat(v.reshape(DT, 2, 1, 64).transpose(1, 2, 0, 3), 64, 1).reshape(128, DT, 64)
    arrays = {
        "xpad": channels(token_rows).transpose(0, 2, 1), "mu": channels(i["rwkv_mu"][0]), "w0": channels(i["rwkv_w0"][0]),
        "a0": channels(i["rwkv_a0"][0]),
        "lora1": np.stack([i["rwkv_w1"][0], i["rwkv_a1"][0]]).reshape(2, DT, 128, 64).transpose(2, 0, 1, 3),
        "lora2": np.stack([i["rwkv_w2"][0], i["rwkv_a2"][0]]).reshape(2, 64, DT, 128).transpose(2, 1, 0, 3),
        "w_in": np.stack([weight_tiles(x) for x in (w[1], w[0], w[2], w[3][:, perm])]),
        "k_k": channels(i["rwkv_k_k"][0]), "k_a": channels(i["rwkv_k_a"][0]), "r_k": channels(i["rwkv_r_k"][0].reshape(D)),
        "gn_g": pairs(i["rwkv_gn_g"][0]), "gn_b": pairs(i["rwkv_gn_b"][0]),
        "s_sample": i["state_wkv"][0].reshape(NB, DT, 2, 64, 64).transpose(2, 4, 1, 0, 3).reshape(128, DT, NB, 64),
        "w_out": weight_tiles(i["rwkv_w_out"][0][perm]), "ln_g": np.stack([channels(x) for x in i["ln_g"]]),
        "ln_b": np.stack([channels(x) for x in i["ln_b"]]), "w_att": weight_tiles(i["att_w_in"][0]),
        "w_att_out": weight_tiles(i["att_w_out"][0]), "sink": np.broadcast_to(i["att_sinks"][0], (128, H)),
        "sink_sample": np.repeat(i["att_sinks"][0], NT).reshape(128, 1),
        "k_cache": i["cache_win_k"][0].reshape(NB, WIN, 2, 128).transpose(3, 0, 2, 1),
        "v_cache": i["cache_win_v"][0].reshape(NB, WIN, 256).transpose(1, 0, 2),
    }
    arrays = {k: np.ascontiguousarray(v) for k, v in {**arrays, **constants()}.items()}
    arrays["x_last"] = np.ascontiguousarray(np.concatenate([i["x_prompt"][:, -1], i["x_sample"][:, -1]]))
    return arrays


def kernel(**inputs):
    import concourse.bacc as _bacc
    from concourse.bass_utils import run_bass_kernel_spmd as _run

    arrays = laid_out(inputs)
    nc = _bacc.Bacc("TRN2", target_bir_lowering=False, num_devices=1)
    a = {k: nc.dram_tensor(f"in_{k}", v.shape, F32, kind="ExternalInput").ap() for k, v in arrays.items()}
    outp = {k: nc.dram_tensor(f"out_{k}", shape, F32, kind="ExternalOutput").ap() for k, shape in _OUTS.items()}
    program(nc, a, outp)
    r = _run(nc, [{f"in_{k}": v for k, v in arrays.items()}], core_ids=[0]).results[0]
    got = {k: r[f"out_{k}"] for k in _OUTS}
    y = got["y"].transpose(2, 1, 0).reshape(N, D)
    window = lambda v: v.transpose(2, 1, 0).reshape(1, 1, WIN, KVH, HD)
    return (y[None, :SEQ], y[SEQ:].reshape(NB, NT, D),
            got["wkv_prompt"].reshape(2, 64, DT, 64).transpose(2, 0, 3, 1).reshape(1, 1, H, HD, HD),
            got["shift"][None, :1], window(got["k_prompt"]), window(got["v_prompt"]),
            got["wkv_sample"].reshape(2, 64, DT, NB, 64).transpose(3, 2, 0, 4, 1).reshape(1, NB, H, HD, HD),
            got["shift"][None, 1:],
            got["k_sample"].transpose(1, 3, 2, 0).reshape(1, NB, WIN, KVH, HD),
            got["v_sample"].transpose(1, 0, 2).reshape(1, NB, WIN, KVH, HD))
```
